# Optimizing a Trainium2 kernel written in Bass

```python
import jax, jax.numpy as jnp
from jax import lax
import numpy as np

D_MODEL = 1024
BATCH = 1
SEQ = 256
DEPTH = 2
DEC_BATCH = 8
DEC_SEQ = 16
PAST_LEN = 256

CHUNK = 64
N_MEM = 256
EPS = 1e-6
NEG_INF = -1e30

A_HEAD_DIM = 64
D_A = D_MODEL // 4
A_HEADS = D_A // A_HEAD_DIM
A_LEFT_CHUNKS = 8
A_REACH = A_LEFT_CHUNKS * CHUNK
A_BAND = (A_LEFT_CHUNKS + 1) * CHUNK
REL_CLIP = 128
A_SCALE = A_HEAD_DIM ** -0.5

B_QK_DIM = 64
B_V_DIM = 128
D_B = D_MODEL // 2
B_HEADS = D_B // B_V_DIM
D_BQK = B_HEADS * B_QK_DIM
RET_GAMMA_EXP0 = 5.0
ROPE_BASE = 10000.0

C_CHANNELS = D_MODEL // 4
CONV_WIDTH = 31

D_MIX = D_A + D_B + C_CHANNELS
D_IN = 3 * D_A + 2 * D_BQK + 2 * D_B + 2 * C_CHANNELS

X_HEADS = 4
X_HEAD_DIM = D_MODEL // X_HEADS

D_FF = 11 * D_MODEL // 4
N_EXPERTS = 8
TOP_K = 2
D_FF_EXPERT = D_FF // 2
N_DENSE = (DEPTH + 1) // 2
N_MOE = DEPTH // 2

kernel_name = 'hybrid_streaming_encoder_step'

def rms_norm(x, g):
    xf = x.astype(jnp.float32)
    y = xf * lax.rsqrt(jnp.mean(xf * xf, axis=-1, keepdims=True) + EPS)
    return (y * g.astype(jnp.float32)).astype(x.dtype)

def layer_norm(x, g, b):
    xf = x.astype(jnp.float32)
    mu = jnp.mean(xf, axis=-1, keepdims=True)
    var = jnp.mean(jnp.square(xf - mu), axis=-1, keepdims=True)
    y = (xf - mu) * lax.rsqrt(var + EPS) * g.astype(jnp.float32) + b.astype(jnp.float32)
    return y.astype(x.dtype)

def rotary(x, pos):
    half = x.shape[-1] // 2
    inv_freq = ROPE_BASE ** (-jnp.arange(half, dtype=jnp.float32) / half)
    ang = pos[:, None] * inv_freq[None, :]
    cos = jnp.cos(ang)[None, :, None, :]
    sin = jnp.sin(ang)[None, :, None, :]
    xf = x.astype(jnp.float32)
    x1, x2 = xf[..., :half], xf[..., half:]
    return jnp.concatenate([x1 * cos - x2 * sin, x2 * cos + x1 * sin], axis=-1).astype(x.dtype)

def band_attention(q, k, v, q_pos, k_pos, k_valid, rel_bias):
    rel = jnp.clip(q_pos[:, :, None] - k_pos[:, None, :], -REL_CLIP, REL_CLIP) + REL_CLIP
    bias = jnp.transpose(rel_bias[:, rel], (1, 0, 2, 3)).astype(jnp.float32)
    s = jnp.einsum('ngqhd,ngkhd->nghqk', q, k).astype(jnp.float32) * A_SCALE + bias[None]
    s = jnp.where(k_valid[None, :, None, None, :], s, NEG_INF)
    p = jax.nn.softmax(s, axis=-1).astype(v.dtype)
    return jnp.einsum('nghqk,ngkhd->ngqhd', p, v)

def band_attention_prompt(qa, ka, va, rel_bias):
    n, t = qa.shape[:2]
    nc = t // CHUNK

    def band(a):
        ac = a.reshape(n, nc, CHUNK, A_HEADS, A_HEAD_DIM)
        ac = jnp.pad(ac, ((0, 0), (A_LEFT_CHUNKS, 0), (0, 0), (0, 0), (0, 0)))
        return jnp.concatenate([ac[:, j:j + nc] for j in range(A_LEFT_CHUNKS + 1)], axis=2)

    c = jnp.arange(nc)[:, None]
    q_pos = c * CHUNK + jnp.arange(CHUNK)[None, :]
    k_pos = (c - A_LEFT_CHUNKS) * CHUNK + jnp.arange(A_BAND)[None, :]
    o = band_attention(qa.reshape(n, nc, CHUNK, A_HEADS, A_HEAD_DIM), band(ka), band(va),
                       q_pos, k_pos, k_pos >= 0, rel_bias)
    return o.reshape(n, t, A_HEADS, A_HEAD_DIM)

def band_attention_sample(qa, ka, va, ck, cv, pos0, rel_bias):
    t = qa.shape[1]
    l = ck.shape[1]
    k_all = jnp.concatenate([ck.astype(ka.dtype), ka], axis=1)[:, None]
    v_all = jnp.concatenate([cv.astype(va.dtype), va], axis=1)[:, None]
    q_pos = (pos0 + jnp.arange(t))[None, :]
    k_pos = (pos0 - l + jnp.arange(l + t))[None, :]
    valid = jnp.ones((1, l + t), dtype=bool)
    return band_attention(qa[:, None], k_all, v_all, q_pos, k_pos, valid, rel_bias)[:, 0]

def retention(q, k, v, s0, gn_g):
    n, t, h, dk = q.shape
    dv = v.shape[-1]
    blk = min(CHUNK, t)
    nb = t // blk
    log_g = jnp.log(1.0 - 2.0 ** (-(RET_GAMMA_EXP0 + jnp.arange(h, dtype=jnp.float32))))
    i = jnp.arange(blk, dtype=jnp.float32)
    diff = i[:, None] - i[None, :]
    dmask = jnp.where(diff[None] >= 0, jnp.exp(jnp.maximum(diff, 0.0)[None] * log_g[:, None, None]), 0.0)
    q_dec = jnp.exp((i[:, None] + 1.0) * log_g[None, :])
    k_dec = jnp.exp((blk - 1.0 - i)[:, None] * log_g[None, :])
    s_dec = jnp.exp(blk * log_g)

    def blocks(a):
        return jnp.moveaxis(a.astype(jnp.float32).reshape(n, nb, blk, h, a.shape[-1]), 1, 0)

    def step(s, inp):
        qi, ki, vi = inp
        att = jnp.einsum('nihd,njhd->nhij', qi, ki) * dmask[None]
        o = (jnp.einsum('nhij,njhe->nihe', att, vi)
             + jnp.einsum('nihd,nhde->nihe', qi * q_dec[None, :, :, None], s))
        s = s * s_dec[None, :, None, None] + jnp.einsum('njhd,njhe->nhde', ki * k_dec[None, :, :, None], vi)
        return s, o

    s_fin, o = lax.scan(step, s0.astype(jnp.float32), (blocks(q), blocks(k), blocks(v)))
    o = jnp.moveaxis(o, 0, 1).reshape(n, t, h, dv)
    mu = jnp.mean(o, axis=-1, keepdims=True)
    var = jnp.mean(jnp.square(o - mu), axis=-1, keepdims=True)
    o = ((o - mu) * lax.rsqrt(var + EPS)).reshape(n, t, h * dv) * gn_g.astype(jnp.float32)
    return o, s_fin

def conv_module(ca, cb, buf, conv_w, conv_b, ln_g, ln_b):
    u = ca * jax.nn.sigmoid(cb)
    up = jnp.concatenate([buf.astype(u.dtype), u], axis=1)
    y = lax.conv_general_dilated(up, conv_w[:, None, :].astype(u.dtype), (1,), 'VALID',
                                 dimension_numbers=('NWC', 'WIO', 'NWC'),
                                 feature_group_count=C_CHANNELS)
    y = jax.nn.silu(layer_norm(y + conv_b.astype(u.dtype), ln_g, ln_b))
    return y, up[:, up.shape[1] - (CONV_WIDTH - 1):]

def token_mixer(h, pos0, attn_cache, ret_state, conv_state,
                w_in, rel_bias, ret_gn_g, conv_w, conv_b, conv_ln_g, conv_ln_b, w_out):
    n, t, _ = h.shape
    splits = [int(s) for s in np.cumsum([D_A, D_A, D_A, D_BQK, D_BQK, D_B, D_B, C_CHANNELS])]
    qa, ka, va, qb, kb, vb, gb, ca, cb = jnp.split(h @ w_in, splits, axis=-1)
    qa = qa.reshape(n, t, A_HEADS, A_HEAD_DIM)
    ka = ka.reshape(n, t, A_HEADS, A_HEAD_DIM)
    va = va.reshape(n, t, A_HEADS, A_HEAD_DIM)
    if attn_cache is None:
        o_a = band_attention_prompt(qa, ka, va, rel_bias)
        keep = min(A_REACH, t)
        new_k, new_v = ka[:, t - keep:], va[:, t - keep:]
    else:
        o_a = band_attention_sample(qa, ka, va, attn_cache[0], attn_cache[1], pos0, rel_bias)
        new_k, new_v = ka, va
    pos = pos0 + jnp.arange(t, dtype=jnp.float32)
    qb = rotary(qb.reshape(n, t, B_HEADS, B_QK_DIM), pos)
    kb = rotary(kb.reshape(n, t, B_HEADS, B_QK_DIM), pos) * (B_QK_DIM ** -0.5)
    vb = vb.reshape(n, t, B_HEADS, B_V_DIM)
    o_b, new_s = retention(qb, kb, vb, ret_state, ret_gn_g)
    o_b = jax.nn.silu(gb) * o_b.astype(h.dtype)
    o_c, new_conv = conv_module(ca, cb, conv_state, conv_w, conv_b, conv_ln_g, conv_ln_b)
    y = jnp.concatenate([o_a.reshape(n, t, D_A), o_b, o_c], axis=-1) @ w_out
    return y, new_k, new_v, new_s, new_conv

def memory_kv(mem, wk, wv):
    n, m, _ = mem.shape
    return ((mem @ wk).reshape(n, m, X_HEADS, X_HEAD_DIM), (mem @ wv).reshape(n, m, X_HEADS, X_HEAD_DIM))

def cross_attention(h, mk, mv, wq, wo):
    n, t, _ = h.shape
    q = (h @ wq).reshape(n, t, X_HEADS, X_HEAD_DIM)
    s = jnp.einsum('nqhd,nkhd->nhqk', q, mk).astype(jnp.float32) * (X_HEAD_DIM ** -0.5)
    p = jax.nn.softmax(s, axis=-1).astype(mv.dtype)
    o = jnp.einsum('nhqk,nkhd->nqhd', p, mv).reshape(n, t, X_HEADS * X_HEAD_DIM)
    return o @ wo

def swiglu(h, wg, wu, wd):
    return (jax.nn.silu(h @ wg) * (h @ wu)) @ wd

def moe_swiglu(h, router, wg, wu, wd):
    probs = jax.nn.softmax((h @ router).astype(jnp.float32), axis=-1)
    top_p, top_i = lax.top_k(probs, TOP_K)
    top_p = top_p / jnp.sum(top_p, axis=-1, keepdims=True)
    combine = jnp.sum(jax.nn.one_hot(top_i, N_EXPERTS, dtype=jnp.float32) * top_p[..., None], axis=-2)
    combine = combine.astype(h.dtype)
    out = jnp.zeros(h.shape, h.dtype)
    for e in range(N_EXPERTS):
        out = out + combine[..., e:e + 1] * swiglu(h, wg[e], wu[e], wd[e])
    return out

def channel_mixer(h, l, ffn_w_gate, ffn_w_up, ffn_w_down, router_w, moe_w_gate, moe_w_up, moe_w_down):
    i = l // 2
    if l % 2 == 0:
        return swiglu(h, ffn_w_gate[i], ffn_w_up[i], ffn_w_down[i])
    return moe_swiglu(h, router_w[i], moe_w_gate[i], moe_w_up[i], moe_w_down[i])

def setup_inputs(seed: int = 0) -> dict:
    key = jax.random.key(seed)
    ks = iter(jax.random.split(key, 40))

    def nrm(shape, scale):
        return jax.random.normal(next(ks), shape, jnp.float32) * scale

    def gain(shape):
        return 1.0 + nrm(shape, 0.01)

    la = min(A_REACH, PAST_LEN)
    return {
        'x_prompt': nrm((BATCH, SEQ, D_MODEL), 1.0),
        'x_sample': nrm((DEC_BATCH, DEC_SEQ, D_MODEL), 1.0),
        'cache_attn_k': nrm((DEPTH, DEC_BATCH, la, A_HEADS, A_HEAD_DIM), 1.0),
        'cache_attn_v': nrm((DEPTH, DEC_BATCH, la, A_HEADS, A_HEAD_DIM), 1.0),
        'state_ret': nrm((DEPTH, DEC_BATCH, B_HEADS, B_QK_DIM, B_V_DIM), 1.0),
        'state_conv': nrm((DEPTH, DEC_BATCH, CONV_WIDTH - 1, C_CHANNELS), 0.5),
        'cache_mem_k': nrm((DEPTH, DEC_BATCH, N_MEM, X_HEADS, X_HEAD_DIM), 1.0),
        'cache_mem_v': nrm((DEPTH, DEC_BATCH, N_MEM, X_HEADS, X_HEAD_DIM), 1.0),
        'mem_prompt': nrm((BATCH, N_MEM, D_MODEL), 1.0),
        'norm_mix_g': gain((DEPTH, D_MODEL)),
        'w_in': nrm((DEPTH, D_MODEL, D_IN), D_MODEL ** -0.5),
        'rel_bias': nrm((DEPTH, A_HEADS, 2 * REL_CLIP + 1), 0.5),
        'ret_gn_g': gain((DEPTH, D_B)),
        'conv_w': nrm((DEPTH, CONV_WIDTH, C_CHANNELS), CONV_WIDTH ** -0.5),
        'conv_b': nrm((DEPTH, C_CHANNELS), 0.01),
        'conv_ln_g': gain((DEPTH, C_CHANNELS)),
        'conv_ln_b': nrm((DEPTH, C_CHANNELS), 0.01),
        'w_out': nrm((DEPTH, D_MIX, D_MODEL), D_MIX ** -0.5),
        'norm_mem_g': gain((DEPTH, D_MODEL)),
        'wx_q': nrm((DEPTH, D_MODEL, X_HEADS * X_HEAD_DIM), D_MODEL ** -0.5),
        'wx_k': nrm((DEPTH, D_MODEL, X_HEADS * X_HEAD_DIM), D_MODEL ** -0.5),
        'wx_v': nrm((DEPTH, D_MODEL, X_HEADS * X_HEAD_DIM), D_MODEL ** -0.5),
        'wx_o': nrm((DEPTH, X_HEADS * X_HEAD_DIM, D_MODEL), (X_HEADS * X_HEAD_DIM) ** -0.5),
        'norm_ffn_g': gain((DEPTH, D_MODEL)),
        'ffn_w_gate': nrm((N_DENSE, D_MODEL, D_FF), D_MODEL ** -0.5),
        'ffn_w_up': nrm((N_DENSE, D_MODEL, D_FF), D_MODEL ** -0.5),
        'ffn_w_down': nrm((N_DENSE, D_FF, D_MODEL), D_FF ** -0.5),
        'router_w': nrm((N_MOE, D_MODEL, N_EXPERTS), D_MODEL ** -0.5),
        'moe_w_gate': nrm((N_MOE, N_EXPERTS, D_MODEL, D_FF_EXPERT), D_MODEL ** -0.5),
        'moe_w_up': nrm((N_MOE, N_EXPERTS, D_MODEL, D_FF_EXPERT), D_MODEL ** -0.5),
        'moe_w_down': nrm((N_MOE, N_EXPERTS, D_FF_EXPERT, D_MODEL), D_FF_EXPERT ** -0.5),
        'final_norm_g': gain((D_MODEL,)),
    }

def reference(x_prompt, x_sample, cache_attn_k, cache_attn_v, state_ret, state_conv, cache_mem_k, cache_mem_v,
              mem_prompt, norm_mix_g, w_in, rel_bias, ret_gn_g, conv_w, conv_b, conv_ln_g, conv_ln_b, w_out,
              norm_mem_g, wx_q, wx_k, wx_v, wx_o, norm_ffn_g, ffn_w_gate, ffn_w_up, ffn_w_down,
              router_w, moe_w_gate, moe_w_up, moe_w_down, final_norm_g):
    xp, xs = x_prompt, x_sample
    n_p = xp.shape[0]
    pk, pv, ps, pc, pmk, pmv = [], [], [], [], [], []
    sk, sv, ss, sc = [], [], [], []
    for l in range(DEPTH):
        mix_w = (w_in[l], rel_bias[l], ret_gn_g[l], conv_w[l], conv_b[l], conv_ln_g[l], conv_ln_b[l], w_out[l])
        ret0 = jnp.zeros((n_p, B_HEADS, B_QK_DIM, B_V_DIM), jnp.float32)
        conv0 = jnp.zeros((n_p, CONV_WIDTH - 1, C_CHANNELS), xp.dtype)
        y, k_new, v_new, s_new, c_new = token_mixer(rms_norm(xp, norm_mix_g[l]), 0, None, ret0, conv0, *mix_w)
        xp = xp + y
        pk.append(k_new)
        pv.append(v_new)
        ps.append(s_new)
        pc.append(c_new)
        y, k_new, v_new, s_new, c_new = token_mixer(rms_norm(xs, norm_mix_g[l]), PAST_LEN,
                                                    (cache_attn_k[l], cache_attn_v[l]),
                                                    state_ret[l], state_conv[l], *mix_w)
        xs = xs + y
        sk.append(k_new)
        sv.append(v_new)
        ss.append(s_new)
        sc.append(c_new)
        mk, mv = memory_kv(mem_prompt, wx_k[l], wx_v[l])
        pmk.append(mk)
        pmv.append(mv)
        xp = xp + cross_attention(rms_norm(xp, norm_mem_g[l]), mk, mv, wx_q[l], wx_o[l])
        xs = xs + cross_attention(rms_norm(xs, norm_mem_g[l]), cache_mem_k[l].astype(xs.dtype),
                                  cache_mem_v[l].astype(xs.dtype), wx_q[l], wx_o[l])
        xp = xp + channel_mixer(rms_norm(xp, norm_ffn_g[l]), l, ffn_w_gate, ffn_w_up, ffn_w_down,
                                router_w, moe_w_gate, moe_w_up, moe_w_down)
        xs = xs + channel_mixer(rms_norm(xs, norm_ffn_g[l]), l, ffn_w_gate, ffn_w_up, ffn_w_down,
                                router_w, moe_w_gate, moe_w_up, moe_w_down)
    y_prompt = rms_norm(xp, final_norm_g)
    y_sample = rms_norm(xs, final_norm_g)
    new_attn_k_prompt = jnp.stack(pk)
    new_attn_v_prompt = jnp.stack(pv)
    new_ret_prompt = jnp.stack(ps)
    new_conv_prompt = jnp.stack(pc)
    new_mem_k_prompt = jnp.stack(pmk)
    new_mem_v_prompt = jnp.stack(pmv)
    new_attn_k_sample = jnp.stack(sk)
    new_attn_v_sample = jnp.stack(sv)
    new_ret_sample = jnp.stack(ss)
    new_conv_sample = jnp.stack(sc)
    return (y_prompt, y_sample, new_attn_k_prompt, new_attn_v_prompt, new_ret_prompt, new_conv_prompt,
            new_mem_k_prompt, new_mem_v_prompt, new_attn_k_sample, new_attn_v_sample, new_ret_sample,
            new_conv_sample)


_drawn_inputs = setup_inputs


def setup_inputs(seed=0):
    import zlib

    import numpy as np

    out = dict(_drawn_inputs(seed))
    spreads = {}
    factors = {'ret_gn_g': 12.188,
     'conv_b': 2.791,
     'conv_ln_g': 15.097,
     'conv_ln_b': 29.27,
     'norm_mem_g': 27.351,
     'final_norm_g': 193.048,
     'norm_ffn_g': 5.716,
     'rel_bias': 3.66}
    for name, (base, spread) in spreads.items():
        noise = np.random.default_rng([zlib.crc32(name.encode()), seed]).standard_normal(out[name].shape)
        drawn = base * np.exp(spread * noise) if base else spread * noise
        out[name] = __import__('jax').numpy.asarray(drawn.astype(out[name].dtype))
    for name, factor in factors.items():
        out[name] = (out[name] * factor).astype(out[name].dtype)
    return out
```

```python
from contextlib import ExitStack

import numpy as np

import concourse.bass as bass
from concourse import mybir

F32 = mybir.dt.float32
ALU = mybir.AluOpType
ACT = mybir.ActivationFunctionType
AX = mybir.AxisListType

P = 128
DEPTH = 2
D = 1024
SEQ = 256
NS = 8
TS = 16
PAST = 256
NT = 3
TOK = NT * P
KC = D // P
CHUNK = 64
NMEM = 256
EPS = 1e-6
NEG = -1e30
AH, AD = 4, 64
BH, BK, BV = 4, 64, 128
CC = 256
CW = 31
REL = 128
DIN = 2816
QA, KA, VA, QB, KB, VB, GB, CA, CB = 0, 256, 512, 768, 1024, 1280, 1792, 2304, 2560
XH, XD = 4, 256
FF = 1408
FFK = FF // P
NE = 8
RLEN = 400
RPAD = 143
R = 4
SLAB = 2048
GAMMA = [1.0 - 2.0 ** (-(5.0 + h)) for h in range(BH)]
IN_CHUNKS = [(2304, 512), (0, 512), (512, 512), (1024, 512), (1536, 512), (2048, 256)]
FF_CHUNKS = [(0, 512), (512, 512), (1024, 384)]
FF_GROUPS = [(0, 4), (4, 4), (8, 3)]

CONST = {}
_at = 0
for _name, _width in (("ident", P), ("cos", NT * 2 * 32), ("sin", NT * 2 * 32), ("decay", BH * 256),
                      ("decay_s", BH * P), ("qdec", BH * TS), ("kdec", 2 * BH), ("kmask", BH * NS),
                      ("smask", 4 * P), ("cmask", P), ("minus_half", 4)):
    CONST[_name] = (_at, _width)
    _at += _width
NCONST = _at


def constants():
    c = np.zeros((P, NCONST), np.float32)

    def put(name, a):
        o, w = CONST[name]
        c[:, o:o + w] = np.asarray(a, np.float64).reshape(P, w)

    p = np.arange(P)
    put("ident", np.eye(P))
    inv = (np.float32(10000.0) ** (-np.arange(32, dtype=np.float32) / np.float32(32))).astype(np.float32)
    pos = np.stack([p, P + p, PAST + p % TS], 1).astype(np.float32)
    ang = (pos[:, :, None] * inv[None, None, :]).astype(np.float32)
    scale = np.array([1.0, BK ** -0.5], np.float32)[None, None, :, None]
    put("cos", np.cos(ang)[:, :, None, :] * scale)
    put("sin", np.sin(ang)[:, :, None, :] * scale)
    lg = np.log(np.array(GAMMA, np.float64))
    dif = np.arange(256)[None, :] - p[:, None]
    put("decay", np.where(dif[:, None] >= 0, np.exp(np.maximum(dif, 0)[:, None] * lg[None, :, None]), 0.0))
    ds = (p % TS)[None, :] - (p % TS)[:, None]
    same = (p // TS)[None, :] == (p // TS)[:, None]
    put("decay_s", np.where((same & (ds >= 0))[:, None], np.exp(np.maximum(ds, 0)[:, None] * lg[None, :, None]), 0.0))
    put("qdec", np.broadcast_to(np.exp((np.arange(TS) + 1.0)[None, :] * lg[:, None])[None], (P, BH, TS)))
    kd = 255.0 - (np.arange(2)[None, :] * P + p[:, None])
    put("kdec", np.exp(kd[:, :, None] * lg[None, None, :]))
    km = np.exp((TS - 1.0 - p % TS)[:, None] * lg[None, :])
    put("kmask", km[:, :, None] * ((p // TS)[:, None, None] == np.arange(NS)[None, None, :]))
    own = (2 * np.arange(4)[None, :] + p[:, None] // 64)
    put("smask", np.where(own[:, :, None] == (p // TS)[None, None, :], 0.0, NEG))
    put("cmask", np.where((p[:, None] < CHUNK) & (p[None, :] >= CHUNK), NEG, 0.0))
    put("minus_half", np.full((P, 4), -0.5))
    return c


def insert(ap, axis, n):
    dims = [list(d) for d in ap.ap]
    return bass.AP(tensor=ap.tensor, offset=ap.offset, ap=dims[:axis] + [[0, n]] + dims[axis:])


def steps(ap, dims):
    return bass.AP(tensor=ap.tensor, offset=ap.offset, ap=[list(ap.ap[0])] + dims)


def rows(tensor_ap, offset, dims):
    return bass.AP(tensor=tensor_ap.tensor, offset=offset, ap=dims)


T = (6, 7)


def psum_jobs():
    jobs = []
    small = [0]
    big = [0]

    def one(key, who):
        jobs.append((key, (T[small[0] % 2],), who))
        small[0] += 1

    def product(name, chunks, tiles, who):
        for c in range(chunks):
            for t in range(tiles):
                jobs.append((name + (c, t), (3 * (big[0] % 2) + t,), who))
            big[0] += 1

    def norm(n):
        for t in range(NT):
            for half in range(2):
                one(("hT", n, t, half), "v")

    one(("gains",), "a")
    for j in range(4):
        one(("memT", j), "a")
    for l in range(DEPTH):
        norm(3 * l)
        one(("cw", l), "a")
        one(("cbuf", l), "a")
        product(("in", l), 2, NT, "a")
        for b in range(2):
            one(("uT", l, b), "a")
        for c in range(2, len(IN_CHUNKS)):
            for t in range(NT):
                jobs.append((("in", l, c, t), (3 * (big[0] % 2) + t,), "a"))
            big[0] += 1
        product(("mk", l), 2, 2, "a")
        product(("mv", l), 2, 2, "a")
        for j in range(4):
            one(("mkT", l, j), "a")
        for t in range(NT):
            one(("qkA", l, t), "a")
        for t in range(NT):
            one(("qkB", l, t), "a")
        for j in range(4):
            one(("sA", l, j), "v")
        for n in range(NS):
            one(("ktA", l, n), "a")
            if n % 2:
                one(("sS", l, n // 2), "v")
        for h in range(AH):
            one(("pTA", l, h), "a")
        one(("oA", l), "a")
        for r in range(4):
            one(("pTS", l, r), "a")
        one(("oS", l), "a")
        for h in range(BH):
            one(("aB", l, h), "v")
        for j in range(2):
            one(("aS", l, j), "v")
        for t in range(NT):
            one(("oB", l, t), "v")
        one(("nsP", l), "a")
        for h in range(BH):
            one(("nsS", l, h), "v")
        for t in range(NT):
            one(("yc", l, t), "v")
        for b in range(BH):
            one(("obT", l, b), "a")
        for b in range(2):
            one(("ocT", l, b), "a")
        product(("out", l), 2, NT, "v")
        norm(3 * l + 1)
        product(("q", l), 2, NT, "a")
        for j in range(4):
            one(("qTx", l, j), "a")
        for j in range(2):
            one(("qTs", l, j), "a")
        for j in range(4):
            one(("xs", l, j), "a")
        for h in range(XH):
            one(("xpT", l, h), "a")
        for h in range(XH):
            one(("xo", l, h), "a")
        for r in range(5):
            if r < 4:
                for n2 in range(2):
                    for j in range(4):
                        one(("kTs", l, 2 * r + n2, j), "v" if j % 2 else "a")
                one(("xss", l, r), "a")
            if r >= 1:
                one(("xpTs", l, r - 1), "a")
        jobs.append((("xos", l), (0, 1), "a"))
        product(("o", l), 2, NT, "v")
        norm(3 * l + 2)
        if l % 2:
            one(("route", l), "v")
        for e in range(NE if l % 2 else 2):
            for c in range(4):
                if c < 3:
                    for kind in ("gate", "up"):
                        for t in range(NT):
                            jobs.append(((kind, l, e, c, t), (3 * (kind == "up") + t,), "a" if kind == "gate" else "v"))
                if c:
                    for t in range(NT):
                        one(("aT", l, e, c - 1, t), "a")
            for c in range(2):
                for t in range(NT):
                    jobs.append((("down", l, e, c, t), (3 * c + t,), "v"))
        big[0] = 0
    return jobs


def slabs():
    out = []

    def product(name, key, l, cols, tiles):
        for c, (c0, w) in enumerate(cols):
            for half in range(2):
                out.append((name, "rows", (l, 4 * half, 4, c0, w), key + (c, 0 if half == 0 else tiles - 1)))

    full = [(0, 512), (512, 512)]
    for l in range(DEPTH):
        product("w_in", ("in", l), l, IN_CHUNKS, NT)
        product("wx_k", ("mk", l), l, full, 2)
        product("wx_v", ("mv", l), l, full, 2)
        for g in range(2):
            out.append(("cache_attn_k", "past", (l, g), ("ktA", l, 4 * g + 3)))
        for g in range(2):
            out.append(("cache_attn_v", "past", (l, g), ("oS", l)))
        product("w_out", ("out", l), l, full, NT)
        product("wx_q", ("q", l), l, full, NT)
        for r in range(5):
            if r < 4:
                for n in (2 * r, 2 * r + 1):
                    out.append(("cache_mem_k", "mem", (l, n), ("kTs", l, n, 3)))
            if r >= 1:
                for n in (2 * r - 2, 2 * r - 1):
                    out.append(("cache_mem_v", "mem", (l, n), ("xpTs", l, r) if r < 4 else ("xos", l)))
        product("wx_o", ("o", l), l, full, NT)
        for e in range(NE if l % 2 else 2):
            for c, (c0, w) in enumerate(FF_CHUNKS):
                for kind in ("gate", "up"):
                    for half in range(2):
                        out.append((kind, "ff", (l, e, 4 * half, 4, c0, w), (kind, l, e, c, 0 if half == 0 else NT - 1)))
            for c in range(2):
                for g, (k0, nk) in enumerate(FF_GROUPS):
                    out.append(("down", "ffd", (l, e, k0, nk, 512 * c), ("down", l, e, c, 0 if g < 2 else NT - 1)))
    return out


def hybrid_encoder(nc, a, o, scratch):
    JOBS = psum_jobs()
    INDEX = {key: i for i, (key, _, _) in enumerate(JOBS)}
    DRAIN, PREV, _last, _n = {}, {}, {}, {"a": 0, "v": 0}
    for key, banks, who in JOBS:
        _n[who] += 1
        DRAIN[key] = (who, _n[who])
        PREV[key] = [_last[b] for b in banks if b in _last]
        for b in banks:
            _last[b] = key
    BANK = {key: banks for key, banks, _ in JOBS}
    SLABS = slabs()

    with ExitStack() as ctx:
        def sem(name):
            return ctx.enter_context(nc.semaphore(name))

        total = [0]

        def sb(name, width):
            total[0] += width
            return ctx.enter_context(nc.sbuf_tensor(name, [P, width], F32))

        bank = [ctx.enter_context(nc.psum_tensor(f"bank{i}", [P, 512], F32)) for i in range(8)]

        x = sb("x", NT * D)[:, :].rearrange("p (t d) -> p t d", t=NT)
        fT_ = sb("features_T", KC * TOK)
        hT = fT_[:, :].rearrange("p (k n) -> p k n", k=KC)
        oT = hT
        ring = sb("ring", R * SLAB)
        memT = sb("memT", KC * NMEM)[:, :].rearrange("p (k n) -> p k n", k=KC)
        mv = sb("mv", 2 * D)[:, :].rearrange("p (t d) -> p t d", t=2)
        mkT = sb("mkT", KC * NMEM)[:, :].rearrange("p (k n) -> p k n", k=KC)
        cst = sb("consts", NCONST)
        gT = sb("gT", 48)
        stat = sb("stat", 64)
        rel_p = sb("rel_p", AH * 256)[:, :].rearrange("p (h k) -> p h k", h=AH)
        rel_s = sb("rel_s", PAST + TS)
        rel_n = sb("rel_n", 4 * P)[:, :].rearrange("p (r k) -> p r k", r=4)
        bc_gn = sb("bc_gn", BH * BV)
        bc_cg = sb("bc_cg", CC)
        bc_cb = sb("bc_cb", CC)
        comb = sb("comb", NT * NE)[:, :].rearrange("p (t e) -> p t e", t=NT)
        rw = sb("rw", KC * NE)[:, :].rearrange("p (k e) -> p k e", k=KC)
        rt = sb("rt", 8 * NT * NE)
        small = sb("small", 128)

        arena_w = (nc.sbuf_bytes_remaining() if callable(nc.sbuf_bytes_remaining) else nc.sbuf_bytes_remaining) // 4 - 128
        arena = ctx.enter_context(nc.sbuf_tensor("arena", [P, arena_w], F32))

        class Plan:
            def __init__(self):
                self.at = 0

            def take(self, w):
                self.at += w
                assert self.at <= arena_w, (self.at, arena_w)
                return arena[:, self.at - w:self.at]

        def cut(ap, **k):
            names = list(k)
            s = "p (" + " ".join(names) + " w) -> p " + " ".join(names) + " w"
            return ap.rearrange(s, **k)

        m = Plan()
        proj = cut(m.take(NT * DIN), t=NT)
        qkA = cut(m.take(4 * TOK), b=4)
        qblk = m.take(2 * NS * 32).rearrange("p (b n c) -> p b n c", b=2, n=NS)
        qkB = cut(m.take(4 * TOK), b=4)
        at0 = m.at
        mk = arena[:, at0:at0 + 2 * D].rearrange("p (t d) -> p t d", t=2)
        lg0 = cut(m.take(AH * P), h=AH)
        lg1 = cut(m.take(AH * 256), h=AH)
        lgS = cut(m.take(4 * TOK), r=4)
        pTA = cut(m.take(AH * TOK), h=AH)
        pTS = m.take(4 * TOK).rearrange("p (r k n) -> p r k n", r=4, k=3)
        end_a = m.at
        m.at = at0
        attT = cut(m.take(BH * TOK), h=BH)
        attS = cut(m.take(BH * P), h=BH)
        q0 = cut(m.take(BH * 512), h=BH)
        ks = m.take(BH * 512).rearrange("p (h n d) -> p h n d", h=BH, n=NS)
        end_b = m.at
        m.at = max(end_a, end_b)
        ktA = m.take(4 * 512).rearrange("p (n b k) -> p n b k", n=4, b=2)
        s0 = m.take(16 * BV).rearrange("p (j h v) -> p j h v", j=4, h=BH)
        kd = cut(m.take(2 * 256), t=2)
        spr = ktA.rearrange("p n b k -> p (n b k)")[:, 0:BH * BV]
        cw = cut(m.take(2 * 32), b=2)
        cwr = m.take(CC)
        cbufr = cut(m.take(2 * CC), g=2)
        up = cut(m.take(2 * (SEQ + 30)), b=2)
        us = m.take(2 * NS * 46).rearrange("p (b n w) -> p b n w", b=2, n=NS)
        conv = cut(m.take(2 * TOK), b=2)
        sig = proj[:, :, CB:CB + CC]
        rtmp = m.take(2 * 256)

        n_ = Plan()
        htok = cut(n_.take(NT * D), t=NT)
        qx = cut(n_.take(NT * D), t=NT)
        qxT = cut(n_.take(KC * SEQ), k=KC)
        qxb = n_.take(KC * NS * 32).rearrange("p (k n c) -> p k n c", k=KC, n=NS)
        px = n_.take(2 * XH * NMEM).rearrange("p (t h m) -> p t h m", t=2, h=XH)
        pxT = n_.take(XH * 2 * SEQ).rearrange("p (h m n) -> p h m n", h=XH, m=2)
        kTs = n_.take(2 * KC * NMEM).rearrange("p (s k m) -> p s k m", s=2, k=KC)
        pxs = cut(n_.take(2 * NMEM), s=2)
        pxsT = n_.take(2 * 2 * P).rearrange("p (s m n) -> p s m n", s=2, m=2)

        f = Plan()
        f.take(NT * D)
        gated = cut(f.take(NT * 512), t=NT)
        acts = cut(f.take(2 * NT * 512), s=2 * NT)
        actT = cut(f.take(FFK * TOK), k=FFK)

        memtok = cut(arena[:, at0:at0 + 2 * D], t=2)
        grow = arena[:, at0 + 2 * D:at0 + 2 * D + P]
        relx = arena[:, at0 + 2 * D + P:at0 + 2 * D + P + RLEN]
        fgain = arena[:, at0:at0 + D]
        gnt = rtmp
        bnst = sb("bnst", 24)
        bnag = sb("bnag", NT * 8)[:, :].rearrange("p (t j) -> p t j", t=NT)
        rstd8 = sb("rstd8", NT * 4)[:, :].rearrange("p (t j) -> p t j", t=NT)
        lnag = sb("lnag", 8)
        lnr = sb("lnr", 4)
        eight = sb("eight", NE)[:, :]

        def rtv(i):
            return cut(rt[:, i * NT * NE:(i + 1) * NT * NE], t=NT)

        def const(name):
            off, w = CONST[name]
            return cst[:, off:off + w]

        ident = const("ident")
        cos_t = const("cos").rearrange("p (t b w) -> p t b w", t=NT, b=2)
        sin_t = const("sin").rearrange("p (t b w) -> p t b w", t=NT, b=2)
        decay = const("decay").rearrange("p (h i) -> p h i", h=BH)
        decay_s = const("decay_s").rearrange("p (h i) -> p h i", h=BH)
        qdec = const("qdec").rearrange("p (h i) -> p h i", h=BH)
        kdec = const("kdec").rearrange("p (t h) -> p t h", t=2)
        kmask = const("kmask").rearrange("p (h n) -> p h n", h=BH)
        smask = const("smask").rearrange("p (r k) -> p r k", r=4)
        cmask = const("cmask")
        minus_half = const("minus_half")

        filled = sem("psum_filled")
        emptied = {"a": sem("psum_emptied_by_scalar"), "v": sem("psum_emptied_by_vector")}
        slab_in = [sem(f"slab_in{i}") for i in range(R)]
        s_const = sem("constants_in")
        s_x = sem("x_in")
        s_mem = sem("memory_in")
        s_gain = sem("gain_rows_in")
        s_relr = sem("rel_rows_in")
        s_relv = sem("rel_vector_out")
        s_rel = sem("rel_bias_in")
        s_cw = sem("conv_weights_in")
        s_cbuf = sem("conv_state_in")
        s_bc = sem("row_params_in")
        s_s0 = sem("ret_state_in")
        s_rw = sem("router_in")
        s_fg = sem("final_gain_in")
        s_kvo = sem("new_attn_rows_out")
        s_mko = sem("new_mem_rows_out")
        s_spo = sem("new_ret_prompt_out")
        s_yo = sem("y_out")
        s_outp = sem("conv_state_out")
        s_st = sem("ret_state_out")
        s_own = {"a": sem("scalar_steps"), "v": sem("vector_steps"), "g": sem("pool_steps")}
        s_sq = sem("squares_summed")
        s_rstd = sem("rstd_ready")
        s_h = sem("h_ready")
        s_relx = sem("rel_vector_ready")
        s_sig = sem("conv_gate_ready")
        s_u = sem("conv_u_ready")
        s_conv = sem("conv_ready")
        s_lnv = sem("conv_var_ready")
        s_lnr = sem("conv_norm_ready")
        s_cln = sem("conv_rstd_ready")
        s_oc = sem("conv_out_ready")
        s_rot = sem("rotary_ready")
        s_blk = sem("query_blocks_ready")
        s_kd = sem("decayed_k_ready")
        s_q0 = sem("decayed_q_ready")
        s_zero = sem("zeros_ready")
        s_max = sem("band_max_ready")
        s_exp = sem("band_exp_ready")
        s_p = sem("band_p_ready")
        s_gnv = sem("group_var_ready")
        s_gnr = sem("group_rstd_ready")
        s_silu = sem("gate_silu_ready")
        s_gs = sem("gate_gain_ready")
        s_ob = sem("ret_out_ready")
        s_xmax = sem("cross_max_ready")
        s_xexp = sem("cross_exp_ready")
        s_xp = sem("cross_p_ready")
        s_rmax = sem("router_max_ready")
        s_rexp = sem("router_exp_ready")
        s_comb = sem("combine_ready")
        s_y = sem("y_ready")

        def wait_filled(eng, *key):
            eng.wait_ge(filled, INDEX[key] + 1)

        def wait_emptied(eng, *key):
            who, n = DRAIN[key]
            eng.wait_ge(emptied[who], n)

        class Steps:

            def __init__(self, eng, who):
                self.eng, self.own, self.count, self.last, self.who = eng, s_own[who], {}, None, who

            def did(self, instruction, signal=None):
                s = self.own if signal is None else signal
                instruction.then_inc(s, 1)
                self.count[id(s)] = self.count.get(id(s), 0) + 1
                self.last = (s, self.count[id(s)])

            def emptied(self, instruction, *key):
                assert DRAIN[key][0] == self.who, key
                self.did(instruction, emptied[self.who])
                assert self.count[id(emptied[self.who])] == DRAIN[key][1], key

            def settle(self):
                self.eng.wait_ge(*self.last)

        def ready_x(eng, n, t):
            l, k = divmod(n, 3)
            if n == 0:
                eng.wait_ge(s_x, 32)
            elif n == 3 * DEPTH:
                wait_emptied(eng, "down", l - 1, NE - 1, 1, t)
            elif k == 0:
                wait_emptied(eng, "down", l - 1, 1, 1, t)
            else:
                wait_emptied(eng, ("out", "o")[k - 1], l, 1, t)

        block = ctx.enter_context(nc.Block())

        @block.sync
        def _(sp):
            for s, (name, how, where, _) in enumerate(SLABS):
                if s >= R:
                    wait_filled(sp, *SLABS[s - R][3])
                base = ring[:, (s % R) * SLAB:(s % R + 1) * SLAB]
                if how == "rows":
                    l, k0, nk, c0, w = where
                    src = a[name][l].rearrange("(k p) n -> p k n", p=P)[:, k0:k0 + nk, c0:c0 + w]
                    dst = base[:, 0:nk * w].rearrange("p (k n) -> p k n", k=nk)
                elif how == "past":
                    l, g = where
                    src = a[name][l, 4 * g:4 * g + 4].rearrange("n (k p) h d -> p (n k) (h d)", p=P)
                    dst = base.rearrange("p (j d) -> p j d", j=8)
                elif how == "mem":
                    l, n = where
                    src = a[name][l, n].rearrange("(m p) h d -> p m (h d)", p=P)
                    dst = base.rearrange("p (j d) -> p j d", j=2)
                elif how == "ff":
                    l, e, k0, nk, c0, w = where
                    if l % 2:
                        t_, q0_ = a["moe_w_" + name][l // 2, e], c0
                    else:
                        t_, q0_ = a["ffn_w_" + name][l // 2], e * FF + c0
                    src = t_.rearrange("(k p) n -> p k n", p=P)[:, k0:k0 + nk, q0_:q0_ + w]
                    dst = base[:, 0:nk * w].rearrange("p (k n) -> p k n", k=nk)
                else:
                    l, e, k0, nk, c0 = where
                    if l % 2:
                        t_, r0 = a["moe_w_down"][l // 2, e], k0
                    else:
                        t_, r0 = a["ffn_w_down"][l // 2], e * FFK + k0
                    src = t_.rearrange("(k p) n -> p k n", p=P)[:, r0:r0 + nk, c0:c0 + 512]
                    dst = base[:, 0:nk * 512].rearrange("p (k n) -> p k n", k=nk)
                sp.dma_start(dst, src).then_inc(slab_in[s % R], 16)

        @block.tensor
        def _(pe):
            at = [0, 0]

            def begin(*key):
                for prev in PREV[key]:
                    wait_emptied(pe, *prev)
                return bank[BANK[key][0]]

            def end(instruction, *key):
                assert JOBS[at[0]][0] == key, (JOBS[at[0]][0], key)
                at[0] += 1
                instruction.then_inc(filled, 1)

            def slab(name):
                s = at[1]
                at[1] += 1
                assert SLABS[s][0] == name, (SLABS[s], name)
                pe.wait_ge(slab_in[s % R], 16 * (s // R + 1))
                return ring[:, (s % R) * SLAB:(s % R + 1) * SLAB]

            def turn(out, src):
                return nc.tensor.transpose(out, src, ident[0:src.shape[0], 0:src.shape[0]])

            def product(key, name, left, groups, w, tiles, c, ready=None):
                for g, (k0, nk) in enumerate(groups):
                    wt = slab(name)[:, 0:nk * w].rearrange("p (k n) -> p k n", k=nk)
                    for t in range(tiles):
                        if g == 0:
                            begin(*key, c, t)
                        out = bank[BANK[key + (c, t)][0]]
                        for k in range(k0, k0 + nk):
                            if ready:
                                ready(k, t)
                            ins = nc.tensor.matmul(out[:, 0:w], left(k, t), wt[:, k - k0, :],
                                                   start=(g == 0 and k == k0),
                                                   stop=(g == len(groups) - 1 and k == k0 + nk - 1))
                        if g == len(groups) - 1:
                            end(ins, *key, c, t)

            halves = [(0, 4), (4, 4)]

            def hT_at(k, t):
                return hT[:, k, t * P:(t + 1) * P]

            def oT_at(k, t):
                return oT[:, k, t * P:(t + 1) * P]

            def norm(n):
                for t in range(NT):
                    pe.wait_ge(s_h, NT * n + t + 1)
                    for half in range(2):
                        b = begin("hT", n, t, half)
                        for j in range(4):
                            k = 4 * half + j
                            ins = turn(b[:, j * P:(j + 1) * P], htok[:, t, k * P:(k + 1) * P])
                        end(ins, "hT", n, t, half)
                wait_emptied(pe, "hT", n, NT - 1, 1)

            pe.wait_ge(s_const, 16)
            pe.wait_ge(s_gain, 48)
            b = begin("gains")
            end(turn(b[:, 0:48], grow[0:48, :]), "gains")
            pe.wait_ge(s_mem, 16)
            for j in range(4):
                b = begin("memT", j)
                for k in range(2):
                    for t in range(2):
                        ins = turn(b[:, k * 256 + t * P:k * 256 + (t + 1) * P],
                                   memtok[:, t, (2 * j + k) * P:(2 * j + k + 1) * P])
                end(ins, "memT", j)
            for l in range(DEPTH):
                norm(3 * l)
                pe.wait_ge(s_cw, 32 * (l + 1))
                b = begin("cw", l)
                for k in range(2):
                    ins = turn(b[:, 32 * k:32 * k + 32], cwr[0:32, k * P:(k + 1) * P])
                end(ins, "cw", l)
                pe.wait_ge(s_cbuf, 16 * (l + 1))
                b = begin("cbuf", l)
                for k in range(2):
                    for g in range(2):
                        ins = turn(b[:, 240 * k + 120 * g:240 * k + 120 * g + 120],
                                   cbufr[0:120, g, k * P:(k + 1) * P])
                end(ins, "cbuf", l)
                for c, (c0, w) in enumerate(IN_CHUNKS):
                    product(("in", l), "w_in", hT_at, halves, w, NT, c)
                    if c == 1:
                        pe.wait_ge(s_u, l + 1)
                        for k in range(2):
                            b = begin("uT", l, k)
                            for t in range(NT):
                                ins = turn(b[:, t * P:(t + 1) * P], proj[:, t, CA + k * P:CA + (k + 1) * P])
                            end(ins, "uT", l, k)
                for c in range(2):
                    product(("mk", l), "wx_k", lambda k, t: memT[:, k, t * P:(t + 1) * P], halves, 512, 2, c,)
                for c in range(2):
                    product(("mv", l), "wx_v", lambda k, t: memT[:, k, t * P:(t + 1) * P], halves, 512, 2, c)
                wait_emptied(pe, "mk", l, 1, 1)
                for j in range(4):
                    b = begin("mkT", l, j)
                    for k in range(2):
                        for t in range(2):
                            ins = turn(b[:, k * 256 + t * P:k * 256 + (t + 1) * P],
                                       mk[:, t, (2 * j + k) * P:(2 * j + k + 1) * P])
                    end(ins, "mkT", l, j)
                for t in range(NT):
                    b = begin("qkA", l, t)
                    for j in range(4):
                        ins = turn(b[:, j * P:(j + 1) * P], proj[:, t, j * P:(j + 1) * P])
                    end(ins, "qkA", l, t)
                for t in range(NT):
                    pe.wait_ge(s_rot, NT * l + t + 1)
                    b = begin("qkB", l, t)
                    for j in range(4):
                        ins = turn(b[:, j * P:(j + 1) * P], proj[:, t, QB + j * P:QB + (j + 1) * P])
                    end(ins, "qkB", l, t)
                wait_emptied(pe, "qkA", l, 2)
                for j in range(4):
                    b = begin("sA", l, j)
                    t, odd = divmod(j, 2)
                    w = (t + 1) * P
                    for i in range(2):
                        ins = nc.tensor.matmul(b[:, i * w:(i + 1) * w],
                                               qkA[64 * odd:64 * odd + 64, i, t * P:(t + 1) * P],
                                               qkA[64 * odd:64 * odd + 64, 2 + i, 0:w], start=True, stop=True)
                    end(ins, "sA", l, j)
                pe.wait_ge(s_blk, l + 1)
                past = None
                for n in range(NS):
                    if n % 4 == 0:
                        past = slab("cache_attn_k").rearrange("p (j d) -> p j d", j=8)
                    b = begin("ktA", l, n)
                    for k in range(2):
                        for t in range(2):
                            ins = turn(b[:, k * 256 + t * P:k * 256 + (t + 1) * P],
                                       past[:, 2 * (n % 4) + t, k * P:(k + 1) * P])
                    end(ins, "ktA", l, n)
                    if n % 2:
                        r = n // 2
                        wait_emptied(pe, "ktA", l, n)
                        b = begin("sS", l, r)
                        for n2 in range(2):
                            for k in range(2):
                                g = 32 * (2 * n2 + k)
                                s_ = 2 * r + n2
                                nc.tensor.matmul(b[g:g + 32, 0:256], qblk[:, k, s_, :], ktA[:, s_ % 4, k, :],
                                                 start=True, stop=True)
                                ins = nc.tensor.matmul(b[g:g + 32, 256:384], qblk[:, k, s_, :],
                                                       qkA[:, 2 + k, 256:384], start=True, stop=True)
                        end(ins, "sS", l, r)
                for h in range(AH):
                    pe.wait_ge(s_p, 6 * l + 2)
                    b = begin("pTA", l, h)
                    turn(b[:, 0:P], lg0[:, h, :])
                    turn(b[:, P:2 * P], lg1[:, h, 0:P])
                    end(turn(b[:, 2 * P:3 * P], lg1[:, h, P:2 * P]), "pTA", l, h)
                wait_emptied(pe, "pTA", l, AH - 1)
                b = begin("oA", l)
                for h in range(AH):
                    lo = 64 * (h % 2)
                    col = 256 * (h // 2)
                    nc.tensor.matmul(b[lo:lo + 64, col:col + 256], proj[:, 0, VA + 64 * h:VA + 64 * h + 64],
                                     pTA[:, h, 0:256], start=True, stop=False)
                    ins = nc.tensor.matmul(b[lo:lo + 64, col + P:col + 256],
                                           proj[:, 1, VA + 64 * h:VA + 64 * h + 64],
                                           pTA[:, h, 256:384], start=False, stop=True)
                end(ins, "oA", l)
                for r in range(4):
                    pe.wait_ge(s_p, 6 * l + 3 + r)
                    b = begin("pTS", l, r)
                    for k in range(3):
                        ins = turn(b[:, k * P:(k + 1) * P], lgS[:, r, k * P:(k + 1) * P])
                    end(ins, "pTS", l, r)
                wait_emptied(pe, "pTS", l, 3)
                b = begin("oS", l)
                for n in range(NS):
                    if n % 4 == 0:
                        past = slab("cache_attn_v").rearrange("p (j d) -> p j d", j=8)
                    for k in range(2):
                        row = 64 * (n % 2) + 32 * k
                        out = b[:, (2 * n + k) * 32:(2 * n + k) * 32 + 32]
                        for t in range(3):
                            left = (past[:, 2 * (n % 4) + t, k * P:(k + 1) * P] if t < 2
                                    else proj[:, 2, VA + k * P:VA + (k + 1) * P])
                            ins = nc.tensor.matmul(out, left, pTS[:, n // 2, t, row:row + 32],
                                                   start=(t == 0), stop=(t == 2))
                end(ins, "oS", l)
                wait_emptied(pe, "qkB", l, 2)
                for h in range(BH):
                    lo = 64 * (h % 2)
                    b = begin("aB", l, h)
                    nc.tensor.matmul(b[:, 0:256], qkB[lo:lo + 64, 2 + h // 2, 0:P], qkB[lo:lo + 64, h // 2, 0:256],
                                     start=True, stop=True)
                    end(nc.tensor.matmul(b[:, 256:384], qkB[lo:lo + 64, 2 + h // 2, P:2 * P],
                                         qkB[lo:lo + 64, h // 2, P:2 * P], start=True, stop=True), "aB", l, h)
                for odd in range(2):
                    b = begin("aS", l, odd)
                    for i in range(2):
                        ins = nc.tensor.matmul(b[:, i * P:(i + 1) * P], qkB[64 * odd:64 * odd + 64, 2 + i, 256:384],
                                               qkB[64 * odd:64 * odd + 64, i, 256:384], start=True, stop=True)
                    end(ins, "aS", l, odd)
                wait_emptied(pe, "aS", l, 1)
                pe.wait_ge(s_q0, BH * (l + 1))
                pe.wait_ge(s_s0, 128 * (l + 1))
                for t in range(NT):
                    b = begin("oB", l, t)
                    for h in range(BH):
                        out = b[:, h * P:(h + 1) * P]

                        def v(j):
                            return proj[:, j, VB + h * P:VB + (h + 1) * P]
                        if t == 0:
                            ins = nc.tensor.matmul(out, attT[:, h, 0:P], v(0), start=True, stop=True)
                        elif t == 1:
                            nc.tensor.matmul(out, attT[:, h, P:256], v(0), start=True, stop=False)
                            ins = nc.tensor.matmul(out, attT[:, h, 256:384], v(1), start=False, stop=True)
                        else:
                            nc.tensor.matmul(out, attS[:, h, :], v(2), start=True, stop=False)
                            for j in range(4):
                                ins = nc.tensor.matmul(out, q0[:, h, j * P:(j + 1) * P], s0[:, j, h, :],
                                                       start=False, stop=(j == 3))
                    end(ins, "oB", l, t)
                pe.wait_ge(s_kd, 2 * l + 1)
                b = begin("nsP", l)
                for h in range(BH):
                    for t in range(2):
                        ins = nc.tensor.matmul(b[0:64, h * P:(h + 1) * P], kd[:, t, h * 64:(h + 1) * 64],
                                               proj[:, t, VB + h * P:VB + (h + 1) * P], start=(t == 0), stop=(t == 1))
                end(ins, "nsP", l)
                pe.wait_ge(s_kd, 2 * l + 2)
                for h in range(BH):
                    b = begin("nsS", l, h)
                    for j in range(4):
                        ins = nc.tensor.matmul(b[:, j * P:(j + 1) * P], ks[:, h, 2 * j:2 * j + 2, :],
                                               proj[:, 2, VB + h * P:VB + (h + 1) * P], start=True, stop=True)
                    end(ins, "nsS", l, h)
                pe.wait_ge(s_conv, 2 * (l + 1))
                for t in range(NT):
                    b = begin("yc", l, t)
                    for k in range(2):
                        ins = turn(b[:, k * P:(k + 1) * P], conv[:, k, t * P:(t + 1) * P])
                    end(ins, "yc", l, t)
                pe.wait_ge(s_ob, NT * (l + 1))
                for k in range(4):
                    b = begin("obT", l, k)
                    for t in range(NT):
                        ins = turn(b[:, t * P:(t + 1) * P], proj[:, t, GB + k * P:GB + (k + 1) * P])
                    end(ins, "obT", l, k)
                pe.wait_ge(s_oc, l + 1)
                for k in range(2):
                    b = begin("ocT", l, k)
                    for t in range(NT):
                        ins = turn(b[:, t * P:(t + 1) * P], proj[:, t, CA + k * P:CA + (k + 1) * P])
                    end(ins, "ocT", l, k)
                wait_emptied(pe, "ocT", l, 1)
                for c in range(2):
                    product(("out", l), "w_out", oT_at, halves, 512, NT, c)
                norm(3 * l + 1)
                for c in range(2):
                    product(("q", l), "wx_q", hT_at, halves, 512, NT, c)
                wait_emptied(pe, "q", l, 1, 2)
                for j in range(4):
                    b = begin("qTx", l, j)
                    for k in range(2):
                        for t in range(2):
                            ins = turn(b[:, k * 256 + t * P:k * 256 + (t + 1) * P],
                                       qx[:, t, (2 * j + k) * P:(2 * j + k + 1) * P])
                    end(ins, "qTx", l, j)
                for j in range(2):
                    b = begin("qTs", l, j)
                    for k in range(4):
                        ins = turn(b[:, k * P:(k + 1) * P], qx[:, 2, (4 * j + k) * P:(4 * j + k + 1) * P])
                    end(ins, "qTs", l, j)
                wait_emptied(pe, "qTs", l, 1)
                for j in range(4):
                    b = begin("xs", l, j)
                    for i in range(2):
                        h = 2 * (j % 2) + i
                        for k in range(2):
                            ins = nc.tensor.matmul(b[:, i * 256:(i + 1) * 256],
                                                   qxT[:, 2 * h + k, (j // 2) * P:(j // 2 + 1) * P],
                                                   mkT[:, 2 * h + k, :], start=(k == 0), stop=(k == 1))
                    end(ins, "xs", l, j)
                pe.wait_ge(s_xp, 6 * l + 2)
                for h in range(XH):
                    b = begin("xpT", l, h)
                    for mt in range(2):
                        for t in range(2):
                            ins = turn(b[:, mt * 256 + t * P:mt * 256 + (t + 1) * P],
                                       px[:, t, h, mt * P:(mt + 1) * P])
                    end(ins, "xpT", l, h)
                wait_emptied(pe, "xpT", l, XH - 1)
                for h in range(XH):
                    b = begin("xo", l, h)
                    for i in range(2):
                        for mt in range(2):
                            ins = nc.tensor.matmul(b[:, i * 256:(i + 1) * 256],
                                                   mv[:, mt, (2 * h + i) * P:(2 * h + i + 1) * P],
                                                   pxT[:, h, mt, :], start=(mt == 0), stop=(mt == 1))
                    end(ins, "xo", l, h)
                for r in range(5):
                    if r < 4:
                        for n2 in range(2):
                            mem = slab("cache_mem_k").rearrange("p (m d) -> p m d", m=2)
                            for j in range(4):
                                b = begin("kTs", l, 2 * r + n2, j)
                                for k in range(2):
                                    for mt in range(2):
                                        ins = turn(b[:, k * 256 + mt * P:k * 256 + (mt + 1) * P],
                                                   mem[:, mt, (2 * j + k) * P:(2 * j + k + 1) * P])
                                end(ins, "kTs", l, 2 * r + n2, j)
                        wait_emptied(pe, "kTs", l, 2 * r + 1, 2)
                        wait_emptied(pe, "kTs", l, 2 * r + 1, 3)
                        b = begin("xss", l, r)
                        for n2 in range(2):
                            for hp in range(2):
                                g = 32 * (2 * n2 + hp)
                                for i in range(4):
                                    ins = nc.tensor.matmul(b[g:g + 32, 0:256], qxb[:, 4 * hp + i, 2 * r + n2, :],
                                                           kTs[:, n2, 4 * hp + i, :], start=(i == 0), stop=(i == 3))
                        end(ins, "xss", l, r)
                    if r >= 1:
                        q = r - 1
                        pe.wait_ge(s_xp, 6 * l + 3 + q)
                        b = begin("xpTs", l, q)
                        for mt in range(2):
                            ins = turn(b[:, mt * P:(mt + 1) * P], pxs[:, q % 2, mt * P:(mt + 1) * P])
                        end(ins, "xpTs", l, q)
                        wait_emptied(pe, "xpTs", l, q)
                        if q == 0:
                            begin("xos", l)
                        for n2 in range(2):
                            n = 2 * q + n2
                            mem = slab("cache_mem_v").rearrange("p (m d) -> p m d", m=2)
                            for k in range(KC):
                                col = 64 * n2 + TS * (k // 2)
                                out = bank[k // 4][:, (k % 4) * P + TS * n:(k % 4) * P + TS * (n + 1)]
                                for mt in range(2):
                                    ins = nc.tensor.matmul(out, mem[:, mt, k * P:(k + 1) * P],
                                                           pxsT[:, q % 2, mt, col:col + TS],
                                                           start=(mt == 0), stop=(mt == 1))
                end(ins, "xos", l)
                wait_emptied(pe, "xos", l)
                for c in range(2):
                    product(("o", l), "wx_o", oT_at, halves, 512, NT, c)
                norm(3 * l + 2)
                if l % 2:
                    pe.wait_ge(s_rw, 16)
                    b = begin("route", l)
                    for t in range(NT):
                        for k in range(KC):
                            ins = nc.tensor.matmul(b[:, t * NE:(t + 1) * NE], hT_at(k, t), rw[:, k, :],
                                                   start=(k == 0), stop=(k == KC - 1))
                    end(ins, "route", l)
                for e in range(NE if l % 2 else 2):
                    for c in range(4):
                        if c < 3:
                            w = FF_CHUNKS[c][1]
                            product(("gate", l, e), "gate", hT_at, halves, w, NT, c)
                            product(("up", l, e), "up", hT_at, halves, w, NT, c)
                        if c:
                            for t in range(NT):
                                wait_emptied(pe, "up", l, e, c - 1, t)
                                b = begin("aT", l, e, c - 1, t)
                                for j in range(FF_GROUPS[c - 1][1]):
                                    ins = turn(b[:, j * P:(j + 1) * P],
                                               acts[:, NT * ((c - 1) % 2) + t, j * P:(j + 1) * P])
                                end(ins, "aT", l, e, c - 1, t)
                    wait_emptied(pe, "aT", l, e, 2, NT - 1)
                    for c in range(2):
                        product(("down", l, e), "down", lambda k, t: actT[:, k, t * P:(t + 1) * P],
                                FF_GROUPS, 512, NT, c)
            assert at == [len(JOBS), len(SLABS)]

        @block.scalar
        def _(act):
            st = Steps(act, "a")
            A = nc.scalar.activation

            def copy(out, in_, *key):
                wait_filled(act, *key)
                st.emptied(A(out, in_, ACT.Copy), *key)

            def squares(n):
                for t in range(NT):
                    ready_x(act, n, t)
                    st.did(A(htok[:, t, :], x[:, t, :], ACT.Square, accum_out=stat[:, t:t + 1]), s_sq)

            act.dma_start(x[:, 0:2, :], a["x_prompt"].rearrange("b (t p) d -> p (b t) d", p=P)).then_inc(s_x, 16)
            act.dma_start(x[:, 2, :], a["x_sample"].rearrange("n t d -> (n t) d")).then_inc(s_x, 16)
            act.dma_start(memtok, a["mem_prompt"].rearrange("b (t p) d -> p (b t) d", p=P)).then_inc(s_mem, 16)
            copy(gT[:, 0:48], bank[BANK[("gains",)][0]][:, 0:48], "gains")
            for j in range(4):
                copy(memT[:, 2 * j:2 * j + 2, :],
                     bank[BANK[("memT", j)][0]][:, :].rearrange("p (k n) -> p k n", k=2), "memT", j)
            squares(0)
            for l in range(DEPTH):
                copy(cw, bank[BANK[("cw", l)][0]][:, 0:64].rearrange("p (k n) -> p k n", k=2), "cw", l)
                b = bank[BANK[("cbuf", l)][0]]
                wait_filled(act, "cbuf", l)
                for k in range(2):
                    ins = A(us[:, k, :, 0:30], b[:, 240 * k:240 * k + 240].rearrange("p (n w) -> p n w", n=NS), ACT.Copy)
                    if k:
                        st.emptied(ins, "cbuf", l)

                def in_chunk(c):
                    c0, w = IN_CHUNKS[c]
                    for t in range(NT):
                        copy(proj[:, t, c0:c0 + w], bank[BANK[("in", l, c, t)][0]][:, 0:w], "in", l, c, t)
                in_chunk(0)
                st.settle()
                for t in range(NT):
                    st.did(A(sig[:, t, :], proj[:, t, CB:CB + CC], ACT.Sigmoid), s_sig)
                in_chunk(1)
                for k in range(2):
                    b = bank[BANK[("uT", l, k)][0]]
                    wait_filled(act, "uT", l, k)
                    A(up[:, k, 30:30 + SEQ], b[:, 0:SEQ], ACT.Copy)
                    st.emptied(A(us[:, k, :, 30:46], b[:, SEQ:TOK].rearrange("p (n w) -> p n w", n=NS), ACT.Copy),
                               "uT", l, k)
                for c in range(2, len(IN_CHUNKS)):
                    in_chunk(c)
                st.settle()
                pk = o["new_attn_k_prompt"][l, 0].rearrange("(t p) h d -> p t (h d)", p=P)
                pv = o["new_attn_v_prompt"][l, 0].rearrange("(t p) h d -> p t (h d)", p=P)
                act.dma_start(pk, proj[:, 0:2, KA:KA + 256]).then_inc(s_kvo, 16)
                act.dma_start(pv, proj[:, 0:2, VA:VA + 256]).then_inc(s_kvo, 16)
                act.dma_start(o["new_attn_k_sample"][l].rearrange("n t h d -> (n t) (h d)"),
                              proj[:, 2, KA:KA + 256]).then_inc(s_kvo, 16)
                act.dma_start(o["new_attn_v_sample"][l].rearrange("n t h d -> (n t) (h d)"),
                              proj[:, 2, VA:VA + 256]).then_inc(s_kvo, 16)
                for t in range(NT):
                    st.did(A(proj[:, t, GB:GB + 512], proj[:, t, GB:GB + 512], ACT.Silu), s_silu)
                for name, dst in (("mk", mk), ("mv", mv)):
                    for c in range(2):
                        for t in range(2):
                            copy(dst[:, t, c * 512:(c + 1) * 512], bank[BANK[(name, l, c, t)][0]][:, :], name, l, c, t)
                for j in range(4):
                    copy(mkT[:, 2 * j:2 * j + 2, :],
                         bank[BANK[("mkT", l, j)][0]][:, :].rearrange("p (k n) -> p k n", k=2), "mkT", l, j)
                st.settle()
                act.dma_start(o["new_mem_k_prompt"][l, 0].rearrange("(t p) h d -> p t (h d)", p=P), mk).then_inc(s_mko, 16)
                act.dma_start(o["new_mem_v_prompt"][l, 0].rearrange("(t p) h d -> p t (h d)", p=P), mv).then_inc(s_mko, 16)
                for kind, dst in (("qkA", qkA), ("qkB", qkB)):
                    for t in range(NT):
                        copy(dst[:, :, t * P:(t + 1) * P],
                             bank[BANK[(kind, l, t)][0]][:, :].rearrange("p (k n) -> p k n", k=4), kind, l, t)

                def softmax_exp(dst, neg_max, sums, value, last):
                    ins = A(dst, dst, ACT.Exp, bias=neg_max, accum_out=sums)
                    st.did(ins, s_exp if last else None)

                def exp_prompt():
                    act.wait_ge(s_max, 6 * l + 2)
                    for h in range(AH):
                        softmax_exp(lg0[:, h, :], small[:, h:h + 1], small[:, 16 + h:17 + h], 0, False)
                    for h in range(AH):
                        softmax_exp(lg1[:, h, :], small[:, 4 + h:5 + h], small[:, 20 + h:21 + h], 0, h == AH - 1)

                def exp_sample(r):
                    act.wait_ge(s_max, 6 * l + 3 + r)
                    softmax_exp(lgS[:, r, :], small[:, 8 + r:9 + r], small[:, 24 + r:25 + r], 0, True)

                for n in range(NS):
                    copy(ktA[:, n % 4, :, :],
                         bank[BANK[("ktA", l, n)][0]][:, :].rearrange("p (k n) -> p k n", k=2), "ktA", l, n)
                    if n == 3:
                        exp_prompt()
                    if n % 2 and n >= 5:
                        exp_sample((n - 5) // 2)
                exp_sample(2)
                exp_sample(3)
                for h in range(AH):
                    copy(pTA[:, h, :], bank[BANK[("pTA", l, h)][0]][:, 0:TOK], "pTA", l, h)
                copy(oT[:, 0:2, 0:SEQ], bank[BANK[("oA", l)][0]][:, :].rearrange("p (k n) -> p k n", k=2), "oA", l)
                for r in range(4):
                    copy(pTS[:, r, :, :], bank[BANK[("pTS", l, r)][0]][:, 0:TOK].rearrange("p (k n) -> p k n", k=3),
                         "pTS", l, r)
                b = bank[BANK[("oS", l)][0]]
                wait_filled(act, "oS", l)
                for i in range(2):
                    for k in range(2):
                        src = b[64 * i:64 * i + 64, :].rearrange("p (n k c) -> p n k c", n=NS, k=2)[
                            :, :, k, TS * i:TS * i + TS]
                        dst = oT[64 * i:64 * i + 64, k, SEQ:TOK].rearrange("p (n w) -> p n w", n=NS)
                        ins = A(dst, src, ACT.Copy)
                st.emptied(ins, "oS", l)
                wait_filled(act, "nsP", l)
                st.emptied(A(spr[0:64, :], bank[BANK[("nsP", l)][0]][0:64, :], ACT.Copy), "nsP", l)
                st.settle()
                act.dma_start(o["new_ret_prompt"][l, 0].rearrange("h k v -> k h v"),
                              spr[0:64, :].rearrange("p (h v) -> p h v", h=BH)).then_inc(s_spo, 16)
                act.wait_ge(s_lnr, 2 * l + 2)
                A(proj[:, :, CA:CA + CC], proj[:, :, CA:CA + CC], ACT.Silu).then_inc(s_oc, 1)
                for k in range(4):
                    copy(oT[:, 2 + k, :], bank[BANK[("obT", l, k)][0]][:, 0:TOK], "obT", l, k)
                for k in range(2):
                    copy(oT[:, 6 + k, :], bank[BANK[("ocT", l, k)][0]][:, 0:TOK], "ocT", l, k)
                wait_emptied(act, "nsS", l, BH - 1)
                for n2 in range(2):
                    dst = o["new_ret_sample"][l].rearrange("(j s) h k v -> s k j h v", s=2)[n2]
                    for j in range(4):
                        act.dma_start(dst[:, j], s0[64 * n2:64 * n2 + 64, j]).then_inc(s_st, 16)
                act.wait_ge(s_kvo, 64 * (l + 1))
                act.wait_ge(s_outp, 48 * (l + 1))
                act.wait_ge(s_spo, 16 * (l + 1))
                squares(3 * l + 1)
                for c in range(2):
                    for t in range(NT):
                        copy(qx[:, t, c * 512:(c + 1) * 512], bank[BANK[("q", l, c, t)][0]][:, :], "q", l, c, t)
                for j in range(4):
                    copy(qxT[:, 2 * j:2 * j + 2, :],
                         bank[BANK[("qTx", l, j)][0]][:, :].rearrange("p (k n) -> p k n", k=2), "qTx", l, j)
                act.wait_ge(s_zero, l + 1)
                for j in range(2):
                    b = bank[BANK[("qTs", l, j)][0]]
                    wait_filled(act, "qTs", l, j)
                    for k in range(4):
                        c0 = TS * (k // 2)
                        ins = A(qxb[:, 4 * j + k, :, c0:c0 + TS],
                                b[:, k * P:(k + 1) * P].rearrange("p (n w) -> p n w", n=NS), ACT.Copy)
                    st.emptied(ins, "qTs", l, j)
                for j in range(4):
                    act.wait_ge(s_xmax, 8 * l + j + 1)
                    b = bank[BANK[("xs", l, j)][0]]
                    for i in range(2):
                        c = 2 * j + i
                        ins = A(px[:, j // 2, 2 * (j % 2) + i, :], b[:, i * 256:(i + 1) * 256], ACT.Exp,
                                bias=small[:, 32 + c:33 + c], scale=XD ** -0.5, accum_out=small[:, 40 + c:41 + c])
                        if i == 0:
                            st.did(ins)
                    st.emptied(ins, "xs", l, j)
                for h in range(XH):
                    copy(pxT[:, h, :, :], bank[BANK[("xpT", l, h)][0]][:, :].rearrange("p (k n) -> p k n", k=2),
                         "xpT", l, h)
                for h in range(XH):
                    copy(oT[:, 2 * h:2 * h + 2, 0:SEQ],
                         bank[BANK[("xo", l, h)][0]][:, :].rearrange("p (k n) -> p k n", k=2), "xo", l, h)
                for r in range(5):
                    if r < 4:
                        for n2 in range(2):
                            for j in (0, 2):
                                copy(kTs[:, n2, 2 * j:2 * j + 2, :],
                                     bank[BANK[("kTs", l, 2 * r + n2, j)][0]][:, :].rearrange("p (k n) -> p k n", k=2),
                                     "kTs", l, 2 * r + n2, j)
                        act.wait_ge(s_xmax, 8 * l + 5 + r)
                        if r >= 2:
                            wait_filled(act, "xpTs", l, r - 2)
                        st.emptied(A(pxs[:, r % 2, :], bank[BANK[("xss", l, r)][0]][:, 0:NMEM], ACT.Exp,
                                     bias=small[:, 48 + r:49 + r], scale=XD ** -0.5,
                                     accum_out=small[:, 52 + r:53 + r]), "xss", l, r)
                    if r >= 1:
                        copy(pxsT[:, (r - 1) % 2, :, :],
                             bank[BANK[("xpTs", l, r - 1)][0]][:, 0:2 * P].rearrange("p (k n) -> p k n", k=2),
                             "xpTs", l, r - 1)
                wait_filled(act, "xos", l)
                for k in range(2):
                    ins = A(oT[:, 4 * k:4 * k + 4, SEQ:TOK], bank[k][:, :].rearrange("p (k n) -> p k n", k=4), ACT.Copy)
                st.emptied(ins, "xos", l)
                squares(3 * l + 2)
                if l % 2:
                    act.wait_ge(s_rmax, 1)
                    for t in range(NT):
                        ins = A(rtv(1)[:, t, :], rtv(0)[:, t, :], ACT.Exp, bias=stat[:, 8 + t:9 + t],
                                accum_out=stat[:, 12 + t:13 + t])
                        st.did(ins, s_rexp)
                for e in range(NE if l % 2 else 2):
                    for c in range(4):
                        if c < 3:
                            w = FF_CHUNKS[c][1]
                            for t in range(NT):
                                if (l, e, c) != (0, 0, 0):
                                    pe_, pc = (e, c - 1) if c else ((e - 1, 2) if e else (1, 2))
                                    pl = l if (c or e) else l - 1
                                    wait_emptied(act, "up", pl, pe_, pc, t)
                                wait_filled(act, "gate", l, e, c, t)
                                st.emptied(A(gated[:, t, 0:w], bank[t][:, 0:w], ACT.Silu), "gate", l, e, c, t)
                        if c:
                            k0, nk = FF_GROUPS[c - 1]
                            for t in range(NT):
                                copy(actT[:, k0:k0 + nk, t * P:(t + 1) * P],
                                     bank[BANK[("aT", l, e, c - 1, t)][0]][:, 0:nk * P].rearrange(
                                         "p (k n) -> p k n", k=nk), "aT", l, e, c - 1, t)
                squares(3 * l + 3)
            for t in range(NT):
                act.wait_ge(s_y, t + 1)
                if t < 2:
                    act.dma_start(o["y_prompt"][0, t * P:(t + 1) * P, :], htok[:, t, :]).then_inc(s_yo, 16)
                else:
                    act.dma_start(o["y_sample"].rearrange("n t d -> (n t) d"), htok[:, t, :]).then_inc(s_yo, 16)
            act.wait_ge(s_kvo, 64 * DEPTH)
            act.wait_ge(s_mko, 32 * DEPTH)
            act.wait_ge(s_spo, 16 * DEPTH)
            act.wait_ge(s_yo, 16 * NT)
            act.wait_ge(s_st, 16 * 8 * DEPTH)

        def route(dve, st):
            V = nc.vector

            def go(ins, signal=None):
                st.did(ins, signal)
                st.settle()
            lgts, e_, p_, w_, h1, h2, p2 = (rtv(i) for i in range(7))
            r3 = rt[:, 7 * NT * NE:7 * NT * NE + 24]
            m1, m2, mw, den = (r3[:, 3 * i:3 * i + 3] for i in range(4))
            wait_filled(dve, "route", 1)
            st.emptied(V.tensor_copy(lgts, bank[BANK[("route", 1)][0]][:, 0:NT * NE].rearrange(
                "p (t e) -> p t e", t=NT)), "route", 1)
            st.settle()
            go(V.tensor_reduce(stat[:, 8:11], lgts, AX.X, ALU.max, negate=True), s_rmax)
            dve.wait_ge(s_rexp, NT)
            go(V.reciprocal(stat[:, 12:15], stat[:, 12:15]))
            go(V.tensor_tensor(p_, e_, insert(stat[:, 12:15], 2, NE), ALU.mult))
            order = insert(eight, 1, NT)
            go(V.tensor_reduce(m1, p_, AX.X, ALU.max))
            go(V.tensor_tensor(w_, p_, insert(m1, 2, NE), ALU.is_equal))
            go(V.tensor_tensor(w_, w_, order, ALU.mult))
            go(V.tensor_reduce(mw, w_, AX.X, ALU.max))
            go(V.tensor_tensor(h1, w_, insert(mw, 2, NE), ALU.is_equal))
            go(V.scalar_tensor_tensor(p2, h1, -2.0, p_, ALU.mult, ALU.add))
            go(V.tensor_reduce(m2, p2, AX.X, ALU.max))
            go(V.tensor_tensor(w_, p2, insert(m2, 2, NE), ALU.is_equal))
            go(V.tensor_tensor(w_, w_, order, ALU.mult))
            go(V.tensor_reduce(mw, w_, AX.X, ALU.max))
            go(V.tensor_tensor(h2, w_, insert(mw, 2, NE), ALU.is_equal))
            go(V.tensor_tensor(den, m1, m2, ALU.add))
            go(V.reciprocal(den, den))
            go(V.tensor_tensor(m1, m1, den, ALU.mult))
            go(V.tensor_tensor(m2, m2, den, ALU.mult))
            go(V.tensor_tensor(h1, h1, insert(m1, 2, NE), ALU.mult))
            go(V.tensor_tensor(h2, h2, insert(m2, 2, NE), ALU.mult))
            go(V.tensor_tensor(comb, h1, h2, ALU.add), s_comb)

        @block.vector
        def _(dve):
            st = Steps(dve, "v")
            V = nc.vector

            def norm_rows(n):
                for t in range(NT):
                    if t == 0:
                        dve.wait_ge(s_rstd, n + 1)
                    st.did(V.tensor_scalar(htok[:, t, :], x[:, t, :], stat[:, 4 + t:5 + t], None, ALU.mult), s_h)

            def norm_T(n):
                norm_rows(n)
                l, k = divmod(n, 3)
                for t in range(NT):
                    for half in range(2):
                        wait_filled(dve, "hT", n, t, half)
                        if n == 0 and t == 0 and half == 0:
                            wait_emptied(dve, "gains")
                        g0 = 16 * k + 8 * l + 4 * half
                        st.emptied(V.tensor_tensor(
                            hT[:, 4 * half:4 * half + 4, t * P:(t + 1) * P],
                            bank[BANK[("hT", n, t, half)][0]][:, :].rearrange("p (k n) -> p k n", k=4),
                            insert(gT[:, g0:g0 + 4], 2, P), ALU.mult), "hT", n, t, half)

            def add_x(name, l, *pre):
                for c in range(2):
                    for t in range(NT):
                        key = (name, l) + pre + (c, t)
                        wait_filled(dve, *key)
                        xs = x[:, t, c * 512:(c + 1) * 512]
                        st.emptied(V.tensor_tensor(xs, bank[BANK[key][0]][:, :], xs, ALU.add), *key)

            dve.wait_ge(s_relr, 16)
            st.did(V.tensor_copy(relx[0:8, 0:RPAD], relx[0:8, RPAD:RPAD + 1].to_broadcast([8, RPAD])), s_relx)
            dve.wait_ge(s_const, 16)
            for l in range(DEPTH):
                norm_T(3 * l)
                st.did(V.memset(up[:, :, 0:30], 0.0))
                dve.wait_ge(s_rel, 16 * 9 * (l + 1))
                st.did(V.tensor_tensor(rel_p[:, :, P:256], rel_p[:, :, P:256], insert(cmask, 1, AH), ALU.add))
                st.did(V.tensor_tensor(rel_n.rearrange("p r (n j) -> p (r n) j", j=TS),
                                       insert(rel_s[:, PAST:PAST + TS], 1, 32),
                                       smask.rearrange("p r (n j) -> p (r n) j", j=TS), ALU.add))
                dve.wait_ge(s_sig, NT * (l + 1))
                st.did(V.tensor_tensor(proj[:, :, CA:CA + CC], proj[:, :, CA:CA + CC], sig, ALU.mult), s_u)
                for k in range(2):
                    wait_emptied(dve, "uT", l, k)
                    outp = conv[:, k, 0:SEQ]
                    outs_ = conv[:, k, SEQ:TOK].rearrange("p (n w) -> p n w", n=NS)
                    for j in range(CW):
                        inp = up[:, k, j:j + SEQ]
                        ins_ = us[:, k, :, j:j + TS]
                        wj = cw[:, k, j:j + 1]
                        if j == 0:
                            st.did(V.tensor_scalar(outp, inp, wj, cw[:, k, 31:32], ALU.mult, ALU.add))
                            st.did(V.tensor_scalar(outs_, ins_, wj, cw[:, k, 31:32], ALU.mult, ALU.add))
                        else:
                            dve.wait_ge(st.own, st.count[id(st.own)] - 1)
                            st.did(V.scalar_tensor_tensor(outp, inp, wj, outp, ALU.mult, ALU.add))
                            dve.wait_ge(st.own, st.count[id(st.own)] - 1)
                            st.did(V.scalar_tensor_tensor(outs_, ins_, wj, outs_, ALU.mult, ALU.add),
                                   s_conv if j == CW - 1 else None)
                dve.wait_ge(s_mko, 32 * (l + 1))
                for j in range(4):
                    wait_filled(dve, "sA", l, j)
                    t, odd = divmod(j, 2)
                    w = (t + 1) * P
                    ins = V.scalar_tensor_tensor((lg0, lg1)[t][:, odd::2, :], bank[BANK[("sA", l, j)][0]][:, 0:2 * w].rearrange(
                        "p (h k) -> p h k", h=2), AD ** -0.5, rel_p[:, odd::2, 256 - w:256], ALU.mult, ALU.add)
                    st.emptied(ins, "sA", l, j)
                st.settle()
                st.did(V.tensor_reduce(small[:, 0:4], lg0, AX.X, ALU.max, negate=True), s_max)
                st.did(V.tensor_reduce(small[:, 4:8], lg1, AX.X, ALU.max, negate=True), s_max)
                for r in range(4):
                    wait_filled(dve, "sS", l, r)
                    b = bank[BANK[("sS", l, r)][0]]
                    st.did(V.scalar_tensor_tensor(lgS[:, r, 0:PAST], b[:, 0:PAST], AD ** -0.5, rel_s[:, 0:PAST],
                                                  ALU.mult, ALU.add))
                    st.emptied(V.scalar_tensor_tensor(lgS[:, r, PAST:TOK], b[:, PAST:TOK], AD ** -0.5, rel_n[:, r, :],
                                                      ALU.mult, ALU.add), "sS", l, r)
                    st.settle()
                    st.did(V.tensor_reduce(small[:, 8 + r:9 + r], lgS[:, r, :], AX.X, ALU.max, negate=True), s_max)
                dve.wait_ge(s_exp, 5 * l + 1)
                st.did(V.reciprocal(small[:, 16:24], small[:, 16:24]))
                st.settle()
                st.did(V.tensor_tensor(lg0, lg0, insert(small[:, 16:20], 2, P), ALU.mult), s_p)
                st.did(V.tensor_tensor(lg1, lg1, insert(small[:, 20:24], 2, 256), ALU.mult), s_p)
                for r in range(4):
                    dve.wait_ge(s_exp, 5 * l + 2 + r)
                    st.did(V.reciprocal(small[:, 24 + r:25 + r], small[:, 24 + r:25 + r]))
                    st.settle()
                    st.did(V.tensor_scalar(lgS[:, r, :], lgS[:, r, :], small[:, 24 + r:25 + r], None, ALU.mult), s_p)
                wait_emptied(dve, "qkB", l, 2)
                wait_emptied(dve, "oS", l)
                st.did(V.memset(q0, 0.0))
                st.settle()
                for h in range(BH):
                    lo = 64 * (h % 2)
                    for n2 in range(2):
                        src = steps(qkB[lo:lo + 64, h // 2, SEQ + TS * n2:SEQ + TS * n2 + 1], [[32, 4], [1, TS]])
                        dst = steps(q0[64 * n2:64 * n2 + 64, h, TS * n2:TS * n2 + 1], [[160, 4], [1, TS]])
                        ins = V.tensor_tensor(dst, src, insert(qdec[lo:lo + 64, h, :], 1, 4), ALU.mult)
                        if n2:
                            st.did(ins, s_q0)
                        else:
                            st.did(ins)
                for h in range(BH):
                    wait_filled(dve, "aB", l, h)
                    b = bank[BANK[("aB", l, h)][0]]
                    st.did(V.tensor_tensor(attT[:, h, 0:256], b[:, 0:256], decay[:, h, :], ALU.mult))
                    st.emptied(V.tensor_tensor(attT[:, h, 256:384], b[:, 256:384], decay[:, h, 0:P], ALU.mult),
                               "aB", l, h)
                for odd in range(2):
                    wait_filled(dve, "aS", l, odd)
                    st.emptied(V.tensor_tensor(attS[:, odd::2, :], bank[BANK[("aS", l, odd)][0]][:, 0:256].rearrange(
                        "p (h k) -> p h k", h=2), decay_s[:, odd::2, :], ALU.mult), "aS", l, odd)
                for t in range(NT):
                    wait_filled(dve, "oB", l, t)
                    b = bank[BANK[("oB", l, t)][0]]
                    for h in range(BH):
                        st.did(V.bn_stats(bnst[:, 6 * h:6 * h + 6], b[:, h * P:(h + 1) * P]))
                    st.settle()
                    for h in range(BH):
                        st.did(V.bn_aggr(bnag[:, t, 2 * h:2 * h + 2], bnst[:, 6 * h:6 * h + 6]),
                               s_gnv if h == 3 else None)
                    dve.wait_ge(s_gnr, NT * l + t + 1)
                    for h in range(BH):
                        st.did(V.tensor_scalar(gnt[:, h * P:(h + 1) * P], b[:, h * P:(h + 1) * P],
                                               bnag[:, t, 2 * h:2 * h + 1], rstd8[:, t, h:h + 1],
                                               ALU.subtract, ALU.mult), emptied["v"] if h == 3 else None)
                    assert st.last[1] == DRAIN[("oB", l, t)][1]
                    dve.wait_ge(s_gs, NT * l + t + 1)
                    st.settle()
                    st.did(V.tensor_tensor(proj[:, t, GB:GB + 512], gnt, proj[:, t, GB:GB + 512], ALU.mult), s_ob)
                for h in range(BH):
                    wait_filled(dve, "nsS", l, h)
                    st.emptied(V.scalar_tensor_tensor(
                        s0[:, :, h, :], s0[:, :, h, :], GAMMA[h] ** TS,
                        bank[BANK[("nsS", l, h)][0]][:, :].rearrange("p (j v) -> p j v", j=4),
                        ALU.mult, ALU.add), "nsS", l, h)
                dve.wait_ge(s_outp, 48 * (l + 1))
                for t in range(NT):
                    wait_filled(dve, "yc", l, t)
                    b = bank[BANK[("yc", l, t)][0]]
                    st.did(V.bn_stats(bnst[:, 0:6], b[:, 0:CC]))
                    st.settle()
                    st.did(V.bn_aggr(lnag[:, 2 * t:2 * t + 2], bnst[:, 0:6]), s_lnv)
                    dve.wait_ge(s_cln, NT * l + t + 1)
                    st.emptied(V.tensor_scalar(proj[:, t, CA:CA + CC], b[:, 0:CC], lnag[:, 2 * t:2 * t + 1],
                                               lnr[:, t:t + 1], ALU.subtract, ALU.mult), "yc", l, t)
                st.settle()
                dve.wait_ge(s_bc, 48 * (l + 1))
                st.did(V.tensor_tensor(proj[:, :, CA:CA + CC], proj[:, :, CA:CA + CC], insert(bc_cg[:, :], 1, NT),
                                       ALU.mult), s_lnr)
                st.settle()
                st.did(V.tensor_tensor(proj[:, :, CA:CA + CC], proj[:, :, CA:CA + CC], insert(bc_cb[:, :], 1, NT),
                                       ALU.add), s_lnr)
                add_x("out", l)
                norm_T(3 * l + 1)
                st.did(V.memset(qxb, 0.0), s_zero)
                for j in range(4):
                    wait_filled(dve, "xs", l, j)
                    b = bank[BANK[("xs", l, j)][0]]
                    cs = small[:, 32 + 2 * j:34 + 2 * j]
                    st.did(V.tensor_reduce(cs, b[:, :].rearrange("p (h k) -> p h k", h=2), AX.X, ALU.max, negate=True))
                    st.settle()
                    st.did(V.tensor_scalar(cs, cs, XD ** -0.5, None, ALU.mult), s_xmax)
                for t in range(2):
                    wait_emptied(dve, "xs", l, 2 * t + 1)
                    ss = small[:, 40 + 4 * t:44 + 4 * t]
                    st.did(V.reciprocal(ss, ss))
                    st.settle()
                    st.did(V.tensor_tensor(px[:, t, :, :], px[:, t, :, :], insert(ss, 2, NMEM), ALU.mult), s_xp)
                for r in range(4):
                    for n2 in range(2):
                        for j in (1, 3):
                            wait_filled(dve, "kTs", l, 2 * r + n2, j)
                            st.emptied(V.tensor_copy(
                                kTs[:, n2, 2 * j:2 * j + 2, :],
                                bank[BANK[("kTs", l, 2 * r + n2, j)][0]][:, :].rearrange("p (k n) -> p k n", k=2)),
                                "kTs", l, 2 * r + n2, j)
                    wait_filled(dve, "xss", l, r)
                    b = bank[BANK[("xss", l, r)][0]]
                    cs = small[:, 48 + r:49 + r]
                    st.did(V.tensor_reduce(cs, b[:, 0:NMEM], AX.X, ALU.max, negate=True))
                    st.settle()
                    st.did(V.tensor_scalar(cs, cs, XD ** -0.5, None, ALU.mult), s_xmax)
                    wait_emptied(dve, "xss", l, r)
                    ss = small[:, 52 + r:53 + r]
                    st.did(V.reciprocal(ss, ss))
                    st.settle()
                    st.did(V.tensor_scalar(pxs[:, r % 2, :], pxs[:, r % 2, :], ss, None, ALU.mult), s_xp)
                add_x("o", l)
                norm_T(3 * l + 2)
                if l % 2:
                    route(dve, st)
                for e in range(NE if l % 2 else 2):
                    for c, (c0, w) in enumerate(FF_CHUNKS):
                        for t in range(NT):
                            if c >= 2:
                                wait_filled(dve, "aT", l, e, c - 2, t)
                            wait_filled(dve, "up", l, e, c, t)
                            wait_emptied(dve, "gate", l, e, c, t)
                            sc = comb[:, t, e:e + 1] if l % 2 else 1.0
                            st.emptied(V.scalar_tensor_tensor(acts[:, NT * (c % 2) + t, 0:w], bank[3 + t][:, 0:w], sc,
                                                              gated[:, t, 0:w], ALU.mult, ALU.mult),
                                       "up", l, e, c, t)
                    add_x("down", l, e)
            n = 3 * DEPTH
            norm_rows(n)
            dve.wait_ge(s_fg, 16)
            st.settle()
            for t in range(NT):
                st.did(V.tensor_tensor(htok[:, t, :], htok[:, t, :], fgain, ALU.mult), s_y)

        @block.gpsimd
        def _(pool):
            st = Steps(pool, "g")
            G = nc.gpsimd

            def rstd(n):
                pool.wait_ge(s_sq, NT * (n + 1))
                st.did(G.tensor_scalar(stat[:, 0:3], stat[:, 0:3], 1.0 / D, EPS, ALU.mult, ALU.add))
                st.settle()
                st.did(G.tensor_tensor(stat[:, 4:7], stat[:, 0:3], minus_half[:, 0:3], ALU.pow), s_rstd)

            pool.dma_start(cst[:, :], a["constants"]).then_inc(s_const, 16)
            for i, name in enumerate(("norm_mix_g", "norm_mem_g", "norm_ffn_g")):
                pool.dma_start(grow[16 * i:16 * i + 16, :], a[name].rearrange("l (k p) -> (l k) p", p=P)).then_inc(s_gain, 16)
            pool.dma_start(relx[0:8, RPAD:RLEN], a["rel_bias_reversed"].rearrange("l h r -> (l h) r")).then_inc(s_relr, 16)
            pool.dma_start(rw, a["router_w"][0].rearrange("(k p) e -> p k e", p=P)).then_inc(s_rw, 16)
            pool.wait_ge(s_relx, 1)
            pool.dma_start(scratch[0], relx[0:8, :]).then_inc(s_relv, 16)
            pool.wait_ge(s_relv, 16)
            pool.dma_start(scratch[1], rows(scratch[0], 0, [[0, P], [1, DEPTH * AH * RLEN]])).then_inc(s_relv, 16)
            for e in range(NE):
                ins = G.memset(eight[:, e:e + 1], float(NE - e))
            st.did(ins)
            pool.wait_ge(s_const, 16)

            def load(l):
                pool.dma_start(cwr[0:31, :], a["conv_w"][l]).then_inc(s_cw, 16)
                pool.dma_start(cwr[31:32, :], a["conv_b"][l:l + 1]).then_inc(s_cw, 16)
                pool.dma_start(cbufr[0:120, :, :],
                               a["state_conv"][l].rearrange("(g n) w c -> (n w) g c", g=2)).then_inc(s_cbuf, 16)
                if l == 0:
                    pool.wait_ge(s_relv, 32)
                pool.dma_start(rel_p, rows(scratch[1], l * AH * RLEN + RPAD, [[DEPTH * AH * RLEN - 1, P], [RLEN, AH], [1, 256]])).then_inc(s_rel, 16)
                for n2 in range(2):
                    for h in range(AH):
                        r0 = 64 * n2 + TS * h
                        pool.dma_start(rel_s[r0:r0 + TS, :],
                                       rows(scratch[1], (l * AH + h) * RLEN + TS - 1,
                                            [[DEPTH * AH * RLEN - 1, TS], [1, PAST + TS]])).then_inc(s_rel, 16)
                for dst, name, w in ((bc_gn, "ret_gn_g", BH * BV), (bc_cg, "conv_ln_g", CC), (bc_cb, "conv_ln_b", CC)):
                    pool.dma_start(dst[:, :], rows(a[name], l * w, [[0, P], [1, w]])).then_inc(s_bc, 16)
                for n2 in range(2):
                    src = a["state_ret"][l].rearrange("(j s) h k v -> s k j h v", s=2)[n2]
                    for j in range(4):
                        pool.dma_start(s0[64 * n2:64 * n2 + 64, j], src[:, j]).then_inc(s_s0, 16)

            for l in range(DEPTH):
                if l == 0:
                    pool.wait_ge(s_mem, 16)
                    wait_emptied(pool, "memT", 3)
                    wait_emptied(pool, "gains")
                load(l)
                if l == 0:
                    rstd(0)
                pool.wait_ge(s_u, l + 1)
                pool.dma_start(o["new_conv_prompt"][l, 0], proj[98:128, 1, CA:CA + CC]).then_inc(s_outp, 16)
                pool.dma_start(o["new_conv_sample"][l, :, 0:14, :], a["state_conv"][l, :, 16:30, :]).then_inc(s_outp, 16)
                pool.dma_start(o["new_conv_sample"][l, :, 14:30, :], proj[:, 2, CA:CA + CC]).then_inc(s_outp, 16)
                for c in range(2, 4):
                    wait_emptied(pool, "in", l, c, 2)
                for t in range(NT):
                    def part(i):
                        return proj[:, t, QB:QB + 512].rearrange("p (b h s w) -> p b h s w", b=2, h=4, s=2)[:, :, :, i, :]

                    def to(i):
                        return part(i)
                    for b_ in range(2):
                        co, si = insert(cos_t[:, t, b_, :], 1, 4), insert(sin_t[:, t, b_, :], 1, 4)
                        tm = [rtmp[:, 128 * i:128 * i + 128].rearrange("p (h w) -> p h w", h=4) for i in range(4)]
                        x1, x2 = part(0)[:, b_], part(1)[:, b_]
                        st.did(G.tensor_tensor(tm[0], x1, co, ALU.mult))
                        st.did(G.tensor_tensor(tm[1], x2, si, ALU.mult))
                        st.did(G.tensor_tensor(tm[2], x2, co, ALU.mult))
                        st.did(G.tensor_tensor(tm[3], x1, si, ALU.mult))
                        st.settle()
                        st.did(G.tensor_tensor(to(0)[:, b_], tm[0], tm[1], ALU.subtract))
                        st.did(G.tensor_tensor(to(1)[:, b_], tm[2], tm[3], ALU.add), s_rot if b_ else None)
                        st.settle()
                for t in range(2):
                    ins = G.tensor_tensor(kd[:, t, :].rearrange("p (h d) -> p h d", h=BH),
                                          proj[:, t, KB:KB + 256].rearrange("p (h d) -> p h d", h=BH),
                                          insert(kdec[:, t, :], 2, BK), ALU.mult)
                    st.did(ins, s_kd if t else None)
                st.did(G.memset(qblk, 0.0))
                wait_emptied(pool, "qkA", l, 2)
                st.settle()
                for i in range(2):
                    for k in range(2):
                        ins = G.tensor_copy(qblk[64 * i:64 * i + 64, k, :, TS * i:TS * i + TS],
                                            qkA[64 * i:64 * i + 64, k, SEQ:TOK].rearrange("p (n w) -> p n w", n=NS))
                        st.did(ins, s_blk if (i, k) == (1, 1) else None)
                wait_emptied(pool, "oS", l)
                for h in range(BH):
                    ins = G.tensor_tensor(ks[:, h, :, :], insert(proj[:, 2, KB + 64 * h:KB + 64 * h + 64], 1, NS),
                                          insert(kmask[:, h, :], 2, BK), ALU.mult)
                    st.did(ins, s_kd if h == 3 else None)
                pool.wait_ge(s_bc, 48 * (l + 1))
                for t in range(NT):
                    pool.wait_ge(s_silu, NT * l + t + 1)
                    st.did(G.tensor_tensor(proj[:, t, GB:GB + 512], proj[:, t, GB:GB + 512], bc_gn[:, :], ALU.mult), s_gs)
                for t in range(NT):
                    pool.wait_ge(s_gnv, NT * l + t + 1)
                    var = bnag[:, t, :].rearrange("p (h s) -> p h s", s=2)[:, :, 1]
                    st.did(G.tensor_scalar(rstd8[:, t, :], var, EPS, None, ALU.add))
                    st.settle()
                    st.did(G.tensor_tensor(rstd8[:, t, :], rstd8[:, t, :], minus_half, ALU.pow), s_gnr)
                for t in range(NT):
                    pool.wait_ge(s_lnv, NT * l + t + 1)
                    st.did(G.tensor_scalar(lnr[:, t:t + 1], lnag[:, 2 * t + 1:2 * t + 2], EPS, None, ALU.add))
                    st.settle()
                    st.did(G.tensor_tensor(lnr[:, t:t + 1], lnr[:, t:t + 1], minus_half[:, 0:1], ALU.pow), s_cln)
                for k in range(1, 4):
                    rstd(3 * l + k)
                    if l == DEPTH - 1 and k == 3:
                        pass
                if l == 0:
                    pool.wait_ge(s_st, 16 * 8)
            wait_emptied(pool, "xos", DEPTH - 1)
            pool.dma_start(fgain, rows(a["final_norm_g"], 0, [[0, P], [1, D]])).then_inc(s_fg, 16)
            pool.wait_ge(s_outp, 16 * 3 * DEPTH)


_INS = ["x_prompt", "x_sample", "cache_attn_k", "cache_attn_v", "state_ret", "state_conv", "cache_mem_k",
        "cache_mem_v", "mem_prompt", "norm_mix_g", "w_in", "ret_gn_g", "conv_w", "conv_b", "conv_ln_g",
        "conv_ln_b", "w_out", "norm_mem_g", "wx_q", "wx_k", "wx_v", "wx_o", "norm_ffn_g", "ffn_w_gate",
        "ffn_w_up", "ffn_w_down", "router_w", "moe_w_gate", "moe_w_up", "moe_w_down", "final_norm_g"]
_OUTS = [("y_prompt", (1, SEQ, D)), ("y_sample", (NS, TS, D)),
         ("new_attn_k_prompt", (DEPTH, 1, SEQ, AH, AD)), ("new_attn_v_prompt", (DEPTH, 1, SEQ, AH, AD)),
         ("new_ret_prompt", (DEPTH, 1, BH, BK, BV)), ("new_conv_prompt", (DEPTH, 1, CW - 1, CC)),
         ("new_mem_k_prompt", (DEPTH, 1, NMEM, XH, XD)), ("new_mem_v_prompt", (DEPTH, 1, NMEM, XH, XD)),
         ("new_attn_k_sample", (DEPTH, NS, TS, AH, AD)), ("new_attn_v_sample", (DEPTH, NS, TS, AH, AD)),
         ("new_ret_sample", (DEPTH, NS, BH, BK, BV)), ("new_conv_sample", (DEPTH, NS, CW - 1, CC))]


def kernel(**inputs):
    import concourse.bacc as _bacc
    from concourse.bass_utils import run_bass_kernel_spmd as _run

    nc = _bacc.Bacc("TRN2", target_bir_lowering=False, num_devices=1)
    arrays, a = {}, {}

    def give(name, array):
        array = np.ascontiguousarray(array)
        arrays[f"in_{name}"] = array
        a[name] = nc.dram_tensor(f"in_{name}", array.shape, mybir.dt.from_np(array.dtype), kind="ExternalInput").ap()

    for name in _INS:
        give(name, np.asarray(inputs[name]))
    give("rel_bias_reversed", np.asarray(inputs["rel_bias"])[:, :, ::-1])
    give("constants", constants())
    o = {name: nc.dram_tensor(f"out_{name}", shape, F32, kind="ExternalOutput").ap() for name, shape in _OUTS}
    scratch = (nc.dram_tensor("bias_vectors", (DEPTH * AH, RLEN), F32, kind="Internal").ap(),
               nc.dram_tensor("bias_vectors_by_row", (P, DEPTH * AH * RLEN), F32, kind="Internal").ap())
    hybrid_encoder(nc, a, o, scratch)
    r = _run(nc, [arrays], core_ids=[0])
    return tuple(r.results[0][f"out_{name}"] for name, _ in _OUTS)
```

```python
from contextlib import ExitStack

import numpy as np

import concourse.bass as bass
from concourse import mybir

F32 = mybir.dt.float32
ALU = mybir.AluOpType
ACT = mybir.ActivationFunctionType
AX = mybir.AxisListType

P = 128
DEPTH = 2
D = 1024
SEQ = 256
NS = 8
TS = 16
PAST = 256
NT = 3
TOK = NT * P
KC = D // P
CHUNK = 64
NMEM = 256
EPS = 1e-6
NEG = -1e30
AH, AD = 4, 64
BH, BK, BV = 4, 64, 128
CC = 256
CW = 31
REL = 128
DIN = 2816
QA, KA, VA, QB, KB, VB, GB, CA, CB = 0, 256, 512, 768, 1024, 1280, 1792, 2304, 2560
XH, XD = 4, 256
FF = 1408
FFK = FF // P
NE = 8
RLEN = 400
RPAD = 143
R = 4
EXTRA = 5
UNITS = NE + EXTRA
RF = 6
SLAB = 2048
GAMMA = [1.0 - 2.0 ** (-(5.0 + h)) for h in range(BH)]
IN_CHUNKS = [(2304, 512), (0, 512), (512, 512), (1024, 512), (1536, 512), (2048, 256)]
FF_CHUNKS = [(0, 512), (512, 512), (1024, 384)]
FF_GROUPS = [(0, 4), (4, 4), (8, 3)]

CONST = {}
_at = 0
for _name, _width in (("ident", P), ("cos", NT * 2 * 32), ("sin", NT * 2 * 32), ("decay", BH * 256),
                      ("decay_s", BH * P), ("qdec", BH * TS), ("kdec", 2 * BH), ("kmask", BH * NS),
                      ("smask", 4 * P), ("cmask", P), ("minus_half", 4),
                      ("before", P), ("ones", P), ("slots", P)):
    CONST[_name] = (_at, _width)
    _at += _width
NCONST = _at


def constants():
    c = np.zeros((P, NCONST), np.float32)

    def put(name, a):
        o, w = CONST[name]
        c[:, o:o + w] = np.asarray(a, np.float64).reshape(P, w)

    p = np.arange(P)
    put("ident", np.eye(P))
    inv = (np.float32(10000.0) ** (-np.arange(32, dtype=np.float32) / np.float32(32))).astype(np.float32)
    pos = np.stack([p, P + p, PAST + p % TS], 1).astype(np.float32)
    ang = (pos[:, :, None] * inv[None, None, :]).astype(np.float32)
    scale = np.array([1.0, BK ** -0.5], np.float32)[None, None, :, None]
    put("cos", np.cos(ang)[:, :, None, :] * scale)
    put("sin", np.sin(ang)[:, :, None, :] * scale)
    lg = np.log(np.array(GAMMA, np.float64))
    dif = np.arange(256)[None, :] - p[:, None]
    put("decay", np.where(dif[:, None] >= 0, np.exp(np.maximum(dif, 0)[:, None] * lg[None, :, None]), 0.0))
    ds = (p % TS)[None, :] - (p % TS)[:, None]
    same = (p // TS)[None, :] == (p // TS)[:, None]
    put("decay_s", np.where((same & (ds >= 0))[:, None], np.exp(np.maximum(ds, 0)[:, None] * lg[None, :, None]), 0.0))
    put("qdec", np.broadcast_to(np.exp((np.arange(TS) + 1.0)[None, :] * lg[:, None])[None], (P, BH, TS)))
    kd = 255.0 - (np.arange(2)[None, :] * P + p[:, None])
    put("kdec", np.exp(kd[:, :, None] * lg[None, None, :]))
    km = np.exp((TS - 1.0 - p % TS)[:, None] * lg[None, :])
    put("kmask", km[:, :, None] * ((p // TS)[:, None, None] == np.arange(NS)[None, None, :]))
    own = (2 * np.arange(4)[None, :] + p[:, None] // 64)
    put("smask", np.where(own[:, :, None] == (p // TS)[None, None, :], 0.0, NEG))
    put("cmask", np.where((p[:, None] < CHUNK) & (p[None, :] >= CHUNK), NEG, 0.0))
    put("minus_half", np.full((P, 4), -0.5))
    put("before", p[:, None] < p[None, :])
    put("ones", np.ones((P, P)))
    put("slots", np.broadcast_to(p[None, :], (P, P)))
    return c


def insert(ap, axis, n):
    dims = [list(d) for d in ap.ap]
    return bass.AP(tensor=ap.tensor, offset=ap.offset, ap=dims[:axis] + [[0, n]] + dims[axis:])


def steps(ap, dims):
    return bass.AP(tensor=ap.tensor, offset=ap.offset, ap=[list(ap.ap[0])] + dims)


def rows(tensor_ap, offset, dims):
    return bass.AP(tensor=tensor_ap.tensor, offset=offset, ap=dims)


T = (6, 7)


def psum_jobs():
    jobs = []
    small = [0]
    big = [0]

    def one(key, who):
        jobs.append((key, (T[small[0] % 2],), who))
        small[0] += 1

    def product(name, chunks, tiles, who):
        for c in range(chunks):
            for t in range(tiles):
                jobs.append((name + (c, t), (3 * (big[0] % 2) + t,), who))
            big[0] += 1

    def norm(n):
        for t in range(NT):
            for half in range(2):
                one(("hT", n, t, half), "v")

    one(("gains",), "a")
    for j in range(4):
        one(("memT", j), "a")
    for l in range(DEPTH):
        norm(3 * l)
        one(("cw", l), "a")
        one(("cbuf", l), "a")
        product(("in", l), 2, NT, "a")
        for b in range(2):
            one(("uT", l, b), "a")
        for c in range(2, len(IN_CHUNKS)):
            for t in range(NT):
                jobs.append((("in", l, c, t), (3 * (big[0] % 2) + t,), "a"))
            big[0] += 1
        product(("mk", l), 2, 2, "a")
        product(("mv", l), 2, 2, "a")
        for j in range(4):
            one(("mkT", l, j), "a")
        for t in range(NT):
            one(("qkA", l, t), "a")
        for t in range(NT):
            one(("qkB", l, t), "a")
        for j in range(4):
            one(("sA", l, j), "v")
        for n in range(NS):
            one(("ktA", l, n), "a")
            if n % 2:
                one(("sS", l, n // 2), "v")
        for h in range(AH):
            one(("pTA", l, h), "a")
        one(("oA", l), "a")
        for r in range(4):
            one(("pTS", l, r), "a")
        one(("oS", l), "a")
        for h in range(BH):
            one(("aB", l, h), "v")
        for j in range(2):
            one(("aS", l, j), "v")
        for t in range(NT):
            one(("oB", l, t), "v")
        one(("nsP", l), "a")
        for h in range(BH):
            one(("nsS", l, h), "v")
        for t in range(NT):
            one(("yc", l, t), "v")
        for b in range(BH):
            one(("obT", l, b), "a")
        for b in range(2):
            one(("ocT", l, b), "a")
        product(("out", l), 2, NT, "v")
        norm(3 * l + 1)
        product(("q", l), 2, NT, "a")
        for j in range(4):
            one(("qTx", l, j), "a")
        for j in range(2):
            one(("qTs", l, j), "a")
        for j in range(4):
            one(("xs", l, j), "a")
        for h in range(XH):
            one(("xpT", l, h), "a")
        for h in range(XH):
            one(("xo", l, h), "a")
        for r in range(5):
            if r < 4:
                for n2 in range(2):
                    for j in range(4):
                        one(("kTs", l, 2 * r + n2, j), "v" if j % 2 else "a")
                one(("xss", l, r), "a")
            if r >= 1:
                one(("xpTs", l, r - 1), "a")
        jobs.append((("xos", l), (0, 1), "a"))
        product(("o", l), 2, NT, "v")
        norm(3 * l + 2)
        if l % 2:
            one(("route", l), "v")
            one(("pos", l), "v")
        big[0] = 0
    return jobs


def slabs():
    out = []

    def product(name, key, l, cols, tiles):
        for c, (c0, w) in enumerate(cols):
            for half in range(2):
                out.append((name, "rows", (l, 4 * half, 4, c0, w), key + (c, 0 if half == 0 else tiles - 1)))

    full = [(0, 512), (512, 512)]
    for l in range(DEPTH):
        product("w_in", ("in", l), l, IN_CHUNKS, NT)
        product("wx_k", ("mk", l), l, full, 2)
        product("wx_v", ("mv", l), l, full, 2)
        for g in range(2):
            out.append(("cache_attn_k", "past", (l, g), ("ktA", l, 4 * g + 3)))
        for g in range(2):
            out.append(("cache_attn_v", "past", (l, g), ("oS", l)))
        product("w_out", ("out", l), l, full, NT)
        product("wx_q", ("q", l), l, full, NT)
        for r in range(5):
            if r < 4:
                for n in (2 * r, 2 * r + 1):
                    out.append(("cache_mem_k", "mem", (l, n), ("kTs", l, n, 3)))
            if r >= 1:
                for n in (2 * r - 2, 2 * r - 1):
                    out.append(("cache_mem_v", "mem", (l, n), ("xpTs", l, r) if r < 4 else ("xos", l)))
        product("wx_o", ("o", l), l, full, NT)
    return out


def dense_jobs():
    jobs, small = [], 0
    for c in range(4):
        if c < 3:
            for kind in ("gate", "up"):
                jobs += [((kind, c, t), (3 * (kind == "up") + t,), "a" if kind == "gate" else "v") for t in range(NT)]
        if c:
            for t in range(NT):
                jobs.append((("aT", c - 1, t), (T[small % 2],), "a"))
                small += 1
    jobs += [(("down", c, t), (3 * c + t,), "v") for c in range(2) for t in range(NT)]
    return jobs


def dense_slabs():
    out = []
    for c, (c0, w) in enumerate(FF_CHUNKS):
        for kind in ("gate", "up"):
            for half in range(2):
                out.append((kind, 4 * half, 4, c0, w, (kind, c, 0 if half == 0 else NT - 1)))
    for c in range(2):
        for g, (k0, nk) in enumerate(FF_GROUPS):
            out.append(("down", k0, nk, 512 * c, 512, ("down", c, 0 if g < 2 else NT - 1)))
    return out


def routed_jobs():
    jobs = [(("gather", 0), (6,), "v"), (("gather", 1), (7,), "v"), (("ST",), (6,), "a")]
    for c in range(3):
        for kind in ("gate", "up"):
            jobs += [((kind, c, "first"), (), None), ((kind, c), (2 * (kind == "up") + c % 2,), "a" if kind == "gate" else "v")]
        if c:
            jobs.append((("aT", c - 1), (T[c % 2],), "a"))
    jobs += [(("down", 0, 0), (), None), (("down", 0, 1), (), None), (("aT", 2), (T[1],), "a"), (("down", 0), (4,), "a"),
             (("down", 1, 0), (), None), (("down", 1, 1), (), None), (("down", 1), (5,), "a")]
    jobs += [(("scatter", c, t), ((0, 1, 2, 3, 6, 7)[3 * c + t],), "v") for c in range(2) for t in range(NT)]
    return jobs


def routed_slabs():
    out = []
    for c, (c0, w) in enumerate(FF_CHUNKS):
        for kind in ("gate", "up"):
            out.append((kind, 0, 4, c0, w, (kind, c, "first")))
            out.append((kind, 4, 4, c0, w, (kind, c)))
    for c in range(2):
        for g, (k0, nk) in enumerate(FF_GROUPS):
            out.append(("down", k0, nk, 512 * c, 512, ("down", c, g) if g < 2 else ("down", c)))
    return out


def hybrid_encoder(nc, a, o, scratch):
    JOBS = psum_jobs()
    INDEX = {key: i for i, (key, _, _) in enumerate(JOBS)}
    DRAIN, PREV, _last, _n = {}, {}, {}, {"a": 0, "v": 0}
    for key, banks, who in JOBS:
        _n[who] += 1
        DRAIN[key] = (who, _n[who])
        PREV[key] = [_last[b] for b in banks if b in _last]
        for b in banks:
            _last[b] = key
    BANK = {key: banks for key, banks, _ in JOBS}
    SLABS = slabs()

    with ExitStack() as ctx:
        def sem(name):
            return ctx.enter_context(nc.semaphore(name))

        total = [0]

        def sb(name, width):
            total[0] += width
            return ctx.enter_context(nc.sbuf_tensor(name, [P, width], F32))

        bank = [ctx.enter_context(nc.psum_tensor(f"bank{i}", [P, 512], F32)) for i in range(8)]

        x = sb("x", NT * D)[:, :].rearrange("p (t d) -> p t d", t=NT)
        fT_ = sb("features_T", KC * TOK)
        hT = fT_[:, :].rearrange("p (k n) -> p k n", k=KC)
        oT = hT
        ring = sb("ring", R * SLAB)
        memT = sb("memT", KC * NMEM)[:, :].rearrange("p (k n) -> p k n", k=KC)
        mv = sb("mv", 2 * D)[:, :].rearrange("p (t d) -> p t d", t=2)
        mkT = sb("mkT", KC * NMEM)[:, :].rearrange("p (k n) -> p k n", k=KC)
        cst = sb("consts", NCONST)
        gT = sb("gT", 48)
        stat = sb("stat", 64)
        rel_p = sb("rel_p", AH * 256)[:, :].rearrange("p (h k) -> p h k", h=AH)
        rel_s = sb("rel_s", PAST + TS)
        rel_n = sb("rel_n", 4 * P)[:, :].rearrange("p (r k) -> p r k", r=4)
        bc_gn = sb("bc_gn", BH * BV)
        bc_cg = sb("bc_cg", CC)
        bc_cb = sb("bc_cb", CC)
        comb = sb("comb", NT * NE)[:, :].rearrange("p (t e) -> p t e", t=NT)
        rw = sb("rw", KC * NE)[:, :].rearrange("p (k e) -> p k e", k=KC)
        rt = sb("rt", 8 * NT * NE)
        small = sb("small", 128)
        mask = sb("chosen", NT * NE)[:, :].rearrange("p (t e) -> p t e", t=NT)
        posm = sb("slot_of", NT * NE)[:, :].rearrange("p (t e) -> p t e", t=NT)
        table = sb("table", UNITS * 2 * NT)[:, :].rearrange("p (e j) -> p e j", e=UNITS)
        cur = sb("current", 2 * NT)[:, :]
        more = sb("more", 2 * NE * (3 + EXTRA + 7) + EXTRA * 7)
        full = sb("counts", 16)[:, :]
        expert = ctx.enter_context(nc.sbuf_tensor("expert_of_unit", [P, UNITS + 1], mybir.dt.int32))

        arena_w = (nc.sbuf_bytes_remaining() if callable(nc.sbuf_bytes_remaining) else nc.sbuf_bytes_remaining) // 4 - 128
        arena = ctx.enter_context(nc.sbuf_tensor("arena", [P, arena_w], F32))

        class Plan:
            def __init__(self):
                self.at = 0

            def take(self, w):
                self.at += w
                assert self.at <= arena_w, (self.at, arena_w)
                return arena[:, self.at - w:self.at]

        def cut(ap, **k):
            names = list(k)
            s = "p (" + " ".join(names) + " w) -> p " + " ".join(names) + " w"
            return ap.rearrange(s, **k)

        m = Plan()
        proj = cut(m.take(NT * DIN), t=NT)
        qkA = cut(m.take(4 * TOK), b=4)
        qblk = m.take(2 * NS * 32).rearrange("p (b n c) -> p b n c", b=2, n=NS)
        qkB = cut(m.take(4 * TOK), b=4)
        at0 = m.at
        mk = arena[:, at0:at0 + 2 * D].rearrange("p (t d) -> p t d", t=2)
        lg0 = cut(m.take(AH * P), h=AH)
        lg1 = cut(m.take(AH * 256), h=AH)
        lgS = cut(m.take(4 * TOK), r=4)
        pTA = cut(m.take(AH * TOK), h=AH)
        pTS = m.take(4 * TOK).rearrange("p (r k n) -> p r k n", r=4, k=3)
        end_a = m.at
        m.at = at0
        attT = cut(m.take(BH * TOK), h=BH)
        attS = cut(m.take(BH * P), h=BH)
        q0 = cut(m.take(BH * 512), h=BH)
        ks = m.take(BH * 512).rearrange("p (h n d) -> p h n d", h=BH, n=NS)
        end_b = m.at
        m.at = max(end_a, end_b)
        ktA = m.take(4 * 512).rearrange("p (n b k) -> p n b k", n=4, b=2)
        s0 = m.take(16 * BV).rearrange("p (j h v) -> p j h v", j=4, h=BH)
        kd = cut(m.take(2 * 256), t=2)
        spr = ktA.rearrange("p n b k -> p (n b k)")[:, 0:BH * BV]
        cw = cut(m.take(2 * 32), b=2)
        up = cut(m.take(2 * (SEQ + 30)), b=2)
        us = m.take(2 * NS * 46).rearrange("p (b n w) -> p b n w", b=2, n=NS)
        conv_ = m.take(2 * TOK)
        conv = cut(conv_, b=2)
        cwr = conv_[:, 0:CC]
        cbufr = cut(conv_[:, CC:3 * CC], g=2)
        sig = proj[:, :, CB:CB + CC]
        rtmp = m.take(2 * 256)

        n_ = Plan()
        htok = cut(n_.take(NT * D), t=NT)
        qx = cut(n_.take(NT * D), t=NT)
        qxT = cut(n_.take(KC * SEQ), k=KC)
        qxb = n_.take(KC * NS * 32).rearrange("p (k n c) -> p k n c", k=KC, n=NS)
        px = n_.take(2 * XH * NMEM).rearrange("p (t h m) -> p t h m", t=2, h=XH)
        pxT = n_.take(XH * 2 * SEQ).rearrange("p (h m n) -> p h m n", h=XH, m=2)
        kTs = n_.take(2 * KC * NMEM).rearrange("p (s k m) -> p s k m", s=2, k=KC)
        pxs = cut(n_.take(2 * NMEM), s=2)
        pxsT = n_.take(2 * 2 * P).rearrange("p (s m n) -> p s m n", s=2, m=2)

        f = Plan()
        f.take(NT * D)
        gated = cut(f.take(NT * 512), t=NT)
        acts = cut(f.take(2 * NT * 512), s=2 * NT)
        actT = cut(f.take(FFK * TOK), k=FFK)

        memtok = cut(arena[:, at0:at0 + 2 * D], t=2)
        grow = arena[:, at0 + 2 * D:at0 + 2 * D + P]
        relx = arena[:, at0 + 2 * D + P:at0 + 2 * D + P + RLEN]
        slot4 = f.take((RF - R) * SLAB)
        end_dense = f.at
        f.at = NT * D
        hTe = cut(f.take(KC * P), k=KC)
        S = cut(f.take(NT * P), t=NT)
        ST = cut(f.take(NT * P), t=NT)
        gated_e = cut(f.take(2 * 512), s=2)
        acts_e = cut(f.take(2 * 512), s=2)
        actT_e = cut(f.take(FFK * P), k=FFK)
        Y = f.take(D)
        assert f.at <= end_dense - (RF - R) * SLAB
        fgain = arena[:, end_dense:end_dense + D]
        gnt = rtmp
        bnst = sb("bnst", 24)
        bnag = sb("bnag", NT * 8)[:, :].rearrange("p (t j) -> p t j", t=NT)
        rstd8 = sb("rstd8", NT * 4)[:, :].rearrange("p (t j) -> p t j", t=NT)
        lnag = sb("lnag", 8)
        lnr = sb("lnr", 4)
        eight = sb("eight", NE)[:, :]

        def rtv(i):
            return cut(rt[:, i * NT * NE:(i + 1) * NT * NE], t=NT)

        def const(name):
            off, w = CONST[name]
            return cst[:, off:off + w]

        ident = const("ident")
        cos_t = const("cos").rearrange("p (t b w) -> p t b w", t=NT, b=2)
        sin_t = const("sin").rearrange("p (t b w) -> p t b w", t=NT, b=2)
        decay = const("decay").rearrange("p (h i) -> p h i", h=BH)
        decay_s = const("decay_s").rearrange("p (h i) -> p h i", h=BH)
        qdec = const("qdec").rearrange("p (h i) -> p h i", h=BH)
        kdec = const("kdec").rearrange("p (t h) -> p t h", t=2)
        kmask = const("kmask").rearrange("p (h n) -> p h n", h=BH)
        smask = const("smask").rearrange("p (r k) -> p r k", r=4)
        cmask = const("cmask")
        minus_half = const("minus_half")
        before, ones, slots = const("before"), const("ones"), const("slots")

        filled = sem("psum_filled")
        emptied = {"a": sem("psum_emptied_by_scalar"), "v": sem("psum_emptied_by_vector")}
        slab_in = [sem(f"slab_in{i}") for i in range(R)]
        s_const = sem("constants_in")
        s_x = sem("x_in")
        s_mem = sem("memory_in")
        s_gain = sem("gain_rows_in")
        s_relr = sem("rel_rows_in")
        s_relv = sem("rel_vector_out")
        s_rel = sem("rel_bias_in")
        s_cw = sem("conv_weights_in")
        s_cbuf = sem("conv_state_in")
        s_bc = sem("row_params_in")
        s_s0 = sem("ret_state_in")
        s_rw = sem("router_in")
        s_fg = sem("final_gain_in")
        s_kvo = sem("new_attn_rows_out")
        s_mko = sem("new_mem_rows_out")
        s_spo = sem("new_ret_prompt_out")
        s_yo = sem("y_out")
        s_outp = sem("conv_state_out")
        s_st = sem("ret_state_out")
        s_own = {"a": sem("scalar_steps"), "v": sem("vector_steps"), "g": sem("pool_steps")}
        s_sq = sem("squares_summed")
        s_rstd = sem("rstd_ready")
        s_h = sem("h_ready")
        s_relx = sem("rel_vector_ready")
        s_sig = sem("conv_gate_ready")
        s_u = sem("conv_u_ready")
        s_conv = sem("conv_ready")
        s_lnv = sem("conv_var_ready")
        s_lnr = sem("conv_norm_ready")
        s_cln = sem("conv_rstd_ready")
        s_oc = sem("conv_out_ready")
        s_rot = sem("rotary_ready")
        s_blk = sem("query_blocks_ready")
        s_kd = sem("decayed_k_ready")
        s_q0 = sem("decayed_q_ready")
        s_zero = sem("zeros_ready")
        s_max = sem("band_max_ready")
        s_exp = sem("band_exp_ready")
        s_p = sem("band_p_ready")
        s_gnv = sem("group_var_ready")
        s_gnr = sem("group_rstd_ready")
        s_silu = sem("gate_silu_ready")
        s_gs = sem("gate_gain_ready")
        s_ob = sem("ret_out_ready")
        s_xmax = sem("cross_max_ready")
        s_xexp = sem("cross_exp_ready")
        s_xp = sem("cross_p_ready")
        s_rmax = sem("router_max_ready")
        s_rexp = sem("router_exp_ready")
        s_comb = sem("combine_ready")
        s_mask = sem("chosen_ready")
        s_cur = sem("current_row_ready")
        s_S = sem("slot_matrix_ready")
        s_units = sem("units_ready")
        s_xlast = sem("last_x_ready")
        s_y = sem("y_ready")

        def wait_filled(eng, *key):
            eng.wait_ge(filled, INDEX[key] + 1)

        def wait_emptied(eng, *key):
            who, n = DRAIN[key]
            eng.wait_ge(emptied[who], n)

        class Loop:

            def __init__(self, name, jobs, slabs, n):
                self.jobs, self.slabs, self.n = jobs, slabs, n
                self.index = {key: i for i, (key, _, _) in enumerate(jobs)}
                self.bank = {key: banks for key, banks, _ in jobs}
                self.filled = sem(name + "_filled")
                self.emptied = {"a": sem(name + "_emptied_by_scalar"), "v": sem(name + "_emptied_by_vector")}
                self.slab_in = [sem(f"{name}_slab_in{i}") for i in range(RF)]
                self.per, self.drain, last = {"a": 0, "v": 0}, {}, {}
                for key, banks, who in jobs:
                    if who:
                        self.per[who] += 1
                        self.drain[key] = (who, self.per[who])
                    for b in banks:
                        last[b] = key
                self.prev = {}
                for key, banks, _ in jobs:
                    self.prev[key] = [(last[b], True) if b not in self.prev else (self.prev[b], False) for b in banks]
                    for b in banks:
                        self.prev[b] = key
                assert len(slabs) % RF == 0

            def prime(self, instruction, who=None):
                if who:
                    instruction.then_inc(self.emptied[who], self.per[who])
                else:
                    instruction.then_inc(self.filled, len(self.jobs))

            def wait_filled(self, eng, i, *key, back=0):
                per = len(self.jobs)
                eng.wait_ge(self.filled, i * per + (per * (1 - back) + self.index[key] + 1))

            def wait_emptied(self, eng, i, *key, back=0):
                who, k = self.drain[key]
                eng.wait_ge(self.emptied[who], i * self.per[who] + (self.per[who] * (1 - back) + k))

            def begin(self, pe, i, *key):
                for prev, back in self.prev[key]:
                    self.wait_emptied(pe, i, *prev, back=int(back))
                return bank[self.bank[key][0]]

            def emptied_by(self, instruction, *key):
                instruction.then_inc(self.emptied[self.drain[key][0]], 1)

            def slot(self, s):
                k = s % RF
                return ring[:, k * SLAB:(k + 1) * SLAB] if k < R else slot4[:, (k - R) * SLAB:(k - R + 1) * SLAB]

            def stream(self, sp, i, which, gate, up_, down):
                for s, (kind, k0, nk, c0, w, _) in enumerate(self.slabs):
                    t_ = {"gate": gate, "up": up_, "down": down}[kind]
                    src = t_[bass.ds(which, 1), :, k0:k0 + nk, c0:c0 + w].rearrange("e p k n -> p (e k) n")
                    dst = self.slot(s)[:, 0:nk * w].rearrange("p (k n) -> p k n", k=nk)
                    self.wait_filled(sp, i, *self.slabs[(s - RF) % len(self.slabs)][5], back=int(s < RF))
                    sp.dma_start(dst, src).then_inc(self.slab_in[s % RF], 16)

            def slab(self, pe, i, s):
                kind, _, nk, _, w, _ = self.slabs[s]
                pe.wait_ge(self.slab_in[s % RF], i * (16 * len(self.slabs) // RF) + 16 * (s // RF + 1))
                return self.slot(s)[:, 0:nk * w].rearrange("p (k n) -> p k n", k=nk)

        half_ffn = Loop("ffn", dense_jobs(), dense_slabs(), 2)
        routed = Loop("routed", routed_jobs(), routed_slabs(), NE)

        def units(eng, step):
            with eng.Fori(0, NE) as i:
                step(i)
            eng.wait_ge(s_units, 1)
            n_units = eng.value_load(expert[0:1, UNITS:UNITS + 1], min_val=NE, max_val=UNITS)
            with eng.Fori(NE, UNITS) as i:
                with eng.If(n_units > i):
                    step(i)

        class Steps:

            def __init__(self, eng, who):
                self.eng, self.own, self.count, self.last, self.who = eng, s_own[who], {}, None, who

            def did(self, instruction, signal=None):
                s = self.own if signal is None else signal
                instruction.then_inc(s, 1)
                self.count[id(s)] = self.count.get(id(s), 0) + 1
                self.last = (s, self.count[id(s)])

            def emptied(self, instruction, *key):
                assert DRAIN[key][0] == self.who, key
                self.did(instruction, emptied[self.who])
                assert self.count[id(emptied[self.who])] == DRAIN[key][1], key

            def settle(self):
                self.eng.wait_ge(*self.last)

        def ready_x(eng, n, t):
            l, k = divmod(n, 3)
            if n == 0:
                eng.wait_ge(s_x, 32)
            elif n == 3 * DEPTH:
                eng.wait_ge(s_xlast, 1)
            elif k == 0:
                half_ffn.wait_emptied(eng, half_ffn.n - 1, "down", 1, t)
            else:
                wait_emptied(eng, ("out", "o")[k - 1], l, 1, t)

        block = ctx.enter_context(nc.Block())

        @block.sync
        def _(sp):
            at_layer = [s for s, sl in enumerate(SLABS) if sl[0] == "w_in" and sl[2][0] == 1][0]

            def ffn(w):
                sp_gate = a["ffn_w_gate"][w].rearrange("(k p) (h n) -> h p k n", p=P, h=2)
                sp_up = a["ffn_w_up"][w].rearrange("(k p) (h n) -> h p k n", p=P, h=2)
                sp_down = a["ffn_w_down"][w].rearrange("(h k p) n -> h p k n", p=P, h=2)
                return sp_gate, sp_up, sp_down

            def moe(w):
                return [a["moe_w_" + k][w].rearrange("e (k p) n -> e p k n", p=P) for k in ("gate", "up", "down")]

            for s, (name, how, where, _) in enumerate(SLABS):
                if s == at_layer:
                    wait_filled(sp, "o", 0, 1, NT - 1)
                    with sp.Fori(0, half_ffn.n) as i:
                        half_ffn.stream(sp, i, i, *ffn(0))
                if at_layer <= s < at_layer + R:
                    key = half_ffn.slabs[len(half_ffn.slabs) - RF + s % R][5]
                    half_ffn.wait_filled(sp, half_ffn.n - 1, *key)
                if s >= R:
                    wait_filled(sp, *SLABS[s - R][3])
                base = ring[:, (s % R) * SLAB:(s % R + 1) * SLAB]
                if how == "rows":
                    l, k0, nk, c0, w = where
                    src = a[name][l].rearrange("(k p) n -> p k n", p=P)[:, k0:k0 + nk, c0:c0 + w]
                    dst = base[:, 0:nk * w].rearrange("p (k n) -> p k n", k=nk)
                elif how == "past":
                    l, g = where
                    src = a[name][l, 4 * g:4 * g + 4].rearrange("n (k p) h d -> p (n k) (h d)", p=P)
                    dst = base.rearrange("p (j d) -> p j d", j=8)
                else:
                    l, n = where
                    src = a[name][l, n].rearrange("(m p) h d -> p m (h d)", p=P)
                    dst = base.rearrange("p (j d) -> p j d", j=2)
                sp.dma_start(dst, src).then_inc(slab_in[s % R], 16)
            wait_filled(sp, "o", 1, 1, NT - 1)
            with sp.Fori(0, NE) as i:
                routed.stream(sp, i, i, *moe(0))
            sp.wait_ge(s_units, 1)
            n_units = sp.value_load(expert[0:1, UNITS:UNITS + 1], min_val=NE, max_val=UNITS)
            with sp.Fori(NE, UNITS) as i:
                with sp.If(n_units > i):
                    e = sp.value_load(expert[0:1, bass.ds(i, 1)], min_val=0, max_val=NE - 1)
                    routed.stream(sp, i, e, *moe(0))

        @block.tensor
        def _(pe):
            at = [0, 0]

            def begin(*key):
                for prev in PREV[key]:
                    wait_emptied(pe, *prev)
                return bank[BANK[key][0]]

            def end(instruction, *key):
                assert JOBS[at[0]][0] == key, (JOBS[at[0]][0], key)
                at[0] += 1
                instruction.then_inc(filled, 1)

            def slab(name):
                s = at[1]
                at[1] += 1
                assert SLABS[s][0] == name, (SLABS[s], name)
                pe.wait_ge(slab_in[s % R], 16 * (s // R + 1))
                return ring[:, (s % R) * SLAB:(s % R + 1) * SLAB]

            def turn(out, src):
                return nc.tensor.transpose(out, src, ident[0:src.shape[0], 0:src.shape[0]])

            def product(key, name, left, groups, w, tiles, c, ready=None):
                for g, (k0, nk) in enumerate(groups):
                    wt = slab(name)[:, 0:nk * w].rearrange("p (k n) -> p k n", k=nk)
                    for t in range(tiles):
                        if g == 0:
                            begin(*key, c, t)
                        out = bank[BANK[key + (c, t)][0]]
                        for k in range(k0, k0 + nk):
                            if ready:
                                ready(k, t)
                            ins = nc.tensor.matmul(out[:, 0:w], left(k, t), wt[:, k - k0, :],
                                                   start=(g == 0 and k == k0),
                                                   stop=(g == len(groups) - 1 and k == k0 + nk - 1))
                        if g == len(groups) - 1:
                            end(ins, *key, c, t)

            halves = [(0, 4), (4, 4)]

            def hT_at(k, t):
                return hT[:, k, t * P:(t + 1) * P]

            def oT_at(k, t):
                return oT[:, k, t * P:(t + 1) * P]

            def norm(n):
                for t in range(NT):
                    pe.wait_ge(s_h, NT * n + t + 1)
                    for half in range(2):
                        b = begin("hT", n, t, half)
                        for j in range(4):
                            k = 4 * half + j
                            ins = turn(b[:, j * P:(j + 1) * P], htok[:, t, k * P:(k + 1) * P])
                        end(ins, "hT", n, t, half)
                wait_emptied(pe, "hT", n, NT - 1, 1)

            def dense_steps(L):
                with pe.Fori(0, L.n) as i:
                    at_ = [0]

                    def product(kind, c, left, groups, w):
                        for g, (k0, nk) in enumerate(groups):
                            wt = L.slab(pe, i, at_[0])
                            at_[0] += 1
                            for t in range(NT):
                                if g == 0:
                                    L.begin(pe, i, kind, c, t)
                                out = bank[L.bank[(kind, c, t)][0]]
                                for k in range(k0, k0 + nk):
                                    ins = nc.tensor.matmul(out[:, 0:w], left(k, t), wt[:, k - k0, :],
                                                           start=(g == 0 and k == k0),
                                                           stop=(g == len(groups) - 1 and k == k0 + nk - 1))
                                if g == len(groups) - 1:
                                    ins.then_inc(L.filled, 1)

                    for c in range(4):
                        if c < 3:
                            product("gate", c, hT_at, halves, FF_CHUNKS[c][1])
                            product("up", c, hT_at, halves, FF_CHUNKS[c][1])
                        if c:
                            for t in range(NT):
                                L.wait_emptied(pe, i, "up", c - 1, t)
                                b = L.begin(pe, i, "aT", c - 1, t)
                                for j in range(FF_GROUPS[c - 1][1]):
                                    ins = turn(b[:, j * P:(j + 1) * P],
                                               acts[:, NT * ((c - 1) % 2) + t, j * P:(j + 1) * P])
                                ins.then_inc(L.filled, 1)
                    L.wait_emptied(pe, i, "aT", 2, NT - 1)
                    for c in range(2):
                        product("down", c, lambda k, t: actT[:, k, t * P:(t + 1) * P], FF_GROUPS, 512)

            def routed_step(i):
                L = routed
                at_ = [0]

                def group(kind, c, left, g, groups, w):
                    wt = L.slab(pe, i, at_[0])
                    at_[0] += 1
                    k0, nk = groups[g]
                    if g == 0:
                        L.begin(pe, i, kind, c)
                    out = bank[L.bank[(kind, c)][0]]
                    for k in range(k0, k0 + nk):
                        ins = nc.tensor.matmul(out[:, 0:w], left[:, k, :], wt[:, k - k0, :],
                                               start=(k == 0), stop=(g == len(groups) - 1 and k == k0 + nk - 1))
                    ins.then_inc(L.filled, 1)

                def turn_acts(c):
                    L.wait_emptied(pe, i, "up", c)
                    b = L.begin(pe, i, "aT", c)
                    for j in range(FF_GROUPS[c][1]):
                        ins = turn(b[:, j * P:(j + 1) * P], acts_e[:, c % 2, j * P:(j + 1) * P])
                    ins.then_inc(L.filled, 1)

                pe.wait_ge(s_S, i + 1)
                for g in range(2):
                    b = L.begin(pe, i, "gather", g)
                    for j in range(4):
                        k = 4 * g + j
                        for t in range(NT):
                            ins = nc.tensor.matmul(b[:, j * P:(j + 1) * P], htok[:, t, k * P:(k + 1) * P],
                                                   S[:, t, :], start=(t == 0), stop=(t == NT - 1))
                    ins.then_inc(L.filled, 1)
                b = L.begin(pe, i, "ST")
                for t in range(NT):
                    ins = turn(b[:, t * P:(t + 1) * P], S[:, t, :])
                ins.then_inc(L.filled, 1)
                L.wait_emptied(pe, i, "gather", 1)
                for c in range(3):
                    for kind in ("gate", "up"):
                        for g in range(2):
                            group(kind, c, hTe, g, halves, FF_CHUNKS[c][1])
                    if c:
                        turn_acts(c - 1)
                L.wait_emptied(pe, i, "aT", 1)
                group("down", 0, actT_e, 0, FF_GROUPS, 512)
                group("down", 0, actT_e, 1, FF_GROUPS, 512)
                turn_acts(2)
                L.wait_emptied(pe, i, "aT", 2)
                group("down", 0, actT_e, 2, FF_GROUPS, 512)
                for g in range(3):
                    group("down", 1, actT_e, g, FF_GROUPS, 512)
                for c in range(2):
                    L.wait_emptied(pe, i, "down", c)
                    for t in range(NT):
                        b = L.begin(pe, i, "scatter", c, t)
                        nc.tensor.matmul(b[:, :], ST[:, t, :], Y[:, c * 512:(c + 1) * 512],
                                         start=True, stop=True).then_inc(L.filled, 1)

            pe.wait_ge(s_const, 16)
            pe.wait_ge(s_gain, 48)
            b = begin("gains")
            end(turn(b[:, 0:48], grow[0:48, :]), "gains")
            pe.wait_ge(s_mem, 16)
            for j in range(4):
                b = begin("memT", j)
                for k in range(2):
                    for t in range(2):
                        ins = turn(b[:, k * 256 + t * P:k * 256 + (t + 1) * P],
                                   memtok[:, t, (2 * j + k) * P:(2 * j + k + 1) * P])
                end(ins, "memT", j)
            for l in range(DEPTH):
                norm(3 * l)
                pe.wait_ge(s_cw, 32 * (l + 1))
                b = begin("cw", l)
                for k in range(2):
                    ins = turn(b[:, 32 * k:32 * k + 32], cwr[0:32, k * P:(k + 1) * P])
                end(ins, "cw", l)
                pe.wait_ge(s_cbuf, 16 * (l + 1))
                b = begin("cbuf", l)
                for k in range(2):
                    for g in range(2):
                        ins = turn(b[:, 240 * k + 120 * g:240 * k + 120 * g + 120],
                                   cbufr[0:120, g, k * P:(k + 1) * P])
                end(ins, "cbuf", l)
                for c, (c0, w) in enumerate(IN_CHUNKS):
                    product(("in", l), "w_in", hT_at, halves, w, NT, c)
                    if c == 1:
                        pe.wait_ge(s_u, l + 1)
                        for k in range(2):
                            b = begin("uT", l, k)
                            for t in range(NT):
                                ins = turn(b[:, t * P:(t + 1) * P], proj[:, t, CA + k * P:CA + (k + 1) * P])
                            end(ins, "uT", l, k)
                for c in range(2):
                    product(("mk", l), "wx_k", lambda k, t: memT[:, k, t * P:(t + 1) * P], halves, 512, 2, c,)
                for c in range(2):
                    product(("mv", l), "wx_v", lambda k, t: memT[:, k, t * P:(t + 1) * P], halves, 512, 2, c)
                wait_emptied(pe, "mk", l, 1, 1)
                for j in range(4):
                    b = begin("mkT", l, j)
                    for k in range(2):
                        for t in range(2):
                            ins = turn(b[:, k * 256 + t * P:k * 256 + (t + 1) * P],
                                       mk[:, t, (2 * j + k) * P:(2 * j + k + 1) * P])
                    end(ins, "mkT", l, j)
                for t in range(NT):
                    b = begin("qkA", l, t)
                    for j in range(4):
                        ins = turn(b[:, j * P:(j + 1) * P], proj[:, t, j * P:(j + 1) * P])
                    end(ins, "qkA", l, t)
                for t in range(NT):
                    pe.wait_ge(s_rot, NT * l + t + 1)
                    b = begin("qkB", l, t)
                    for j in range(4):
                        ins = turn(b[:, j * P:(j + 1) * P], proj[:, t, QB + j * P:QB + (j + 1) * P])
                    end(ins, "qkB", l, t)
                wait_emptied(pe, "qkA", l, 2)
                for j in range(4):
                    b = begin("sA", l, j)
                    t, odd = divmod(j, 2)
                    w = (t + 1) * P
                    for i in range(2):
                        ins = nc.tensor.matmul(b[:, i * w:(i + 1) * w],
                                               qkA[64 * odd:64 * odd + 64, i, t * P:(t + 1) * P],
                                               qkA[64 * odd:64 * odd + 64, 2 + i, 0:w], start=True, stop=True)
                    end(ins, "sA", l, j)
                pe.wait_ge(s_blk, l + 1)
                past = None
                for n in range(NS):
                    if n % 4 == 0:
                        past = slab("cache_attn_k").rearrange("p (j d) -> p j d", j=8)
                    b = begin("ktA", l, n)
                    for k in range(2):
                        for t in range(2):
                            ins = turn(b[:, k * 256 + t * P:k * 256 + (t + 1) * P],
                                       past[:, 2 * (n % 4) + t, k * P:(k + 1) * P])
                    end(ins, "ktA", l, n)
                    if n % 2:
                        r = n // 2
                        wait_emptied(pe, "ktA", l, n)
                        b = begin("sS", l, r)
                        for n2 in range(2):
                            for k in range(2):
                                g = 32 * (2 * n2 + k)
                                s_ = 2 * r + n2
                                nc.tensor.matmul(b[g:g + 32, 0:256], qblk[:, k, s_, :], ktA[:, s_ % 4, k, :],
                                                 start=True, stop=True)
                                ins = nc.tensor.matmul(b[g:g + 32, 256:384], qblk[:, k, s_, :],
                                                       qkA[:, 2 + k, 256:384], start=True, stop=True)
                        end(ins, "sS", l, r)
                for h in range(AH):
                    pe.wait_ge(s_p, 6 * l + 2)
                    b = begin("pTA", l, h)
                    turn(b[:, 0:P], lg0[:, h, :])
                    turn(b[:, P:2 * P], lg1[:, h, 0:P])
                    end(turn(b[:, 2 * P:3 * P], lg1[:, h, P:2 * P]), "pTA", l, h)
                wait_emptied(pe, "pTA", l, AH - 1)
                b = begin("oA", l)
                for h in range(AH):
                    lo = 64 * (h % 2)
                    col = 256 * (h // 2)
                    nc.tensor.matmul(b[lo:lo + 64, col:col + 256], proj[:, 0, VA + 64 * h:VA + 64 * h + 64],
                                     pTA[:, h, 0:256], start=True, stop=False)
                    ins = nc.tensor.matmul(b[lo:lo + 64, col + P:col + 256],
                                           proj[:, 1, VA + 64 * h:VA + 64 * h + 64],
                                           pTA[:, h, 256:384], start=False, stop=True)
                end(ins, "oA", l)
                for r in range(4):
                    pe.wait_ge(s_p, 6 * l + 3 + r)
                    b = begin("pTS", l, r)
                    for k in range(3):
                        ins = turn(b[:, k * P:(k + 1) * P], lgS[:, r, k * P:(k + 1) * P])
                    end(ins, "pTS", l, r)
                wait_emptied(pe, "pTS", l, 3)
                b = begin("oS", l)
                for n in range(NS):
                    if n % 4 == 0:
                        past = slab("cache_attn_v").rearrange("p (j d) -> p j d", j=8)
                    for k in range(2):
                        row = 64 * (n % 2) + 32 * k
                        out = b[:, (2 * n + k) * 32:(2 * n + k) * 32 + 32]
                        for t in range(3):
                            left = (past[:, 2 * (n % 4) + t, k * P:(k + 1) * P] if t < 2
                                    else proj[:, 2, VA + k * P:VA + (k + 1) * P])
                            ins = nc.tensor.matmul(out, left, pTS[:, n // 2, t, row:row + 32],
                                                   start=(t == 0), stop=(t == 2))
                end(ins, "oS", l)
                wait_emptied(pe, "qkB", l, 2)
                for h in range(BH):
                    lo = 64 * (h % 2)
                    b = begin("aB", l, h)
                    nc.tensor.matmul(b[:, 0:256], qkB[lo:lo + 64, 2 + h // 2, 0:P], qkB[lo:lo + 64, h // 2, 0:256],
                                     start=True, stop=True)
                    end(nc.tensor.matmul(b[:, 256:384], qkB[lo:lo + 64, 2 + h // 2, P:2 * P],
                                         qkB[lo:lo + 64, h // 2, P:2 * P], start=True, stop=True), "aB", l, h)
                for odd in range(2):
                    b = begin("aS", l, odd)
                    for i in range(2):
                        ins = nc.tensor.matmul(b[:, i * P:(i + 1) * P], qkB[64 * odd:64 * odd + 64, 2 + i, 256:384],
                                               qkB[64 * odd:64 * odd + 64, i, 256:384], start=True, stop=True)
                    end(ins, "aS", l, odd)
                wait_emptied(pe, "aS", l, 1)
                pe.wait_ge(s_q0, BH * (l + 1))
                pe.wait_ge(s_s0, 128 * (l + 1))
                for t in range(NT):
                    b = begin("oB", l, t)
                    for h in range(BH):
                        out = b[:, h * P:(h + 1) * P]

                        def v(j):
                            return proj[:, j, VB + h * P:VB + (h + 1) * P]
                        if t == 0:
                            ins = nc.tensor.matmul(out, attT[:, h, 0:P], v(0), start=True, stop=True)
                        elif t == 1:
                            nc.tensor.matmul(out, attT[:, h, P:256], v(0), start=True, stop=False)
                            ins = nc.tensor.matmul(out, attT[:, h, 256:384], v(1), start=False, stop=True)
                        else:
                            nc.tensor.matmul(out, attS[:, h, :], v(2), start=True, stop=False)
                            for j in range(4):
                                ins = nc.tensor.matmul(out, q0[:, h, j * P:(j + 1) * P], s0[:, j, h, :],
                                                       start=False, stop=(j == 3))
                    end(ins, "oB", l, t)
                pe.wait_ge(s_kd, 2 * l + 1)
                b = begin("nsP", l)
                for h in range(BH):
                    for t in range(2):
                        ins = nc.tensor.matmul(b[0:64, h * P:(h + 1) * P], kd[:, t, h * 64:(h + 1) * 64],
                                               proj[:, t, VB + h * P:VB + (h + 1) * P], start=(t == 0), stop=(t == 1))
                end(ins, "nsP", l)
                pe.wait_ge(s_kd, 2 * l + 2)
                for h in range(BH):
                    b = begin("nsS", l, h)
                    for j in range(4):
                        ins = nc.tensor.matmul(b[:, j * P:(j + 1) * P], ks[:, h, 2 * j:2 * j + 2, :],
                                               proj[:, 2, VB + h * P:VB + (h + 1) * P], start=True, stop=True)
                    end(ins, "nsS", l, h)
                pe.wait_ge(s_conv, 2 * (l + 1))
                for t in range(NT):
                    b = begin("yc", l, t)
                    for k in range(2):
                        ins = turn(b[:, k * P:(k + 1) * P], conv[:, k, t * P:(t + 1) * P])
                    end(ins, "yc", l, t)
                pe.wait_ge(s_ob, NT * (l + 1))
                for k in range(4):
                    b = begin("obT", l, k)
                    for t in range(NT):
                        ins = turn(b[:, t * P:(t + 1) * P], proj[:, t, GB + k * P:GB + (k + 1) * P])
                    end(ins, "obT", l, k)
                pe.wait_ge(s_oc, l + 1)
                for k in range(2):
                    b = begin("ocT", l, k)
                    for t in range(NT):
                        ins = turn(b[:, t * P:(t + 1) * P], proj[:, t, CA + k * P:CA + (k + 1) * P])
                    end(ins, "ocT", l, k)
                wait_emptied(pe, "ocT", l, 1)
                for c in range(2):
                    product(("out", l), "w_out", oT_at, halves, 512, NT, c)
                norm(3 * l + 1)
                for c in range(2):
                    product(("q", l), "wx_q", hT_at, halves, 512, NT, c)
                wait_emptied(pe, "q", l, 1, 2)
                for j in range(4):
                    b = begin("qTx", l, j)
                    for k in range(2):
                        for t in range(2):
                            ins = turn(b[:, k * 256 + t * P:k * 256 + (t + 1) * P],
                                       qx[:, t, (2 * j + k) * P:(2 * j + k + 1) * P])
                    end(ins, "qTx", l, j)
                for j in range(2):
                    b = begin("qTs", l, j)
                    for k in range(4):
                        ins = turn(b[:, k * P:(k + 1) * P], qx[:, 2, (4 * j + k) * P:(4 * j + k + 1) * P])
                    end(ins, "qTs", l, j)
                wait_emptied(pe, "qTs", l, 1)
                for j in range(4):
                    b = begin("xs", l, j)
                    for i in range(2):
                        h = 2 * (j % 2) + i
                        for k in range(2):
                            ins = nc.tensor.matmul(b[:, i * 256:(i + 1) * 256],
                                                   qxT[:, 2 * h + k, (j // 2) * P:(j // 2 + 1) * P],
                                                   mkT[:, 2 * h + k, :], start=(k == 0), stop=(k == 1))
                    end(ins, "xs", l, j)
                pe.wait_ge(s_xp, 6 * l + 2)
                for h in range(XH):
                    b = begin("xpT", l, h)
                    for mt in range(2):
                        for t in range(2):
                            ins = turn(b[:, mt * 256 + t * P:mt * 256 + (t + 1) * P],
                                       px[:, t, h, mt * P:(mt + 1) * P])
                    end(ins, "xpT", l, h)
                wait_emptied(pe, "xpT", l, XH - 1)
                for h in range(XH):
                    b = begin("xo", l, h)
                    for i in range(2):
                        for mt in range(2):
                            ins = nc.tensor.matmul(b[:, i * 256:(i + 1) * 256],
                                                   mv[:, mt, (2 * h + i) * P:(2 * h + i + 1) * P],
                                                   pxT[:, h, mt, :], start=(mt == 0), stop=(mt == 1))
                    end(ins, "xo", l, h)
                for r in range(5):
                    if r < 4:
                        for n2 in range(2):
                            mem = slab("cache_mem_k").rearrange("p (m d) -> p m d", m=2)
                            for j in range(4):
                                b = begin("kTs", l, 2 * r + n2, j)
                                for k in range(2):
                                    for mt in range(2):
                                        ins = turn(b[:, k * 256 + mt * P:k * 256 + (mt + 1) * P],
                                                   mem[:, mt, (2 * j + k) * P:(2 * j + k + 1) * P])
                                end(ins, "kTs", l, 2 * r + n2, j)
                        wait_emptied(pe, "kTs", l, 2 * r + 1, 2)
                        wait_emptied(pe, "kTs", l, 2 * r + 1, 3)
                        b = begin("xss", l, r)
                        for n2 in range(2):
                            for hp in range(2):
                                g = 32 * (2 * n2 + hp)
                                for i in range(4):
                                    ins = nc.tensor.matmul(b[g:g + 32, 0:256], qxb[:, 4 * hp + i, 2 * r + n2, :],
                                                           kTs[:, n2, 4 * hp + i, :], start=(i == 0), stop=(i == 3))
                        end(ins, "xss", l, r)
                    if r >= 1:
                        q = r - 1
                        pe.wait_ge(s_xp, 6 * l + 3 + q)
                        b = begin("xpTs", l, q)
                        for mt in range(2):
                            ins = turn(b[:, mt * P:(mt + 1) * P], pxs[:, q % 2, mt * P:(mt + 1) * P])
                        end(ins, "xpTs", l, q)
                        wait_emptied(pe, "xpTs", l, q)
                        if q == 0:
                            begin("xos", l)
                        for n2 in range(2):
                            n = 2 * q + n2
                            mem = slab("cache_mem_v").rearrange("p (m d) -> p m d", m=2)
                            for k in range(KC):
                                col = 64 * n2 + TS * (k // 2)
                                out = bank[k // 4][:, (k % 4) * P + TS * n:(k % 4) * P + TS * (n + 1)]
                                for mt in range(2):
                                    ins = nc.tensor.matmul(out, mem[:, mt, k * P:(k + 1) * P],
                                                           pxsT[:, q % 2, mt, col:col + TS],
                                                           start=(mt == 0), stop=(mt == 1))
                end(ins, "xos", l)
                wait_emptied(pe, "xos", l)
                for c in range(2):
                    product(("o", l), "wx_o", oT_at, halves, 512, NT, c)
                (routed if l % 2 else half_ffn).prime(turn(bank[7][:, 0:P], ident))
                norm(3 * l + 2)
                if l % 2:
                    pe.wait_ge(s_rw, 16)
                    b = begin("route", l)
                    for t in range(NT):
                        for k in range(KC):
                            ins = nc.tensor.matmul(b[:, t * NE:(t + 1) * NE], hT_at(k, t), rw[:, k, :],
                                                   start=(k == 0), stop=(k == KC - 1))
                    end(ins, "route", l)
                    pe.wait_ge(s_mask, 1)
                    b = begin("pos", l)
                    for t in range(NT):
                        for j in range(t + 1):
                            nc.tensor.matmul(b[:, t * NE:(t + 1) * NE], before if j == t else ones, mask[:, j, :],
                                             start=(j == 0), stop=(j == t))
                    for t in range(NT):
                        ins = nc.tensor.matmul(b[:, NT * NE:(NT + 1) * NE], ones, mask[:, t, :],
                                               start=(t == 0), stop=(t == NT - 1))
                    end(ins, "pos", l)
                    units(pe, routed_step)
                else:
                    dense_steps(half_ffn)
                    half_ffn.wait_emptied(pe, half_ffn.n - 1, "aT", 2, NT - 1)
                    half_ffn.wait_emptied(pe, half_ffn.n - 1, "down", 1, NT - 1)
            assert at == [len(JOBS), len(SLABS)]

        @block.scalar
        def _(act):
            st = Steps(act, "a")
            A = nc.scalar.activation

            def copy(out, in_, *key):
                wait_filled(act, *key)
                st.emptied(A(out, in_, ACT.Copy), *key)

            def squares(n):
                for t in range(NT):
                    ready_x(act, n, t)
                    st.did(A(htok[:, t, :], x[:, t, :], ACT.Square, accum_out=stat[:, t:t + 1]), s_sq)

            def dense_steps(L):
                with act.Fori(0, L.n) as i:
                    for c in range(4):
                        if c < 3:
                            w = FF_CHUNKS[c][1]
                            for t in range(NT):
                                L.wait_emptied(act, i, "up", (c - 1) % 3, t, back=int(c == 0))
                                L.wait_filled(act, i, "gate", c, t)
                                L.emptied_by(A(gated[:, t, 0:w], bank[t][:, 0:w], ACT.Silu), "gate", c, t)
                        if c:
                            k0, nk = FF_GROUPS[c - 1]
                            for t in range(NT):
                                L.wait_filled(act, i, "aT", c - 1, t)
                                L.emptied_by(A(actT[:, k0:k0 + nk, t * P:(t + 1) * P],
                                               bank[L.bank[("aT", c - 1, t)][0]][:, 0:nk * P].rearrange(
                                                   "p (k n) -> p k n", k=nk), ACT.Copy), "aT", c - 1, t)

            def routed_step(i):
                L = routed
                def copy(out, w, *key):
                    L.wait_filled(act, i, *key)
                    L.emptied_by(A(out, bank[L.bank[key][0]][:, 0:w], ACT.Copy), *key)

                def turned(c):
                    k0, nk = FF_GROUPS[c]
                    copy(actT_e[:, k0:k0 + nk, :].rearrange("p k n -> p (k n)"), nk * P, "aT", c)

                copy(ST.rearrange("p t n -> p (t n)"), NT * P, "ST")
                for c in range(3):
                    w = FF_CHUNKS[c][1]
                    L.wait_emptied(act, i, "up", (0, 1, 0)[c], back=int(c < 2))
                    L.wait_filled(act, i, "gate", c)
                    L.emptied_by(A(gated_e[:, c % 2, 0:w], bank[L.bank[("gate", c)][0]][:, 0:w], ACT.Silu), "gate", c)
                    if c:
                        turned(c - 1)
                turned(2)
                for c in range(2):
                    copy(Y[:, c * 512:(c + 1) * 512], 512, "down", c)

            act.dma_start(x[:, 0:2, :], a["x_prompt"].rearrange("b (t p) d -> p (b t) d", p=P)).then_inc(s_x, 16)
            act.dma_start(x[:, 2, :], a["x_sample"].rearrange("n t d -> (n t) d")).then_inc(s_x, 16)
            act.dma_start(memtok, a["mem_prompt"].rearrange("b (t p) d -> p (b t) d", p=P)).then_inc(s_mem, 16)
            copy(gT[:, 0:48], bank[BANK[("gains",)][0]][:, 0:48], "gains")
            for j in range(4):
                copy(memT[:, 2 * j:2 * j + 2, :],
                     bank[BANK[("memT", j)][0]][:, :].rearrange("p (k n) -> p k n", k=2), "memT", j)
            squares(0)
            for l in range(DEPTH):
                copy(cw, bank[BANK[("cw", l)][0]][:, 0:64].rearrange("p (k n) -> p k n", k=2), "cw", l)
                b = bank[BANK[("cbuf", l)][0]]
                wait_filled(act, "cbuf", l)
                for k in range(2):
                    ins = A(us[:, k, :, 0:30], b[:, 240 * k:240 * k + 240].rearrange("p (n w) -> p n w", n=NS), ACT.Copy)
                    if k:
                        st.emptied(ins, "cbuf", l)

                def in_chunk(c):
                    c0, w = IN_CHUNKS[c]
                    for t in range(NT):
                        copy(proj[:, t, c0:c0 + w], bank[BANK[("in", l, c, t)][0]][:, 0:w], "in", l, c, t)
                in_chunk(0)
                st.settle()
                for t in range(NT):
                    st.did(A(sig[:, t, :], proj[:, t, CB:CB + CC], ACT.Sigmoid), s_sig)
                in_chunk(1)
                for k in range(2):
                    b = bank[BANK[("uT", l, k)][0]]
                    wait_filled(act, "uT", l, k)
                    A(up[:, k, 30:30 + SEQ], b[:, 0:SEQ], ACT.Copy)
                    st.emptied(A(us[:, k, :, 30:46], b[:, SEQ:TOK].rearrange("p (n w) -> p n w", n=NS), ACT.Copy),
                               "uT", l, k)
                for c in range(2, len(IN_CHUNKS)):
                    in_chunk(c)
                st.settle()
                pk = o["new_attn_k_prompt"][l, 0].rearrange("(t p) h d -> p t (h d)", p=P)
                pv = o["new_attn_v_prompt"][l, 0].rearrange("(t p) h d -> p t (h d)", p=P)
                act.dma_start(pk, proj[:, 0:2, KA:KA + 256]).then_inc(s_kvo, 16)
                act.dma_start(pv, proj[:, 0:2, VA:VA + 256]).then_inc(s_kvo, 16)
                act.dma_start(o["new_attn_k_sample"][l].rearrange("n t h d -> (n t) (h d)"),
                              proj[:, 2, KA:KA + 256]).then_inc(s_kvo, 16)
                act.dma_start(o["new_attn_v_sample"][l].rearrange("n t h d -> (n t) (h d)"),
                              proj[:, 2, VA:VA + 256]).then_inc(s_kvo, 16)
                for t in range(NT):
                    st.did(A(proj[:, t, GB:GB + 512], proj[:, t, GB:GB + 512], ACT.Silu), s_silu)
                for name, dst in (("mk", mk), ("mv", mv)):
                    for c in range(2):
                        for t in range(2):
                            copy(dst[:, t, c * 512:(c + 1) * 512], bank[BANK[(name, l, c, t)][0]][:, :], name, l, c, t)
                for j in range(4):
                    copy(mkT[:, 2 * j:2 * j + 2, :],
                         bank[BANK[("mkT", l, j)][0]][:, :].rearrange("p (k n) -> p k n", k=2), "mkT", l, j)
                st.settle()
                act.dma_start(o["new_mem_k_prompt"][l, 0].rearrange("(t p) h d -> p t (h d)", p=P), mk).then_inc(s_mko, 16)
                act.dma_start(o["new_mem_v_prompt"][l, 0].rearrange("(t p) h d -> p t (h d)", p=P), mv).then_inc(s_mko, 16)
                for kind, dst in (("qkA", qkA), ("qkB", qkB)):
                    for t in range(NT):
                        copy(dst[:, :, t * P:(t + 1) * P],
                             bank[BANK[(kind, l, t)][0]][:, :].rearrange("p (k n) -> p k n", k=4), kind, l, t)

                def softmax_exp(dst, neg_max, sums, value, last):
                    ins = A(dst, dst, ACT.Exp, bias=neg_max, accum_out=sums)
                    st.did(ins, s_exp if last else None)

                def exp_prompt():
                    act.wait_ge(s_max, 6 * l + 2)
                    for h in range(AH):
                        softmax_exp(lg0[:, h, :], small[:, h:h + 1], small[:, 16 + h:17 + h], 0, False)
                    for h in range(AH):
                        softmax_exp(lg1[:, h, :], small[:, 4 + h:5 + h], small[:, 20 + h:21 + h], 0, h == AH - 1)

                def exp_sample(r):
                    act.wait_ge(s_max, 6 * l + 3 + r)
                    softmax_exp(lgS[:, r, :], small[:, 8 + r:9 + r], small[:, 24 + r:25 + r], 0, True)

                for n in range(NS):
                    copy(ktA[:, n % 4, :, :],
                         bank[BANK[("ktA", l, n)][0]][:, :].rearrange("p (k n) -> p k n", k=2), "ktA", l, n)
                    if n == 3:
                        exp_prompt()
                    if n % 2 and n >= 5:
                        exp_sample((n - 5) // 2)
                exp_sample(2)
                exp_sample(3)
                for h in range(AH):
                    copy(pTA[:, h, :], bank[BANK[("pTA", l, h)][0]][:, 0:TOK], "pTA", l, h)
                copy(oT[:, 0:2, 0:SEQ], bank[BANK[("oA", l)][0]][:, :].rearrange("p (k n) -> p k n", k=2), "oA", l)
                for r in range(4):
                    copy(pTS[:, r, :, :], bank[BANK[("pTS", l, r)][0]][:, 0:TOK].rearrange("p (k n) -> p k n", k=3),
                         "pTS", l, r)
                b = bank[BANK[("oS", l)][0]]
                wait_filled(act, "oS", l)
                for i in range(2):
                    for k in range(2):
                        src = b[64 * i:64 * i + 64, :].rearrange("p (n k c) -> p n k c", n=NS, k=2)[
                            :, :, k, TS * i:TS * i + TS]
                        dst = oT[64 * i:64 * i + 64, k, SEQ:TOK].rearrange("p (n w) -> p n w", n=NS)
                        ins = A(dst, src, ACT.Copy)
                st.emptied(ins, "oS", l)
                wait_filled(act, "nsP", l)
                st.emptied(A(spr[0:64, :], bank[BANK[("nsP", l)][0]][0:64, :], ACT.Copy), "nsP", l)
                st.settle()
                act.dma_start(o["new_ret_prompt"][l, 0].rearrange("h k v -> k h v"),
                              spr[0:64, :].rearrange("p (h v) -> p h v", h=BH)).then_inc(s_spo, 16)
                act.wait_ge(s_lnr, 2 * l + 2)
                A(proj[:, :, CA:CA + CC], proj[:, :, CA:CA + CC], ACT.Silu).then_inc(s_oc, 1)
                for k in range(4):
                    copy(oT[:, 2 + k, :], bank[BANK[("obT", l, k)][0]][:, 0:TOK], "obT", l, k)
                for k in range(2):
                    copy(oT[:, 6 + k, :], bank[BANK[("ocT", l, k)][0]][:, 0:TOK], "ocT", l, k)
                wait_emptied(act, "nsS", l, BH - 1)
                for n2 in range(2):
                    dst = o["new_ret_sample"][l].rearrange("(j s) h k v -> s k j h v", s=2)[n2]
                    for j in range(4):
                        act.dma_start(dst[:, j], s0[64 * n2:64 * n2 + 64, j]).then_inc(s_st, 16)
                act.wait_ge(s_kvo, 64 * (l + 1))
                act.wait_ge(s_outp, 48 * (l + 1))
                act.wait_ge(s_spo, 16 * (l + 1))
                squares(3 * l + 1)
                for c in range(2):
                    for t in range(NT):
                        copy(qx[:, t, c * 512:(c + 1) * 512], bank[BANK[("q", l, c, t)][0]][:, :], "q", l, c, t)
                for j in range(4):
                    copy(qxT[:, 2 * j:2 * j + 2, :],
                         bank[BANK[("qTx", l, j)][0]][:, :].rearrange("p (k n) -> p k n", k=2), "qTx", l, j)
                act.wait_ge(s_zero, l + 1)
                for j in range(2):
                    b = bank[BANK[("qTs", l, j)][0]]
                    wait_filled(act, "qTs", l, j)
                    for k in range(4):
                        c0 = TS * (k // 2)
                        ins = A(qxb[:, 4 * j + k, :, c0:c0 + TS],
                                b[:, k * P:(k + 1) * P].rearrange("p (n w) -> p n w", n=NS), ACT.Copy)
                    st.emptied(ins, "qTs", l, j)
                for j in range(4):
                    act.wait_ge(s_xmax, 8 * l + j + 1)
                    b = bank[BANK[("xs", l, j)][0]]
                    for i in range(2):
                        c = 2 * j + i
                        ins = A(px[:, j // 2, 2 * (j % 2) + i, :], b[:, i * 256:(i + 1) * 256], ACT.Exp,
                                bias=small[:, 32 + c:33 + c], scale=XD ** -0.5, accum_out=small[:, 40 + c:41 + c])
                        if i == 0:
                            st.did(ins)
                    st.emptied(ins, "xs", l, j)
                for h in range(XH):
                    copy(pxT[:, h, :, :], bank[BANK[("xpT", l, h)][0]][:, :].rearrange("p (k n) -> p k n", k=2),
                         "xpT", l, h)
                for h in range(XH):
                    copy(oT[:, 2 * h:2 * h + 2, 0:SEQ],
                         bank[BANK[("xo", l, h)][0]][:, :].rearrange("p (k n) -> p k n", k=2), "xo", l, h)
                for r in range(5):
                    if r < 4:
                        for n2 in range(2):
                            for j in (0, 2):
                                copy(kTs[:, n2, 2 * j:2 * j + 2, :],
                                     bank[BANK[("kTs", l, 2 * r + n2, j)][0]][:, :].rearrange("p (k n) -> p k n", k=2),
                                     "kTs", l, 2 * r + n2, j)
                        act.wait_ge(s_xmax, 8 * l + 5 + r)
                        if r >= 2:
                            wait_filled(act, "xpTs", l, r - 2)
                        st.emptied(A(pxs[:, r % 2, :], bank[BANK[("xss", l, r)][0]][:, 0:NMEM], ACT.Exp,
                                     bias=small[:, 48 + r:49 + r], scale=XD ** -0.5,
                                     accum_out=small[:, 52 + r:53 + r]), "xss", l, r)
                    if r >= 1:
                        copy(pxsT[:, (r - 1) % 2, :, :],
                             bank[BANK[("xpTs", l, r - 1)][0]][:, 0:2 * P].rearrange("p (k n) -> p k n", k=2),
                             "xpTs", l, r - 1)
                wait_filled(act, "xos", l)
                for k in range(2):
                    ins = A(oT[:, 4 * k:4 * k + 4, SEQ:TOK], bank[k][:, :].rearrange("p (k n) -> p k n", k=4), ACT.Copy)
                st.emptied(ins, "xos", l)
                squares(3 * l + 2)
                if l % 2:
                    act.wait_ge(s_rmax, 1)
                    for t in range(NT):
                        ins = A(rtv(1)[:, t, :], rtv(0)[:, t, :], ACT.Exp, bias=stat[:, 8 + t:9 + t],
                                accum_out=stat[:, 12 + t:13 + t])
                        st.did(ins, s_rexp)
                if l % 2:
                    routed.prime(A(full[:, 0:1], minus_half[:, 0:1], ACT.Copy), "a")
                    units(act, routed_step)
                else:
                    half_ffn.prime(A(full[:, 0:1], minus_half[:, 0:1], ACT.Copy), "a")
                    dense_steps(half_ffn)
                squares(3 * l + 3)
            for t in range(NT):
                act.wait_ge(s_y, t + 1)
                if t < 2:
                    act.dma_start(o["y_prompt"][0, t * P:(t + 1) * P, :], htok[:, t, :]).then_inc(s_yo, 16)
                else:
                    act.dma_start(o["y_sample"].rearrange("n t d -> (n t) d"), htok[:, t, :]).then_inc(s_yo, 16)
            act.wait_ge(s_kvo, 64 * DEPTH)
            act.wait_ge(s_mko, 32 * DEPTH)
            act.wait_ge(s_spo, 16 * DEPTH)
            act.wait_ge(s_yo, 16 * NT)
            act.wait_ge(s_st, 16 * 8 * DEPTH)

        def route(dve, st):
            V = nc.vector

            def go(ins, signal=None):
                st.did(ins, signal)
                st.settle()
            lgts, e_, p_, w_, h1, h2, p2 = (rtv(i) for i in range(7))
            r3 = rt[:, 7 * NT * NE:7 * NT * NE + 24]
            m1, m2, mw, den = (r3[:, 3 * i:3 * i + 3] for i in range(4))
            wait_filled(dve, "route", 1)
            st.emptied(V.tensor_copy(lgts, bank[BANK[("route", 1)][0]][:, 0:NT * NE].rearrange(
                "p (t e) -> p t e", t=NT)), "route", 1)
            st.settle()
            go(V.tensor_reduce(stat[:, 8:11], lgts, AX.X, ALU.max, negate=True), s_rmax)
            dve.wait_ge(s_rexp, NT)
            go(V.reciprocal(stat[:, 12:15], stat[:, 12:15]))
            go(V.tensor_tensor(p_, e_, insert(stat[:, 12:15], 2, NE), ALU.mult))
            order = insert(eight, 1, NT)
            go(V.tensor_reduce(m1, p_, AX.X, ALU.max))
            go(V.tensor_tensor(w_, p_, insert(m1, 2, NE), ALU.is_equal))
            go(V.tensor_tensor(w_, w_, order, ALU.mult))
            go(V.tensor_reduce(mw, w_, AX.X, ALU.max))
            go(V.tensor_tensor(h1, w_, insert(mw, 2, NE), ALU.is_equal))
            go(V.scalar_tensor_tensor(p2, h1, -2.0, p_, ALU.mult, ALU.add))
            go(V.tensor_reduce(m2, p2, AX.X, ALU.max))
            go(V.tensor_tensor(w_, p2, insert(m2, 2, NE), ALU.is_equal))
            go(V.tensor_tensor(w_, w_, order, ALU.mult))
            go(V.tensor_reduce(mw, w_, AX.X, ALU.max))
            go(V.tensor_tensor(h2, w_, insert(mw, 2, NE), ALU.is_equal))
            go(V.tensor_tensor(mask, h1, h2, ALU.add), s_mask)
            go(V.tensor_tensor(den, m1, m2, ALU.add))
            go(V.reciprocal(den, den))
            go(V.tensor_tensor(m1, m1, den, ALU.mult))
            go(V.tensor_tensor(m2, m2, den, ALU.mult))
            go(V.tensor_tensor(h1, h1, insert(m1, 2, NE), ALU.mult))
            go(V.tensor_tensor(h2, h2, insert(m2, 2, NE), ALU.mult))
            go(V.tensor_tensor(comb, h1, h2, ALU.add), s_comb)
            wait_filled(dve, "pos", 1)
            b = bank[BANK[("pos", 1)][0]]
            st.did(V.tensor_copy(full[:, 4:4 + NE], b[:, NT * NE:(NT + 1) * NE]))
            st.emptied(V.scalar_tensor_tensor(posm, b[:, 0:NT * NE].rearrange("p (t e) -> p t e", t=NT), 1.0, mask,
                                              ALU.add, ALU.mult), "pos", 1)
            st.settle()
            go(V.tensor_scalar(posm, posm, 1.0, None, ALU.subtract))
            for t in range(NT):
                ins = V.tensor_scalar(S[:, t, :], slots, posm[:, t, 0:1], None, ALU.is_equal)
                st.did(ins, s_S if t == NT - 1 else None)
            K = 2 * NE
            here, sums, sums2 = (more[:, i * K:(i + 1) * K] for i in range(3))
            pick = cut(more[:, 3 * K:(3 + EXTRA) * K], u=EXTRA)
            src = cut(more[:, (3 + EXTRA) * K:(10 + EXTRA) * K], j=7)
            got = cut(more[:, (10 + EXTRA) * K:(10 + EXTRA) * K + EXTRA * 7], u=EXTRA)
            prod = Y[:, 0:EXTRA * 7 * K].rearrange("p (u j c) -> p u j c", u=EXTRA, j=7)
            here_ = here.rearrange("p (e b) -> p e b", b=2)
            src_ = src.rearrange("p j (e b) -> p j e b", b=2)
            for i in range(2):
                st.did(V.tensor_scalar(here_[:, :, i], full[:, 4:4 + NE], P * (i + 1) + 0.5, None, ALU.is_ge))
                st.did(V.tensor_scalar(src_[:, NT:2 * NT, :, i], posm, float(P * (i + 1)), None, ALU.subtract))
                st.did(V.tensor_copy(src_[:, 0:NT, :, i], comb))
                st.did(V.tensor_scalar(src_[:, 6, :, i], eight, -1.0, float(NE), ALU.mult, ALU.add))
            st.settle()
            was, now = here, sums
            for d in (1, 2, 4, 8):
                st.did(V.tensor_copy(now[:, 0:d], was[:, 0:d]))
                go(V.tensor_tensor(now[:, d:K], was[:, d:K], was[:, 0:K - d], ALU.add))
                was, now = now, (sums2 if now is sums else sums)
            st.did(V.memset(expert[:, :], 0))
            st.did(V.tensor_scalar(full[:, 12:13], was[:, K - 1:K], float(NE), None, ALU.add))
            go(V.tensor_tensor(now, was, here, ALU.mult))
            for u in range(EXTRA):
                st.did(V.tensor_scalar(pick[:, u, :], now, float(u + 1), None, ALU.is_equal))
            st.settle()
            go(V.tensor_tensor(prod, insert(pick, 2, 7), insert(src, 1, EXTRA), ALU.mult))
            go(V.tensor_reduce(got, prod, AX.X, ALU.add))
            st.did(V.tensor_copy(expert[:, NE:UNITS], got[:, :, 6]))
            st.did(V.tensor_copy(expert[:, UNITS:UNITS + 1], full[:, 12:13]), s_units)
            go(V.memset(table[:, UNITS - 1, NT:2 * NT], -1.0))
            st.did(V.tensor_copy(table[:, 0:NE, 0:NT], comb.rearrange("p t e -> p e t")))
            st.did(V.tensor_copy(table[:, 0:NE - 1, NT:2 * NT], posm[:, :, 1:NE].rearrange("p t e -> p e t")))
            st.did(V.tensor_copy(table[:, NE:UNITS, 0:NT], got[:, :, 0:NT]))
            go(V.tensor_copy(table[:, NE - 1:UNITS - 1, NT:2 * NT], got[:, :, NT:2 * NT]))

        @block.vector
        def _(dve):
            st = Steps(dve, "v")
            V = nc.vector

            def norm_rows(n):
                for t in range(NT):
                    if t == 0:
                        dve.wait_ge(s_rstd, n + 1)
                    st.did(V.tensor_scalar(htok[:, t, :], x[:, t, :], stat[:, 4 + t:5 + t], None, ALU.mult), s_h)

            def norm_T(n):
                norm_rows(n)
                l, k = divmod(n, 3)
                for t in range(NT):
                    for half in range(2):
                        wait_filled(dve, "hT", n, t, half)
                        if n == 0 and t == 0 and half == 0:
                            wait_emptied(dve, "gains")
                        g0 = 16 * k + 8 * l + 4 * half
                        st.emptied(V.tensor_tensor(
                            hT[:, 4 * half:4 * half + 4, t * P:(t + 1) * P],
                            bank[BANK[("hT", n, t, half)][0]][:, :].rearrange("p (k n) -> p k n", k=4),
                            insert(gT[:, g0:g0 + 4], 2, P), ALU.mult), "hT", n, t, half)

            def add_x(name, l, *pre):
                for c in range(2):
                    for t in range(NT):
                        key = (name, l) + pre + (c, t)
                        wait_filled(dve, *key)
                        xs = x[:, t, c * 512:(c + 1) * 512]
                        st.emptied(V.tensor_tensor(xs, bank[BANK[key][0]][:, :], xs, ALU.add), *key)

            def dense_steps(L):
                with dve.Fori(0, L.n) as i:
                    for c, (c0, w) in enumerate(FF_CHUNKS):
                        for t in range(NT):
                            if c >= 2:
                                L.wait_filled(dve, i, "aT", c - 2, t)
                            L.wait_filled(dve, i, "up", c, t)
                            L.wait_emptied(dve, i, "gate", c, t)
                            L.emptied_by(V.tensor_tensor(acts[:, NT * (c % 2) + t, 0:w], bank[3 + t][:, 0:w],
                                                         gated[:, t, 0:w], ALU.mult), "up", c, t)
                    for c in range(2):
                        for t in range(NT):
                            L.wait_filled(dve, i, "down", c, t)
                            xs = x[:, t, c * 512:(c + 1) * 512]
                            L.emptied_by(V.tensor_tensor(xs, bank[3 * c + t][:, :], xs, ALU.add), "down", c, t)

            def routed_step(i):
                L = routed
                L.wait_emptied(dve, i, "scatter", 1, NT - 1, back=1)
                V.tensor_copy(cur, table[:, bass.ds(i, 1), :].rearrange("p e j -> p (e j)")).then_inc(s_cur, 1)
                for g in range(2):
                    L.wait_filled(dve, i, "gather", g)
                    g0 = 16 * 2 + 8 + 4 * g
                    L.emptied_by(V.tensor_tensor(
                        hTe[:, 4 * g:4 * g + 4, :], bank[L.bank[("gather", g)][0]][:, :].rearrange(
                            "p (k n) -> p k n", k=4), insert(gT[:, g0:g0 + 4], 2, P), ALU.mult), "gather", g)
                L.wait_filled(dve, i, "ST")
                dve.wait_ge(s_cur, i + 1)
                for t in range(NT):
                    ins = V.tensor_scalar(S[:, t, :], slots, cur[:, NT + t:NT + t + 1], None, ALU.is_equal)
                ins.then_inc(s_S, 1)
                for c, (c0, w) in enumerate(FF_CHUNKS):
                    L.wait_filled(dve, i, "up", c)
                    L.wait_emptied(dve, i, "gate", c)
                    if c == 2:
                        L.wait_filled(dve, i, "aT", 0)
                    L.emptied_by(V.tensor_tensor(acts_e[:, c % 2, 0:w], bank[L.bank[("up", c)][0]][:, 0:w],
                                                 gated_e[:, c % 2, 0:w], ALU.mult), "up", c)
                for c in range(2):
                    for t in range(NT):
                        L.wait_filled(dve, i, "scatter", c, t)
                        xs = x[:, t, c * 512:(c + 1) * 512]
                        L.emptied_by(V.scalar_tensor_tensor(xs, bank[L.bank[("scatter", c, t)][0]][:, :],
                                                            cur[:, t:t + 1], xs, ALU.mult, ALU.add), "scatter", c, t)

            dve.wait_ge(s_relr, 16)
            st.did(V.tensor_copy(relx[0:8, 0:RPAD], relx[0:8, RPAD:RPAD + 1].to_broadcast([8, RPAD])), s_relx)
            dve.wait_ge(s_const, 16)
            for l in range(DEPTH):
                norm_T(3 * l)
                st.did(V.memset(up[:, :, 0:30], 0.0))
                dve.wait_ge(s_rel, 16 * 9 * (l + 1))
                st.did(V.tensor_tensor(rel_p[:, :, P:256], rel_p[:, :, P:256], insert(cmask, 1, AH), ALU.add))
                st.did(V.tensor_tensor(rel_n.rearrange("p r (n j) -> p (r n) j", j=TS),
                                       insert(rel_s[:, PAST:PAST + TS], 1, 32),
                                       smask.rearrange("p r (n j) -> p (r n) j", j=TS), ALU.add))
                dve.wait_ge(s_sig, NT * (l + 1))
                st.did(V.tensor_tensor(proj[:, :, CA:CA + CC], proj[:, :, CA:CA + CC], sig, ALU.mult), s_u)
                for k in range(2):
                    wait_emptied(dve, "uT", l, k)
                    outp = conv[:, k, 0:SEQ]
                    outs_ = conv[:, k, SEQ:TOK].rearrange("p (n w) -> p n w", n=NS)
                    for j in range(CW):
                        inp = up[:, k, j:j + SEQ]
                        ins_ = us[:, k, :, j:j + TS]
                        wj = cw[:, k, j:j + 1]
                        if j == 0:
                            st.did(V.tensor_scalar(outp, inp, wj, cw[:, k, 31:32], ALU.mult, ALU.add))
                            st.did(V.tensor_scalar(outs_, ins_, wj, cw[:, k, 31:32], ALU.mult, ALU.add))
                        else:
                            dve.wait_ge(st.own, st.count[id(st.own)] - 1)
                            st.did(V.scalar_tensor_tensor(outp, inp, wj, outp, ALU.mult, ALU.add))
                            dve.wait_ge(st.own, st.count[id(st.own)] - 1)
                            st.did(V.scalar_tensor_tensor(outs_, ins_, wj, outs_, ALU.mult, ALU.add),
                                   s_conv if j == CW - 1 else None)
                dve.wait_ge(s_mko, 32 * (l + 1))
                for j in range(4):
                    wait_filled(dve, "sA", l, j)
                    t, odd = divmod(j, 2)
                    w = (t + 1) * P
                    ins = V.scalar_tensor_tensor((lg0, lg1)[t][:, odd::2, :], bank[BANK[("sA", l, j)][0]][:, 0:2 * w].rearrange(
                        "p (h k) -> p h k", h=2), AD ** -0.5, rel_p[:, odd::2, 256 - w:256], ALU.mult, ALU.add)
                    st.emptied(ins, "sA", l, j)
                st.settle()
                st.did(V.tensor_reduce(small[:, 0:4], lg0, AX.X, ALU.max, negate=True), s_max)
                st.did(V.tensor_reduce(small[:, 4:8], lg1, AX.X, ALU.max, negate=True), s_max)
                for r in range(4):
                    wait_filled(dve, "sS", l, r)
                    b = bank[BANK[("sS", l, r)][0]]
                    st.did(V.scalar_tensor_tensor(lgS[:, r, 0:PAST], b[:, 0:PAST], AD ** -0.5, rel_s[:, 0:PAST],
                                                  ALU.mult, ALU.add))
                    st.emptied(V.scalar_tensor_tensor(lgS[:, r, PAST:TOK], b[:, PAST:TOK], AD ** -0.5, rel_n[:, r, :],
                                                      ALU.mult, ALU.add), "sS", l, r)
                    st.settle()
                    st.did(V.tensor_reduce(small[:, 8 + r:9 + r], lgS[:, r, :], AX.X, ALU.max, negate=True), s_max)
                dve.wait_ge(s_exp, 5 * l + 1)
                st.did(V.reciprocal(small[:, 16:24], small[:, 16:24]))
                st.settle()
                st.did(V.tensor_tensor(lg0, lg0, insert(small[:, 16:20], 2, P), ALU.mult), s_p)
                st.did(V.tensor_tensor(lg1, lg1, insert(small[:, 20:24], 2, 256), ALU.mult), s_p)
                for r in range(4):
                    dve.wait_ge(s_exp, 5 * l + 2 + r)
                    st.did(V.reciprocal(small[:, 24 + r:25 + r], small[:, 24 + r:25 + r]))
                    st.settle()
                    st.did(V.tensor_scalar(lgS[:, r, :], lgS[:, r, :], small[:, 24 + r:25 + r], None, ALU.mult), s_p)
                wait_emptied(dve, "qkB", l, 2)
                wait_emptied(dve, "oS", l)
                st.did(V.memset(q0, 0.0))
                st.settle()
                for h in range(BH):
                    lo = 64 * (h % 2)
                    for n2 in range(2):
                        src = steps(qkB[lo:lo + 64, h // 2, SEQ + TS * n2:SEQ + TS * n2 + 1], [[32, 4], [1, TS]])
                        dst = steps(q0[64 * n2:64 * n2 + 64, h, TS * n2:TS * n2 + 1], [[160, 4], [1, TS]])
                        ins = V.tensor_tensor(dst, src, insert(qdec[lo:lo + 64, h, :], 1, 4), ALU.mult)
                        if n2:
                            st.did(ins, s_q0)
                        else:
                            st.did(ins)
                for h in range(BH):
                    wait_filled(dve, "aB", l, h)
                    b = bank[BANK[("aB", l, h)][0]]
                    st.did(V.tensor_tensor(attT[:, h, 0:256], b[:, 0:256], decay[:, h, :], ALU.mult))
                    st.emptied(V.tensor_tensor(attT[:, h, 256:384], b[:, 256:384], decay[:, h, 0:P], ALU.mult),
                               "aB", l, h)
                for odd in range(2):
                    wait_filled(dve, "aS", l, odd)
                    st.emptied(V.tensor_tensor(attS[:, odd::2, :], bank[BANK[("aS", l, odd)][0]][:, 0:256].rearrange(
                        "p (h k) -> p h k", h=2), decay_s[:, odd::2, :], ALU.mult), "aS", l, odd)
                for t in range(NT):
                    wait_filled(dve, "oB", l, t)
                    b = bank[BANK[("oB", l, t)][0]]
                    for h in range(BH):
                        st.did(V.bn_stats(bnst[:, 6 * h:6 * h + 6], b[:, h * P:(h + 1) * P]))
                    st.settle()
                    for h in range(BH):
                        st.did(V.bn_aggr(bnag[:, t, 2 * h:2 * h + 2], bnst[:, 6 * h:6 * h + 6]),
                               s_gnv if h == 3 else None)
                    dve.wait_ge(s_gnr, NT * l + t + 1)
                    for h in range(BH):
                        st.did(V.tensor_scalar(gnt[:, h * P:(h + 1) * P], b[:, h * P:(h + 1) * P],
                                               bnag[:, t, 2 * h:2 * h + 1], rstd8[:, t, h:h + 1],
                                               ALU.subtract, ALU.mult), emptied["v"] if h == 3 else None)
                    assert st.last[1] == DRAIN[("oB", l, t)][1]
                    dve.wait_ge(s_gs, NT * l + t + 1)
                    st.settle()
                    st.did(V.tensor_tensor(proj[:, t, GB:GB + 512], gnt, proj[:, t, GB:GB + 512], ALU.mult), s_ob)
                for h in range(BH):
                    wait_filled(dve, "nsS", l, h)
                    st.emptied(V.scalar_tensor_tensor(
                        s0[:, :, h, :], s0[:, :, h, :], GAMMA[h] ** TS,
                        bank[BANK[("nsS", l, h)][0]][:, :].rearrange("p (j v) -> p j v", j=4),
                        ALU.mult, ALU.add), "nsS", l, h)
                dve.wait_ge(s_outp, 48 * (l + 1))
                for t in range(NT):
                    wait_filled(dve, "yc", l, t)
                    b = bank[BANK[("yc", l, t)][0]]
                    st.did(V.bn_stats(bnst[:, 0:6], b[:, 0:CC]))
                    st.settle()
                    st.did(V.bn_aggr(lnag[:, 2 * t:2 * t + 2], bnst[:, 0:6]), s_lnv)
                    dve.wait_ge(s_cln, NT * l + t + 1)
                    st.emptied(V.tensor_scalar(proj[:, t, CA:CA + CC], b[:, 0:CC], lnag[:, 2 * t:2 * t + 1],
                                               lnr[:, t:t + 1], ALU.subtract, ALU.mult), "yc", l, t)
                st.settle()
                dve.wait_ge(s_bc, 48 * (l + 1))
                st.did(V.tensor_tensor(proj[:, :, CA:CA + CC], proj[:, :, CA:CA + CC], insert(bc_cg[:, :], 1, NT),
                                       ALU.mult), s_lnr)
                st.settle()
                st.did(V.tensor_tensor(proj[:, :, CA:CA + CC], proj[:, :, CA:CA + CC], insert(bc_cb[:, :], 1, NT),
                                       ALU.add), s_lnr)
                add_x("out", l)
                norm_T(3 * l + 1)
                st.did(V.memset(qxb, 0.0), s_zero)
                for j in range(4):
                    wait_filled(dve, "xs", l, j)
                    b = bank[BANK[("xs", l, j)][0]]
                    cs = small[:, 32 + 2 * j:34 + 2 * j]
                    st.did(V.tensor_reduce(cs, b[:, :].rearrange("p (h k) -> p h k", h=2), AX.X, ALU.max, negate=True))
                    st.settle()
                    st.did(V.tensor_scalar(cs, cs, XD ** -0.5, None, ALU.mult), s_xmax)
                for t in range(2):
                    wait_emptied(dve, "xs", l, 2 * t + 1)
                    ss = small[:, 40 + 4 * t:44 + 4 * t]
                    st.did(V.reciprocal(ss, ss))
                    st.settle()
                    st.did(V.tensor_tensor(px[:, t, :, :], px[:, t, :, :], insert(ss, 2, NMEM), ALU.mult), s_xp)
                for r in range(4):
                    for n2 in range(2):
                        for j in (1, 3):
                            wait_filled(dve, "kTs", l, 2 * r + n2, j)
                            st.emptied(V.tensor_copy(
                                kTs[:, n2, 2 * j:2 * j + 2, :],
                                bank[BANK[("kTs", l, 2 * r + n2, j)][0]][:, :].rearrange("p (k n) -> p k n", k=2)),
                                "kTs", l, 2 * r + n2, j)
                    wait_filled(dve, "xss", l, r)
                    b = bank[BANK[("xss", l, r)][0]]
                    cs = small[:, 48 + r:49 + r]
                    st.did(V.tensor_reduce(cs, b[:, 0:NMEM], AX.X, ALU.max, negate=True))
                    st.settle()
                    st.did(V.tensor_scalar(cs, cs, XD ** -0.5, None, ALU.mult), s_xmax)
                    wait_emptied(dve, "xss", l, r)
                    ss = small[:, 52 + r:53 + r]
                    st.did(V.reciprocal(ss, ss))
                    st.settle()
                    st.did(V.tensor_scalar(pxs[:, r % 2, :], pxs[:, r % 2, :], ss, None, ALU.mult), s_xp)
                add_x("o", l)
                norm_T(3 * l + 2)
                if l % 2:
                    route(dve, st)
                    routed.prime(V.memset(full[:, 2:3], 0.0), "v")
                    units(dve, routed_step)
                    V.memset(full[:, 3:4], 0.0).then_inc(s_xlast, 1)
                else:
                    half_ffn.prime(V.memset(full[:, 2:3], 0.0), "v")
                    dense_steps(half_ffn)
            n = 3 * DEPTH
            norm_rows(n)
            dve.wait_ge(s_fg, 16)
            st.settle()
            for t in range(NT):
                st.did(V.tensor_tensor(htok[:, t, :], htok[:, t, :], fgain, ALU.mult), s_y)

        @block.gpsimd
        def _(pool):
            st = Steps(pool, "g")
            G = nc.gpsimd

            def rstd(n):
                pool.wait_ge(s_sq, NT * (n + 1))
                st.did(G.tensor_scalar(stat[:, 0:3], stat[:, 0:3], 1.0 / D, EPS, ALU.mult, ALU.add))
                st.settle()
                st.did(G.tensor_tensor(stat[:, 4:7], stat[:, 0:3], minus_half[:, 0:3], ALU.pow), s_rstd)

            pool.dma_start(cst[:, :], a["constants"]).then_inc(s_const, 16)
            for i, name in enumerate(("norm_mix_g", "norm_mem_g", "norm_ffn_g")):
                pool.dma_start(grow[16 * i:16 * i + 16, :], a[name].rearrange("l (k p) -> (l k) p", p=P)).then_inc(s_gain, 16)
            pool.dma_start(relx[0:8, RPAD:RLEN], a["rel_bias_reversed"].rearrange("l h r -> (l h) r")).then_inc(s_relr, 16)
            pool.dma_start(rw, a["router_w"][0].rearrange("(k p) e -> p k e", p=P)).then_inc(s_rw, 16)
            pool.wait_ge(s_relx, 1)
            pool.dma_start(scratch[0], relx[0:8, :]).then_inc(s_relv, 16)
            pool.wait_ge(s_relv, 16)
            pool.dma_start(scratch[1], rows(scratch[0], 0, [[0, P], [1, DEPTH * AH * RLEN]])).then_inc(s_relv, 16)
            for e in range(NE):
                ins = G.memset(eight[:, e:e + 1], float(NE - e))
            st.did(ins)
            pool.wait_ge(s_const, 16)

            def load(l):
                pool.dma_start(cwr[0:31, :], a["conv_w"][l]).then_inc(s_cw, 16)
                pool.dma_start(cwr[31:32, :], a["conv_b"][l:l + 1]).then_inc(s_cw, 16)
                pool.dma_start(cbufr[0:120, :, :],
                               a["state_conv"][l].rearrange("(g n) w c -> (n w) g c", g=2)).then_inc(s_cbuf, 16)
                if l == 0:
                    pool.wait_ge(s_relv, 32)
                pool.dma_start(rel_p, rows(scratch[1], l * AH * RLEN + RPAD, [[DEPTH * AH * RLEN - 1, P], [RLEN, AH], [1, 256]])).then_inc(s_rel, 16)
                for n2 in range(2):
                    for h in range(AH):
                        r0 = 64 * n2 + TS * h
                        pool.dma_start(rel_s[r0:r0 + TS, :],
                                       rows(scratch[1], (l * AH + h) * RLEN + TS - 1,
                                            [[DEPTH * AH * RLEN - 1, TS], [1, PAST + TS]])).then_inc(s_rel, 16)
                for dst, name, w in ((bc_gn, "ret_gn_g", BH * BV), (bc_cg, "conv_ln_g", CC), (bc_cb, "conv_ln_b", CC)):
                    pool.dma_start(dst[:, :], rows(a[name], l * w, [[0, P], [1, w]])).then_inc(s_bc, 16)
                for n2 in range(2):
                    src = a["state_ret"][l].rearrange("(j s) h k v -> s k j h v", s=2)[n2]
                    for j in range(4):
                        pool.dma_start(s0[64 * n2:64 * n2 + 64, j], src[:, j]).then_inc(s_s0, 16)

            for l in range(DEPTH):
                if l == 0:
                    pool.wait_ge(s_mem, 16)
                    wait_emptied(pool, "memT", 3)
                    wait_emptied(pool, "gains")
                load(l)
                if l == 0:
                    rstd(0)
                pool.wait_ge(s_u, l + 1)
                pool.dma_start(o["new_conv_prompt"][l, 0], proj[98:128, 1, CA:CA + CC]).then_inc(s_outp, 16)
                pool.dma_start(o["new_conv_sample"][l, :, 0:14, :], a["state_conv"][l, :, 16:30, :]).then_inc(s_outp, 16)
                pool.dma_start(o["new_conv_sample"][l, :, 14:30, :], proj[:, 2, CA:CA + CC]).then_inc(s_outp, 16)
                for c in range(2, 4):
                    wait_emptied(pool, "in", l, c, 2)
                for t in range(NT):
                    def part(i):
                        return proj[:, t, QB:QB + 512].rearrange("p (b h s w) -> p b h s w", b=2, h=4, s=2)[:, :, :, i, :]

                    def to(i):
                        return part(i)
                    for b_ in range(2):
                        co, si = insert(cos_t[:, t, b_, :], 1, 4), insert(sin_t[:, t, b_, :], 1, 4)
                        tm = [rtmp[:, 128 * i:128 * i + 128].rearrange("p (h w) -> p h w", h=4) for i in range(4)]
                        x1, x2 = part(0)[:, b_], part(1)[:, b_]
                        st.did(G.tensor_tensor(tm[0], x1, co, ALU.mult))
                        st.did(G.tensor_tensor(tm[1], x2, si, ALU.mult))
                        st.did(G.tensor_tensor(tm[2], x2, co, ALU.mult))
                        st.did(G.tensor_tensor(tm[3], x1, si, ALU.mult))
                        st.settle()
                        st.did(G.tensor_tensor(to(0)[:, b_], tm[0], tm[1], ALU.subtract))
                        st.did(G.tensor_tensor(to(1)[:, b_], tm[2], tm[3], ALU.add), s_rot if b_ else None)
                        st.settle()
                for t in range(2):
                    ins = G.tensor_tensor(kd[:, t, :].rearrange("p (h d) -> p h d", h=BH),
                                          proj[:, t, KB:KB + 256].rearrange("p (h d) -> p h d", h=BH),
                                          insert(kdec[:, t, :], 2, BK), ALU.mult)
                    st.did(ins, s_kd if t else None)
                st.did(G.memset(qblk, 0.0))
                wait_emptied(pool, "qkA", l, 2)
                st.settle()
                for i in range(2):
                    for k in range(2):
                        ins = G.tensor_copy(qblk[64 * i:64 * i + 64, k, :, TS * i:TS * i + TS],
                                            qkA[64 * i:64 * i + 64, k, SEQ:TOK].rearrange("p (n w) -> p n w", n=NS))
                        st.did(ins, s_blk if (i, k) == (1, 1) else None)
                wait_emptied(pool, "oS", l)
                for h in range(BH):
                    ins = G.tensor_tensor(ks[:, h, :, :], insert(proj[:, 2, KB + 64 * h:KB + 64 * h + 64], 1, NS),
                                          insert(kmask[:, h, :], 2, BK), ALU.mult)
                    st.did(ins, s_kd if h == 3 else None)
                pool.wait_ge(s_bc, 48 * (l + 1))
                for t in range(NT):
                    pool.wait_ge(s_silu, NT * l + t + 1)
                    st.did(G.tensor_tensor(proj[:, t, GB:GB + 512], proj[:, t, GB:GB + 512], bc_gn[:, :], ALU.mult), s_gs)
                for t in range(NT):
                    pool.wait_ge(s_gnv, NT * l + t + 1)
                    var = bnag[:, t, :].rearrange("p (h s) -> p h s", s=2)[:, :, 1]
                    st.did(G.tensor_scalar(rstd8[:, t, :], var, EPS, None, ALU.add))
                    st.settle()
                    st.did(G.tensor_tensor(rstd8[:, t, :], rstd8[:, t, :], minus_half, ALU.pow), s_gnr)
                for t in range(NT):
                    pool.wait_ge(s_lnv, NT * l + t + 1)
                    st.did(G.tensor_scalar(lnr[:, t:t + 1], lnag[:, 2 * t + 1:2 * t + 2], EPS, None, ALU.add))
                    st.settle()
                    st.did(G.tensor_tensor(lnr[:, t:t + 1], lnr[:, t:t + 1], minus_half[:, 0:1], ALU.pow), s_cln)
                for k in range(1, 4):
                    rstd(3 * l + k)
                    if l == DEPTH - 1 and k == 3:
                        pass
                if l == 0:
                    pool.wait_ge(s_st, 16 * 8)
            wait_emptied(pool, "xos", DEPTH - 1)
            pool.dma_start(fgain, rows(a["final_norm_g"], 0, [[0, P], [1, D]])).then_inc(s_fg, 16)
            pool.wait_ge(s_outp, 16 * 3 * DEPTH)


_INS = ["x_prompt", "x_sample", "cache_attn_k", "cache_attn_v", "state_ret", "state_conv", "cache_mem_k",
        "cache_mem_v", "mem_prompt", "norm_mix_g", "w_in", "ret_gn_g", "conv_w", "conv_b", "conv_ln_g",
        "conv_ln_b", "w_out", "norm_mem_g", "wx_q", "wx_k", "wx_v", "wx_o", "norm_ffn_g", "ffn_w_gate",
        "ffn_w_up", "ffn_w_down", "router_w", "moe_w_gate", "moe_w_up", "moe_w_down", "final_norm_g"]
_OUTS = [("y_prompt", (1, SEQ, D)), ("y_sample", (NS, TS, D)),
         ("new_attn_k_prompt", (DEPTH, 1, SEQ, AH, AD)), ("new_attn_v_prompt", (DEPTH, 1, SEQ, AH, AD)),
         ("new_ret_prompt", (DEPTH, 1, BH, BK, BV)), ("new_conv_prompt", (DEPTH, 1, CW - 1, CC)),
         ("new_mem_k_prompt", (DEPTH, 1, NMEM, XH, XD)), ("new_mem_v_prompt", (DEPTH, 1, NMEM, XH, XD)),
         ("new_attn_k_sample", (DEPTH, NS, TS, AH, AD)), ("new_attn_v_sample", (DEPTH, NS, TS, AH, AD)),
         ("new_ret_sample", (DEPTH, NS, BH, BK, BV)), ("new_conv_sample", (DEPTH, NS, CW - 1, CC))]


def kernel(**inputs):
    import concourse.bacc as _bacc
    from concourse.bass_utils import run_bass_kernel_spmd as _run

    nc = _bacc.Bacc("TRN2", target_bir_lowering=False, num_devices=1)
    arrays, a = {}, {}

    def give(name, array):
        array = np.ascontiguousarray(array)
        arrays[f"in_{name}"] = array
        a[name] = nc.dram_tensor(f"in_{name}", array.shape, mybir.dt.from_np(array.dtype), kind="ExternalInput").ap()

    for name in _INS:
        give(name, np.asarray(inputs[name]))
    give("rel_bias_reversed", np.asarray(inputs["rel_bias"])[:, :, ::-1])
    give("constants", constants())
    o = {name: nc.dram_tensor(f"out_{name}", shape, F32, kind="ExternalOutput").ap() for name, shape in _OUTS}
    scratch = (nc.dram_tensor("bias_vectors", (DEPTH * AH, RLEN), F32, kind="Internal").ap(),
               nc.dram_tensor("bias_vectors_by_row", (P, DEPTH * AH * RLEN), F32, kind="Internal").ap())
    hybrid_encoder(nc, a, o, scratch)
    r = _run(nc, [arrays], core_ids=[0])
    return tuple(r.results[0][f"out_{name}"] for name, _ in _OUTS)
```

```python
from contextlib import ExitStack

import numpy as np

import concourse.bass as bass
from concourse import mybir

F32 = mybir.dt.float32
F32R = mybir.dt.float32r
ALU = mybir.AluOpType
ACT = mybir.ActivationFunctionType
AX = mybir.AxisListType

P = 128
DEPTH = 2
D = 1024
SEQ = 256
NS = 8
TS = 16
PAST = 256
NT = 3
TOK = NT * P
KC = D // P
CHUNK = 64
NMEM = 256
EPS = 1e-6
NEG = -1e30
AH, AD = 4, 64
BH, BK, BV = 4, 64, 128
CC = 256
CW = 31
REL = 128
DIN = 2816
QA, KA, VA, QB, KB, VB, GB, CA, CB = 0, 256, 512, 768, 1024, 1280, 1792, 2304, 2560
XH, XD = 4, 256
FF = 1408
FFK = FF // P
NE = 8
RLEN = 400
RPAD = 143
R = 4
EXTRA = 5
UNITS = NE + EXTRA
NSPLIT = 3
SLAB = 2048
GAMMA = [1.0 - 2.0 ** (-(5.0 + h)) for h in range(BH)]
IN_CHUNKS = [(2304, 512), (0, 512), (512, 512), (1024, 512), (1536, 512), (2048, 256)]
FF_CHUNKS = [(0, 512), (512, 512), (1024, 384)]
FF_GROUPS = [(0, 4), (4, 4), (8, 3)]

CONST = {}
_at = 0
for _name, _width in (("ident", P), ("minus_half", 4), ("cos", NT * 2 * 32), ("sin", NT * 2 * 32), ("decay", BH * 256),
                      ("decay_s", BH * P), ("qdec", BH * TS), ("kdec", 2 * BH), ("kmask", BH * NS),
                      ("smask", 4 * P), ("cmask", P),
                      ("before", P), ("ones", P), ("slots", P)):
    CONST[_name] = (_at, _width)
    _at += _width
NCONST = _at
NFIRST = P + 4


def constants():
    c = np.zeros((P, NCONST), np.float32)

    def put(name, a):
        o, w = CONST[name]
        c[:, o:o + w] = np.asarray(a, np.float64).reshape(P, w)

    p = np.arange(P)
    put("ident", np.eye(P))
    inv = (np.float32(10000.0) ** (-np.arange(32, dtype=np.float32) / np.float32(32))).astype(np.float32)
    pos = np.stack([p, P + p, PAST + p % TS], 1).astype(np.float32)
    ang = (pos[:, :, None] * inv[None, None, :]).astype(np.float32)
    scale = np.array([1.0, BK ** -0.5], np.float32)[None, None, :, None]
    put("cos", np.cos(ang)[:, :, None, :] * scale)
    put("sin", np.sin(ang)[:, :, None, :] * scale)
    lg = np.log(np.array(GAMMA, np.float64))
    dif = np.arange(256)[None, :] - p[:, None]
    put("decay", np.where(dif[:, None] >= 0, np.exp(np.maximum(dif, 0)[:, None] * lg[None, :, None]), 0.0))
    ds = (p % TS)[None, :] - (p % TS)[:, None]
    same = (p // TS)[None, :] == (p // TS)[:, None]
    put("decay_s", np.where((same & (ds >= 0))[:, None], np.exp(np.maximum(ds, 0)[:, None] * lg[None, :, None]), 0.0))
    put("qdec", np.broadcast_to(np.exp((np.arange(TS) + 1.0)[None, :] * lg[:, None])[None], (P, BH, TS)))
    kd = 255.0 - (np.arange(2)[None, :] * P + p[:, None])
    put("kdec", np.exp(kd[:, :, None] * lg[None, None, :]))
    km = np.exp((TS - 1.0 - p % TS)[:, None] * lg[None, :])
    put("kmask", km[:, :, None] * ((p // TS)[:, None, None] == np.arange(NS)[None, None, :]))
    own = (2 * np.arange(4)[None, :] + p[:, None] // 64)
    put("smask", np.where(own[:, :, None] == (p // TS)[None, None, :], 0.0, NEG))
    put("cmask", np.where((p[:, None] < CHUNK) & (p[None, :] >= CHUNK), NEG, 0.0))
    put("minus_half", np.full((P, 4), -0.5))
    put("before", p[:, None] < p[None, :])
    put("ones", np.ones((P, P)))
    put("slots", np.broadcast_to(p[None, :], (P, P)))
    return c


def insert(ap, axis, n):
    dims = [list(d) for d in ap.ap]
    return bass.AP(tensor=ap.tensor, offset=ap.offset, ap=dims[:axis] + [[0, n]] + dims[axis:])


def steps(ap, dims):
    return bass.AP(tensor=ap.tensor, offset=ap.offset, ap=[list(ap.ap[0])] + dims)


def rows(tensor_ap, offset, dims):
    return bass.AP(tensor=tensor_ap.tensor, offset=offset, ap=dims)


T = (6, 7)


def psum_jobs():
    jobs = []
    small = [0]
    big = [0]

    def one(key, who):
        jobs.append((key, (T[small[0] % 2],), who))
        small[0] += 1

    def product(name, chunks, tiles, who):
        for c in range(chunks):
            for t in range(tiles):
                jobs.append((name + (c, t), (3 * (big[0] % 2) + t,), who))
            big[0] += 1

    def memory_values(l, c):
        for t in range(2):
            jobs.append((("mv", l, c, t), (3 * (big[0] % 2) + t,), "a"))
        big[0] += 1

    def norm(n, tiles=range(NT)):
        for t in tiles:
            for half in range(2):
                one(("hT", n, t, half), "v")

    def first_chunk(name, n):
        for t in range(NT):
            if t == 1:
                norm(n, (2,))
            jobs.append((name + (0, t), (3 * (big[0] % 2) + t,), "a"))
        big[0] += 1

    for l in range(DEPTH):
        norm(3 * l, range(NT - 1))
        first_chunk(("in", l), 3 * l)
        one(("cw", l), "a")
        one(("cbuf", l), "a")
        for t in range(NT):
            jobs.append((("in", l, 1, t), (3 * (big[0] % 2) + t,), "a"))
        big[0] += 1
        for b in range(2):
            one(("uT", l, b), "a")
        for c in range(2, len(IN_CHUNKS)):
            if (l, c) == (0, 3):
                for j in range(4):
                    one(("memT", j), "a")
            for t in range(NT):
                jobs.append((("in", l, c, t), (3 * (big[0] % 2) + t,), "a"))
            big[0] += 1
        product(("mk", l), 2, 2, "a")
        for j in range(4):
            one(("mkT", l, j), "a")
        for t in range(NT):
            one(("qkA", l, t), "a")
        for t in range(NT):
            one(("qkB", l, t), "a")
        for j in range(4):
            one(("sA", l, j), "v")
        for n in range(NS):
            one(("ktA", l, n), "a")
            if n % 2:
                one(("sS", l, n // 2), "v")
        memory_values(l, 0)
        for h in range(AH):
            one(("pTA", l, h), "a")
        one(("oA", l), "a")
        for r in range(4):
            one(("pTS", l, r), "a")
        one(("oS", l), "a")
        for h in range(BH):
            one(("aB", l, h), "v")
        one(("oST", l), "a")
        for j in range(2):
            one(("aS", l, j), "v")
        for t in range(NT):
            one(("oB", l, t), "v")
        one(("nsP", l), "a")
        for h in range(BH):
            one(("nsS", l, h), "v")
        for t in range(NT):
            one(("yc", l, t), "v")
        memory_values(l, 1)
        for b in range(BH):
            one(("obT", l, b), "a")
        for b in range(2):
            one(("ocT", l, b), "a")
        product(("out", l), 2, NT, "v")
        norm(3 * l + 1, range(NT - 1))
        first_chunk(("q", l), 3 * l + 1)
        for t in range(NT):
            jobs.append((("q", l, 1, t), (3 * (big[0] % 2) + t,), "a"))
        big[0] += 1
        for j in range(4):
            one(("qTx", l, j), "a")
        for j in range(2):
            one(("qTs", l, j), "a")
        for j in range(4):
            one(("xs", l, j), "a")
        for h in range(XH):
            one(("xpT", l, h), "a")
        for h in range(XH):
            one(("xo", l, h), "v")
        for r in range(5):
            if r < 4:
                for n2 in range(2):
                    for j in range(4):
                        one(("kTs", l, 2 * r + n2, j), "v" if j % 2 else "a")
                one(("xss", l, r), "a")
            if r >= 2:
                one(("xvT", l, r - 2), "v")
            if r >= 1:
                one(("xpTs", l, r - 1), "a")
                one(("xv", l, r - 1), "v")
        one(("xvT", l, 3), "v")
        product(("o", l), 2, NT, "v")
        norm(3 * l + 2)
        if l % 2:
            one(("route", l), "v")
            one(("pos", l), "v")
        big[0] = 0
    return jobs


def slabs():
    out = []

    def product(name, key, l, cols, tiles):
        for c, (c0, w) in enumerate(cols):
            for half in range(2):
                last = tiles - 1 if half or (c == 0 and key[0] == "in") else 0
                reader = ("split", l, 2 * c + half + (4 if key[0] == "o" else 0)) if key[0] in ("q", "o") else key + (c, last)
                out.append((name, "rows", (l, 4 * half, 4, c0, w), reader))

    full = [(0, 512), (512, 512)]

    def memory_values(l, c):
        for half in range(2):
            out.append(("wx_v", "rows", (l, 4 * half, 4, 512 * c, 512), ("mv", l, c, half)))

    for l in range(DEPTH):
        product("w_in", ("in", l), l, IN_CHUNKS, NT)
        product("wx_k", ("mk", l), l, full, 2)
        for g in range(2):
            out.append(("cache_attn_k", "past", (l, g), ("ktA", l, 4 * g + 3)))
        memory_values(l, 0)
        for g in range(2):
            out.append(("cache_attn_v", "past", (l, g), ("oS", l)))
        memory_values(l, 1)
        product("w_out", ("out", l), l, full, NT)
        product("wx_q", ("q", l), l, full, NT)
        for r in range(5):
            if r < 4:
                for n in (2 * r, 2 * r + 1):
                    out.append(("cache_mem_k", "mem", (l, n), ("kTs", l, n, 3)))
            if r >= 1:
                for n in (2 * r - 2, 2 * r - 1):
                    out.append(("cache_mem_v", "mem", (l, n), ("xv", l, r - 1)))
        product("wx_o", ("o", l), l, full, NT)
    return out


def dense_jobs():
    jobs, small = [], 0
    for c in range(4):
        if c < 3:
            for kind in ("gate", "up"):
                jobs += [((kind, c, t), (3 * (kind == "up") + t,), "a" if kind == "gate" else "v") for t in range(NT)]
        if c:
            for t in range(NT):
                jobs.append((("aT", c - 1, t), (T[small % 2],), "v"))
                small += 1
    jobs += [(("down", c, t), (3 * c + t,), "v") for c in range(2) for t in range(NT)]
    return jobs


def dense_slabs():
    out = []
    for c, (c0, w) in enumerate(FF_CHUNKS):
        for kind in ("gate", "up"):
            for half in range(2):
                out.append((kind, 4 * half, 4, c0, w, (kind, c, 0 if half == 0 else NT - 1)))
    for c in range(2):
        for g, (k0, nk) in enumerate(FF_GROUPS):
            out.append(("down", k0, nk, 512 * c, 512, ("down", c, 0 if g < 2 else NT - 1)))
    return out


def routed_jobs():
    jobs = [(("gather", 0), (6,), "v"), (("gather", 1), (7,), "v"), (("ST",), (6,), "a")]
    for c in range(3):
        for kind in ("gate", "up"):
            jobs += [((kind, c, "first"), (), None), ((kind, c), (2 * (kind == "up") + c % 2,), "a" if kind == "gate" else "v")]
        if c:
            jobs.append((("aT", c - 1), (T[c % 2],), "a"))
    jobs += [(("down", 0, 0), (), None), (("down", 0, 1), (), None), (("aT", 2), (T[1],), "a"), (("down", 0), (4,), "v"),
             (("down", 1, 0), (), None), (("down", 1, 1), (), None), (("down", 1), (5,), "v")]
    jobs += [(("scatter", c, t), (3 * c + t,), "v") for c in range(2) for t in range(NT)]
    return jobs


def routed_slabs():
    out = []
    for c, (c0, w) in enumerate(FF_CHUNKS):
        for kind in ("gate", "up"):
            out.append((kind, 0, 4, c0, w, (kind, c, "first")))
            out.append((kind, 4, 4, c0, w, (kind, c)))
    for c in range(2):
        for g, (k0, nk) in enumerate(FF_GROUPS):
            out.append(("down", k0, nk, 512 * c, 512, ("down", c, g) if g < 2 else ("down", c)))
    return out


def hybrid_encoder(nc, a, o, scratch):
    JOBS = psum_jobs()
    INDEX = {key: i for i, (key, _, _) in enumerate(JOBS)}
    DRAIN, PREV, _last, _n = {}, {}, {}, {"a": 0, "v": 0}
    for key, banks, who in JOBS:
        _n[who] += 1
        DRAIN[key] = (who, _n[who])
        PREV[key] = [_last[b] for b in banks if b in _last]
        for b in banks:
            _last[b] = key
    BANK = {key: banks for key, banks, _ in JOBS}
    SLABS = slabs()

    with ExitStack() as ctx:
        def sem(name):
            return ctx.enter_context(nc.semaphore(name))

        total = [0]

        def sb(name, width):
            total[0] += width
            return ctx.enter_context(nc.sbuf_tensor(name, [P, width], F32))

        bank = [ctx.enter_context(nc.psum_tensor(f"bank{i}", [P, 512], F32)) for i in range(8)]

        x = sb("x", NT * D)[:, :].rearrange("p (t d) -> p t d", t=NT)
        fT_ = sb("features_T", KC * TOK)
        features_at = nc.sbuf_base - 4 * KC * TOK
        hT = fT_[:, :].rearrange("p (k n) -> p k n", k=KC)
        oT = hT
        ring = sb("ring", R * SLAB)
        memT_ = sb("memT", KC * NMEM)
        memT = memT_[:, :].rearrange("p (k n) -> p k n", k=KC)
        mem_kv = sb("mem_kv", 4 * D)
        mv = mem_kv[:, 0:2 * D].rearrange("p (t d) -> p t d", t=2)
        mkT = mem_kv[:, 2 * D:4 * D].rearrange("p (k n) -> p k n", k=KC)
        cst = sb("consts", NCONST)
        stat = sb("stat", 64)
        rel_p = sb("rel_p", AH * 256)[:, :].rearrange("p (h k) -> p h k", h=AH)
        rel_s = sb("rel_s", PAST + TS)
        rel_n = sb("rel_n", 4 * P)[:, :].rearrange("p (r k) -> p r k", r=4)
        bc_gn = sb("bc_gn", BH * BV)
        bc_cg = sb("bc_cg", CC)
        bc_cb = sb("bc_cb", CC)
        comb = sb("comb", NT * NE)[:, :].rearrange("p (t e) -> p t e", t=NT)
        rw = sb("rw", KC * NE)[:, :].rearrange("p (k e) -> p k e", k=KC)
        rt = sb("rt", 8 * NT * NE)
        small = sb("small", 128)
        mask = sb("chosen", NT * NE)[:, :].rearrange("p (t e) -> p t e", t=NT)
        posm = sb("slot_of", NT * NE)[:, :].rearrange("p (t e) -> p t e", t=NT)
        table = sb("table", UNITS * 2 * NT)[:, :].rearrange("p (e j) -> p e j", e=UNITS)
        cur = sb("current", 2 * NT)[:, :]
        more = sb("more", 2 * NE * (3 + EXTRA + 7) + EXTRA * 7)
        full = sb("counts", 16)[:, :]
        expert = ctx.enter_context(nc.sbuf_tensor("expert_of_unit", [P, UNITS + 1], mybir.dt.int32))

        arena_w = (nc.sbuf_bytes_remaining() if callable(nc.sbuf_bytes_remaining) else nc.sbuf_bytes_remaining) // 4 - 128
        arena = ctx.enter_context(nc.sbuf_tensor("arena", [P, arena_w], F32))
        arena_at = nc.sbuf_base - 4 * arena_w

        class Plan:
            def __init__(self):
                self.at = 0

            def take(self, w):
                self.at += w
                assert self.at <= arena_w, (self.at, arena_w)
                return arena[:, self.at - w:self.at]

        def cut(ap, **k):
            names = list(k)
            s = "p (" + " ".join(names) + " w) -> p " + " ".join(names) + " w"
            return ap.rearrange(s, **k)

        m = Plan()
        proj = cut(m.take(NT * DIN), t=NT)
        qkA = cut(m.take(4 * TOK), b=4)
        qblk = m.take(2 * NS * 32).rearrange("p (b n c) -> p b n c", b=2, n=NS)
        qkB = cut(m.take(4 * TOK), b=4)
        at0 = m.at
        mk = arena[:, at0:at0 + 2 * D].rearrange("p (t d) -> p t d", t=2)
        lg0 = cut(m.take(AH * P), h=AH)
        lg1 = cut(m.take(AH * 256), h=AH)
        lgS = cut(m.take(4 * TOK), r=4)
        pTA = cut(m.take(AH * TOK), h=AH)
        pTS = m.take(4 * TOK).rearrange("p (r k n) -> p r k n", r=4, k=3)
        end_a = m.at
        m.at = at0
        attT = cut(m.take(BH * TOK), h=BH)
        attS = cut(m.take(BH * P), h=BH)
        q0 = cut(m.take(BH * 512), h=BH)
        ks = m.take(BH * 512).rearrange("p (h n d) -> p h n d", h=BH, n=NS)
        end_b = m.at
        m.at = max(end_a, end_b)
        ktA = m.take(4 * 512).rearrange("p (n b k) -> p n b k", n=4, b=2)
        s0 = m.take(16 * BV).rearrange("p (j h v) -> p j h v", j=4, h=BH)
        kd = cut(m.take(2 * 256), t=2)
        spr = ktA.rearrange("p n b k -> p (n b k)")[:, 0:BH * BV]
        svals = ktA.rearrange("p n b k -> p (n b k)")[:, BH * BV:BH * BV + 512]
        cw = cut(m.take(2 * 32), b=2)
        up = cut(m.take(2 * (SEQ + 30)), b=2)
        us = m.take(2 * NS * 46).rearrange("p (b n w) -> p b n w", b=2, n=NS)
        conv_ = m.take(2 * TOK)
        conv = cut(conv_, b=2)
        cwr = conv_[:, 0:CC]
        cbufr = cut(conv_[:, CC:3 * CC], g=2)
        sig = proj[:, :, CB:CB + CC]
        rtmp = m.take(2 * 256)

        n_ = Plan()
        htok = cut(n_.take(NT * D), t=NT)
        qx = cut(n_.take(NT * D), t=NT)
        qxT = cut(n_.take(KC * SEQ), k=KC)
        qxb = n_.take(KC * NS * 32).rearrange("p (k n c) -> p k n c", k=KC, n=NS)
        px = n_.take(2 * XH * NMEM).rearrange("p (t h m) -> p t h m", t=2, h=XH)
        pxT = n_.take(XH * 2 * SEQ).rearrange("p (h m n) -> p h m n", h=XH, m=2)
        kTs = n_.take(2 * KC * NMEM).rearrange("p (s k m) -> p s k m", s=2, k=KC)
        m_ = Plan()
        m_.at = n_.at - 2 * KC * NMEM - 2 * XH * 2 * SEQ
        pxs = cut(m_.take(2 * NMEM), s=2)
        xvals = m_.take(512)
        pxsT = m_.take(2 * 2 * P).rearrange("p (s m n) -> p s m n", s=2, m=2)

        arena_r = nc.alloc_sbuf_tensor_at("arena_parts", [P, arena_w], F32R, offset=arena_at)
        features_r = nc.alloc_sbuf_tensor_at("features_parts", [P, KC * TOK], F32R, offset=features_at)
        split0 = (arena_w - NSPLIT * 2 * SLAB) // 8 * 8

        def parts(width, **k):
            f.at += 2 * width
            assert f.at <= split0, (f.at, split0)
            return [cut(arena_r[:, f.at - n * width:f.at - (n - 1) * width], **k) for n in (2, 1)]

        f = Plan()
        actT = parts(FFK * TOK, k=FFK)
        f.take(KC * TOK)
        hT_parts = [cut(features_r[:, :], k=KC), cut(arena_r[:, f.at - KC * TOK:f.at], k=KC)]
        assert f.at <= split0
        oT_parts = [hT_parts[0], cut(arena_r[:, NT * D:2 * NT * D], k=KC)]
        acts = cut(mem_kv[:, 0:2 * NT * 512], s=2 * NT)
        f.at = 0
        Y = parts(D, k=1)
        S = cut(arena[:, f.at:f.at + NT * P], t=NT)
        S_r = cut(arena_r[:, f.at:f.at + NT * P], t=NT)
        ST = cut(arena_r[:, f.at + NT * P:f.at + 2 * NT * P], t=NT)
        prod_at = arena[:, 0:EXTRA * 7 * 2 * NE]
        f.at = NT * D
        h_parts = parts(NT * D, t=NT)
        actT_e = cut(f.take(FFK * P), k=FFK)
        hTe = [cut(features_r[:, i * D:(i + 1) * D], k=KC) for i in range(2)]
        acts_e = cut(fT_[:, 2 * D:3 * D], s=2)

        g_row = [arena[:, NT * D:NT * D + D]] * 2 + [mem_kv[:, 3 * D:4 * D]] * 2 + [
            memT_[:, 0:D], memT_[:, D:2 * D], memT_[:, 0:D]]
        memtok = cut(arena[:, at0:at0 + 2 * D], t=2)
        relx = arena[:, at0 + 2 * D + P:at0 + 2 * D + P + RLEN]
        gnt = rtmp
        bnst = sb("bnst", 24)
        bnag = sb("bnag", NT * 8)[:, :].rearrange("p (t j) -> p t j", t=NT)
        rstd8 = sb("rstd8", NT * 4)[:, :].rearrange("p (t j) -> p t j", t=NT)
        lnag = sb("lnag", 8)
        lnr = sb("lnr", 4)
        eight = sb("eight", NE)[:, :]

        def rtv(i):
            return cut(rt[:, i * NT * NE:(i + 1) * NT * NE], t=NT)

        def const(name):
            off, w = CONST[name]
            return cst[:, off:off + w]

        ident = const("ident")
        cos_t = const("cos").rearrange("p (t b w) -> p t b w", t=NT, b=2)
        sin_t = const("sin").rearrange("p (t b w) -> p t b w", t=NT, b=2)
        decay = const("decay").rearrange("p (h i) -> p h i", h=BH)
        decay_s = const("decay_s").rearrange("p (h i) -> p h i", h=BH)
        qdec = const("qdec").rearrange("p (h i) -> p h i", h=BH)
        kdec = const("kdec").rearrange("p (t h) -> p t h", t=2)
        kmask = const("kmask").rearrange("p (h n) -> p h n", h=BH)
        smask = const("smask").rearrange("p (r k) -> p r k", r=4)
        cmask = const("cmask")
        minus_half = const("minus_half")
        before, ones, slots = const("before"), const("ones"), const("slots")

        filled = sem("psum_filled")
        emptied = {"a": sem("psum_emptied_by_scalar"), "v": sem("psum_emptied_by_vector")}
        slab_in = [sem(f"slab_in{i}") for i in range(R)]
        s_const = sem("constants_in")
        s_first = sem("first_constants_in")
        s_x = [sem(f"x_tile_in{t}") for t in range(NT)]
        s_mem = sem("memory_in")
        s_gain = [sem(f"gain_row_in{n}") for n in range(3 * DEPTH + 1)]
        s_hpart = sem("h_high_part_ready")
        s_opart = sem("cross_result_high_part_ready")
        s_whigh = sem("cross_slab_high_part_ready")
        s_wsplit = sem("cross_slab_split")
        s_gpart = sem("h_token_high_part_ready")
        s_relr = sem("rel_rows_in")
        s_relv = sem("rel_vector_out")
        s_rel = sem("rel_bias_in")
        s_cw = sem("conv_weights_in")
        s_cbuf = sem("conv_state_in")
        s_bc = sem("row_params_in")
        s_s0 = sem("ret_state_in")
        s_rw = sem("router_in")
        s_kvo = sem("new_attn_rows_out")
        s_mko = sem("new_mem_keys_out")
        s_mvo = sem("new_mem_values_out")
        s_spo = sem("new_ret_prompt_out")
        s_yo = sem("y_out")
        s_outp = sem("conv_state_out")
        s_st = sem("ret_state_out")
        s_own = {"a": sem("scalar_steps"), "v": sem("vector_steps"), "g": sem("pool_steps")}
        s_sq = sem("squares_summed")
        s_rstd = sem("rstd_ready")
        s_h = sem("h_ready")
        s_relx = sem("rel_vector_ready")
        s_sig = sem("conv_gate_ready")
        s_u = sem("conv_u_ready")
        s_conv = sem("conv_ready")
        s_lnv = sem("conv_var_ready")
        s_lnr = sem("conv_norm_ready")
        s_cln = sem("conv_rstd_ready")
        s_oc = sem("conv_out_ready")
        s_rot = sem("rotary_ready")
        s_blk = sem("query_blocks_ready")
        s_kd = sem("decayed_k_ready")
        s_q0 = sem("decayed_q_ready")
        s_zero = sem("zeros_ready")
        s_max = sem("band_max_ready")
        s_exp = sem("band_exp_ready")
        s_p = sem("band_p_ready")
        s_gnv = sem("group_var_ready")
        s_gnr = sem("group_rstd_ready")
        s_silu = sem("gate_silu_ready")
        s_gs = sem("gate_gain_ready")
        s_ob = sem("ret_out_ready")
        s_xmax = sem("cross_max_ready")
        s_xp = sem("cross_p_ready")
        s_rmax = sem("router_max_ready")
        s_rexp = sem("router_exp_ready")
        s_comb = sem("combine_ready")
        s_mask = sem("chosen_ready")
        s_cur = sem("current_row_ready")
        s_S = sem("slot_matrix_ready")
        s_units = sem("units_ready")
        s_xlast = sem("last_x_ready")

        def wait_filled(eng, *key):
            eng.wait_ge(filled, INDEX[key] + 1)

        def wait_emptied(eng, *key):
            who, n = DRAIN[key]
            eng.wait_ge(emptied[who], n)

        class Loop:

            def __init__(self, name, jobs, slabs, n, slots, paired, n_split, head):
                self.jobs, self.slabs, self.n, self.slots = jobs, slabs, n, slots
                self.n_split = n_split
                self.index = {key: i for i, (key, _, _) in enumerate(jobs)}
                self.bank = {key: banks for key, banks, _ in jobs}
                self.filled = sem(name + "_filled")
                self.emptied = {"a": sem(name + "_emptied_by_scalar"), "v": sem(name + "_emptied_by_vector")}
                self.slab_in = [sem(f"{name}_slab_in{i}") for i in range(len(slots))]
                self.high = sem(name + "_slab_high_part_ready")
                self.split = sem(name + "_slab_split")
                self.high_out = sem(name + "_result_high_part_ready")
                self.per, self.drain, last = {"a": 0, "v": 0}, {}, {}
                for key, banks, who in jobs:
                    if who:
                        self.per[who] += 1
                        self.drain[key] = (who, self.per[who])
                    for b in banks:
                        last[b] = key
                self.prev = {}
                for key, banks, _ in jobs:
                    self.prev[key] = [(last[b], True) if b not in self.prev else (self.prev[b], False) for b in banks]
                    for b in banks:
                        self.prev[b] = key
                assert len(slabs) % len(slots) == 0 and n_split % NSPLIT == 0
                self.pairs = [key for key, _, who in jobs if who and key[0] in paired]
                self.events, at = [], 0
                for s in range(n_split):
                    to = self.index[slabs[s - NSPLIT][5]] + 1 if s >= NSPLIT else head[s]
                    for key, _, who in jobs[at:to]:
                        if who:
                            self.events.append(key)
                    at = max(at, to)
                    self.events.append(("split", s))
                self.events += [key for key, _, who in jobs[at:] if who]

            def prime(self, instruction, who=None):
                if who == "split":
                    instruction.then_inc(self.split, self.n_split)
                elif who:
                    instruction.then_inc(self.emptied[who], self.per[who])
                else:
                    instruction.then_inc(self.filled, len(self.jobs))

            def wait_filled(self, eng, i, *key, back=0):
                per = len(self.jobs)
                eng.wait_ge(self.filled, i * per + (per * (1 - back) + self.index[key] + 1))

            def wait_emptied(self, eng, i, *key, back=0):
                who, k = self.drain[key]
                eng.wait_ge(self.emptied[who], i * self.per[who] + (self.per[who] * (1 - back) + k))

            def begin(self, pe, i, *key):
                for prev, back in self.prev[key]:
                    self.wait_emptied(pe, i, *prev, back=int(back))
                return bank[self.bank[key][0]]

            def emptied_by(self, instruction, *key):
                instruction.then_inc(self.emptied[self.drain[key][0]], 1)

            def raw(self, s):
                _, _, nk, _, w, _ = self.slabs[s]
                return self.slots[s % len(self.slots)][:, 0:nk * w]

            def part(self, s, low):
                _, _, nk, _, w, _ = self.slabs[s]
                o_ = split0 + (s % NSPLIT) * 2 * SLAB + low * SLAB
                return arena_r[:, o_:o_ + nk * w]

            def wait_split(self, eng, i, s, back=0):
                per = self.n_split
                eng.wait_ge(self.split, i * per + (per * (1 - back) + s + 1))

            def split_high(self, act, i, s):
                n_ = len(self.slots)
                act.wait_ge(self.slab_in[s % n_], i * (16 * len(self.slabs) // n_) + 16 * (s // n_ + 1))
                self.wait_filled(act, i, *self.slabs[(s - NSPLIT) % self.n_split][5], back=int(s < NSPLIT))
                nc.scalar.activation(self.part(s, 0), self.raw(s), ACT.Copy).then_inc(self.high, 1)

            def split_low(self, dve, i, s):
                dve.wait_ge(self.high, i * self.n_split + s + 1)
                nc.vector.tensor_tensor(self.part(s, 1), self.raw(s), self.part(s, 0).bitcast(F32),
                                        ALU.subtract).then_inc(self.split, 1)

            def high_part(self, act, i, out, in_, *key):
                self.wait_filled(act, i, *key)
                nc.scalar.activation(out, in_, ACT.Copy).then_inc(self.high_out, 1)

            def low_part(self, dve, i, out, in_, high, *key):
                dve.wait_ge(self.high_out, i * len(self.pairs) + self.pairs.index(key) + 1)
                self.emptied_by(nc.vector.tensor_tensor(out, in_, high.bitcast(F32), ALU.subtract), *key)

            def stream(self, sp, i, which, gate, up_, down):
                for s, (kind, k0, nk, c0, w, _) in enumerate(self.slabs):
                    t_ = {"gate": gate, "up": up_, "down": down}[kind]
                    src = t_[bass.ds(which, 1), :, k0:k0 + nk, c0:c0 + w].rearrange("e p k n -> p (e k) n")
                    dst = self.raw(s).rearrange("p (k n) -> p k n", k=nk)
                    n_ = len(self.slots)
                    was = (s - n_) % len(self.slabs)
                    if was < self.n_split:
                        self.wait_split(sp, i, was, back=int(s < n_))
                    else:
                        self.wait_filled(sp, i, *self.slabs[was][5], back=int(s < n_))
                    sp.dma_start(dst, src).then_inc(self.slab_in[s % n_], 16)

            def slab(self, pe, i, s):
                nk, w = self.slabs[s][2], self.slabs[s][4]
                if s >= self.n_split:
                    n_ = len(self.slots)
                    pe.wait_ge(self.slab_in[s % n_], i * (16 * len(self.slabs) // n_) + 16 * (s // n_ + 1))
                    return self.raw(s).rearrange("p (k n) -> p k n", k=nk)
                self.wait_split(pe, i, s)
                return [self.part(s, low).rearrange("p (k n) -> p k n", k=nk) for low in range(2)]

        ring_slots = [ring[:, k * SLAB:(k + 1) * SLAB] for k in range(R)]
        kv_slots = [mem_kv[:, k * SLAB:(k + 1) * SLAB] for k in range(2)]
        half_ffn = Loop("ffn", dense_jobs(), dense_slabs(), 2, ring_slots[0:3], ("aT",), len(dense_slabs()),
                        (0, 0, 0))
        routed = Loop("routed", routed_jobs(), routed_slabs(), NE, ring_slots + kv_slots, ("gather", "down"),
                      12, (0, 2, 3))

        def units(eng, step):
            with eng.Fori(0, NE) as i:
                step(i)
            eng.wait_ge(s_units, 1)
            n_units = eng.value_load(expert[0:1, UNITS:UNITS + 1], min_val=NE, max_val=UNITS)
            with eng.Fori(NE, UNITS) as i:
                with eng.If(n_units > i):
                    step(i)

        class Steps:

            def __init__(self, eng, who):
                self.eng, self.own, self.count, self.last, self.who = eng, s_own[who], {}, None, who

            def did(self, instruction, signal=None):
                s = self.own if signal is None else signal
                instruction.then_inc(s, 1)
                self.count[id(s)] = self.count.get(id(s), 0) + 1
                self.last = (s, self.count[id(s)])

            def emptied(self, instruction, *key):
                assert DRAIN[key][0] == self.who, key
                self.did(instruction, emptied[self.who])
                assert self.count[id(emptied[self.who])] == DRAIN[key][1], key

            def settle(self):
                self.eng.wait_ge(*self.last)

        def ready_x(eng, n, t):
            l, k = divmod(n, 3)
            if n == 0:
                eng.wait_ge(s_x[t], 16)
            elif n == 3 * DEPTH:
                eng.wait_ge(s_xlast, 1)
            elif k == 0:
                half_ffn.wait_emptied(eng, half_ffn.n - 1, "down", 1, t)
            else:
                wait_emptied(eng, ("out", "o")[k - 1], l, 1, t)

        def part(l, m, low):
            o_ = split0 + ((2 * (m % NSPLIT)) + low) * SLAB
            return arena_r[:, o_:o_ + SLAB]

        WHERE = {sl[3]: s for s, sl in enumerate(SLABS) if sl[3][0] == "split"}

        def w_high(act, l, m):
            s = WHERE[("split", l, m)]
            act.wait_ge(slab_in[s % R], 16 * (s // R + 1))
            if m >= NSPLIT:
                q = m - NSPLIT
                key = ("q", l, 0, NT - 1) if q < 2 else ("q", l, 1, NT - 1 if q == 3 else 0) if q < 4 else ("o", l, 0, 0)
                wait_filled(act, *key)
            nc.scalar.activation(part(l, m, 0), ring[:, (s % R) * SLAB:(s % R + 1) * SLAB], ACT.Copy).then_inc(s_whigh, 1)

        def w_low(dve, l, m):
            s = WHERE[("split", l, m)]
            dve.wait_ge(s_whigh, 8 * l + m + 1)
            nc.vector.tensor_tensor(part(l, m, 1), ring[:, (s % R) * SLAB:(s % R + 1) * SLAB], part(l, m, 0).bitcast(F32),
                                    ALU.subtract).then_inc(s_wsplit, 1)

        def stream_values(l, q):
            b = bank[BANK[("xvT", l, q)][0]][:, :].rearrange("p (k n g h i) -> p k g n h i", k=4, n=2, g=2, h=2)
            outs = [y[:, :, SEQ:TOK].rearrange("p (g k) (n i) -> p g k n i", g=2, i=TS) for y in oT_parts]
            return [(b[:, kk, :, :, kk // 2, :], *(y[:, :, kk, 2 * q:2 * q + 2, :] for y in outs)) for kk in range(4)]

        block = ctx.enter_context(nc.Block())

        @block.sync
        def _(sp):
            for t in range(2):
                sp.dma_start(x[:, t, :], a["x_prompt"][0, t * P:(t + 1) * P, :]).then_inc(s_x[t], 16)
            sp.dma_start(x[:, 2, :], a["x_sample"].rearrange("n t d -> (n t) d")).then_inc(s_x[2], 16)
            at_layer = [s for s, sl in enumerate(SLABS) if sl[0] == "w_in" and sl[2][0] == 1][0]

            def ffn(w):
                sp_gate = a["ffn_w_gate"][w].rearrange("(k p) (h n) -> h p k n", p=P, h=2)
                sp_up = a["ffn_w_up"][w].rearrange("(k p) (h n) -> h p k n", p=P, h=2)
                sp_down = a["ffn_w_down"][w].rearrange("(h k p) n -> h p k n", p=P, h=2)
                return sp_gate, sp_up, sp_down

            def moe(w):
                return [a["moe_w_" + k][w].rearrange("e (k p) n -> e p k n", p=P) for k in ("gate", "up", "down")]

            for s, (name, how, where, _) in enumerate(SLABS):
                if s == at_layer:
                    wait_filled(sp, "o", 0, 1, NT - 1)
                    with sp.Fori(0, half_ffn.n) as i:
                        half_ffn.stream(sp, i, i, *ffn(0))
                if at_layer <= s < at_layer + R and s % R < len(half_ffn.slots):
                    half_ffn.wait_split(sp, half_ffn.n - 1, len(half_ffn.slabs) - len(half_ffn.slots) + s % R)
                if s >= R:
                    key = SLABS[s - R][3]
                    if key[0] == "split":
                        sp.wait_ge(s_wsplit, 8 * key[1] + key[2] + 1)
                    else:
                        wait_filled(sp, *key)
                base = ring[:, (s % R) * SLAB:(s % R + 1) * SLAB]
                if how == "rows":
                    l, k0, nk, c0, w = where
                    src = a[name][l].rearrange("(k p) n -> p k n", p=P)[:, k0:k0 + nk, c0:c0 + w]
                    dst = base[:, 0:nk * w].rearrange("p (k n) -> p k n", k=nk)
                elif how == "past":
                    l, g = where
                    src = a[name][l, 4 * g:4 * g + 4].rearrange("n (k p) h d -> p (n k) (h d)", p=P)
                    dst = base.rearrange("p (j d) -> p j d", j=8)
                else:
                    l, n = where
                    src = a[name][l, n].rearrange("(m p) h d -> p m (h d)", p=P)
                    dst = base.rearrange("p (j d) -> p j d", j=2)
                sp.dma_start(dst, src).then_inc(slab_in[s % R], 16)
            wait_filled(sp, "o", 1, 1, NT - 1)
            sp.wait_ge(s_mvo, 16 * DEPTH)
            with sp.Fori(0, NE) as i:
                routed.stream(sp, i, i, *moe(0))
            sp.wait_ge(s_units, 1)
            n_units = sp.value_load(expert[0:1, UNITS:UNITS + 1], min_val=NE, max_val=UNITS)
            with sp.Fori(NE, UNITS) as i:
                with sp.If(n_units > i):
                    e = sp.value_load(expert[0:1, bass.ds(i, 1)], min_val=0, max_val=NE - 1)
                    routed.stream(sp, i, e, *moe(0))

        @block.tensor
        def _(pe):
            at = [0, 0]

            def begin(*key):
                for prev in PREV[key]:
                    wait_emptied(pe, *prev)
                return bank[BANK[key][0]]

            def end(instruction, *key):
                assert JOBS[at[0]][0] == key, (JOBS[at[0]][0], key)
                at[0] += 1
                instruction.then_inc(filled, 1)

            def slab(name):
                s = at[1]
                at[1] += 1
                assert SLABS[s][0] == name, (SLABS[s], name)
                pe.wait_ge(slab_in[s % R], 16 * (s // R + 1))
                return ring[:, (s % R) * SLAB:(s % R + 1) * SLAB]

            def turn(out, src):
                return nc.tensor.transpose(out, src, ident[0:src.shape[0], 0:src.shape[0]])

            def product(key, name, left, groups, w, tiles, c, ready=None):
                for g, (k0, nk) in enumerate(groups):
                    wt = slab(name)[:, 0:nk * w].rearrange("p (k n) -> p k n", k=nk)
                    for t in range(tiles):
                        if g == 0:
                            begin(*key, c, t)
                        out = bank[BANK[key + (c, t)][0]]
                        for k in range(k0, k0 + nk):
                            if ready:
                                ready(k, t)
                            ins = nc.tensor.matmul(out[:, 0:w], left(k, t), wt[:, k - k0, :],
                                                   start=(g == 0 and k == k0),
                                                   stop=(g == len(groups) - 1 and k == k0 + nk - 1))
                        if g == len(groups) - 1:
                            end(ins, *key, c, t)

            halves = [(0, 4), (4, 4)]

            def first_chunk(key, name, w, n):
                wt = [slab(name)[:, 0:4 * w].rearrange("p (k n) -> p k n", k=4) for _ in range(2)]
                for t in range(NT):
                    wait_emptied(pe, "hT", n, t, 1)
                    b = begin(*key, 0, t)
                    for k in range(KC):
                        if k == KC // 2 and t < NT - 1:
                            norm(n, (t + 1,))
                        ins = nc.tensor.matmul(b[:, 0:w], hT_at(k, t), wt[k // 4][:, k % 4, :],
                                               start=(k == 0), stop=(k == KC - 1))
                    end(ins, *key, 0, t)

            def hT_at(k, t):
                return hT[:, k, t * P:(t + 1) * P]

            def oT_at(k, t):
                return oT[:, k, t * P:(t + 1) * P]

            def norm(n, tiles=range(NT)):
                for t in tiles:
                    pe.wait_ge(s_h, NT * n + t + 1)
                    for half in range(2):
                        b = begin("hT", n, t, half)
                        for j in range(4):
                            k = 4 * half + j
                            ins = turn(b[:, j * P:(j + 1) * P], htok[:, t, k * P:(k + 1) * P])
                        end(ins, "hT", n, t, half)

            def matmul3(out, left, right, start, stop):
                nc.tensor.matmul(out, left[0], right[0], start=start, stop=False)
                nc.tensor.matmul(out, left[0], right[1], start=False, stop=False)
                return nc.tensor.matmul(out, left[1], right[0], start=False, stop=stop)

            def w_parts(l, m):
                assert SLABS[at[1]][3] == ("split", l, m)
                at[1] += 1
                pe.wait_ge(s_wsplit, 8 * l + m + 1)
                return [part(l, m, low).rearrange("p (k n) -> p k n", k=4) for low in range(2)]

            def split_tile(b, left, k0, wt, t):
                for k in range(k0, k0 + 4):
                    ins = matmul3(b[:, :], [q[:, k, t * P:(t + 1) * P] for q in left], [q[:, k - k0, :] for q in wt],
                                  k == 0, k == KC - 1)
                return ins

            def split_product(key, l, m, left, c):
                for g in range(2):
                    wt = w_parts(l, m + g)
                    for t in range(NT):
                        b = begin(*key, c, t) if g == 0 else bank[BANK[key + (c, t)][0]]
                        ins = split_tile(b, left, 4 * g, wt, t)
                        if g:
                            end(ins, *key, c, t)

            def dense_steps(L):
                with pe.Fori(0, L.n) as i:
                    at_ = [0]

                    def group(kind, c, left, g, groups, w):
                        k0, nk = groups[g]
                        wt = L.slab(pe, i, at_[0])
                        at_[0] += 1
                        for t in range(NT):
                            if g == 0:
                                L.begin(pe, i, kind, c, t)
                            out = bank[L.bank[(kind, c, t)][0]][:, 0:w]
                            for k in range(k0, k0 + nk):
                                ins = matmul3(out, [q[:, k, t * P:(t + 1) * P] for q in left],
                                              [q[:, k - k0, :] for q in wt], k == 0,
                                              g == len(groups) - 1 and k == k0 + nk - 1)
                            if g == len(groups) - 1:
                                ins.then_inc(L.filled, 1)

                    def turn_acts(c):
                        for t in range(NT):
                            L.wait_emptied(pe, i, "up", c, t)
                            b = L.begin(pe, i, "aT", c, t)
                            for j in range(FF_GROUPS[c][1]):
                                ins = turn(b[:, j * P:(j + 1) * P], acts[:, NT * (c % 2) + t, j * P:(j + 1) * P])
                            ins.then_inc(L.filled, 1)

                    for c in range(3):
                        for kind in ("gate", "up"):
                            for g in range(2):
                                group(kind, c, hT_parts, g, halves, FF_CHUNKS[c][1])
                        if c:
                            turn_acts(c - 1)
                    for c in range(2):
                        for g in range(3):
                            if (c, g) == (0, 2):
                                turn_acts(2)
                            if c == 0:
                                L.wait_emptied(pe, i, "aT", g, NT - 1)
                            group("down", c, actT, g, FF_GROUPS, 512)

            def routed_step(i):
                L = routed
                at_ = [0]

                def group(kind, c, left, g, groups, w):
                    wt = L.slab(pe, i, at_[0])
                    at_[0] += 1
                    k0, nk = groups[g]
                    if g == 0:
                        L.begin(pe, i, kind, c)
                    out = bank[L.bank[(kind, c)][0]][:, 0:w]
                    for k in range(k0, k0 + nk):
                        start, stop = k == 0, g == len(groups) - 1 and k == k0 + nk - 1
                        if kind == "down":
                            ins = nc.tensor.matmul(out, left[:, k, :], wt[:, k - k0, :], start=start, stop=stop)
                        else:
                            ins = matmul3(out, [q[:, k, :] for q in left], [q[:, k - k0, :] for q in wt], start, stop)
                    ins.then_inc(L.filled, 1)

                def turn_acts(c):
                    L.wait_emptied(pe, i, "up", c)
                    b = L.begin(pe, i, "aT", c)
                    for j in range(FF_GROUPS[c][1]):
                        ins = turn(b[:, j * P:(j + 1) * P], acts_e[:, c % 2, j * P:(j + 1) * P])
                    ins.then_inc(L.filled, 1)

                pe.wait_ge(s_S, i + 1)
                for g in range(2):
                    b = L.begin(pe, i, "gather", g)
                    for j in range(4):
                        k = 4 * g + j
                        for t in range(NT):
                            for low in range(2):
                                ins = nc.tensor.matmul(b[:, j * P:(j + 1) * P], h_parts[low][:, t, k * P:(k + 1) * P],
                                                       S_r[:, t, :], start=(t == 0 and low == 0),
                                                       stop=(t == NT - 1 and low == 1))
                    ins.then_inc(L.filled, 1)
                b = L.begin(pe, i, "ST")
                for t in range(NT):
                    ins = turn(b[:, t * P:(t + 1) * P], S[:, t, :])
                ins.then_inc(L.filled, 1)
                for c in range(3):
                    for kind in ("gate", "up"):
                        for g in range(2):
                            if (c, kind) == (0, "gate"):
                                L.wait_emptied(pe, i, "gather", g)
                            group(kind, c, hTe, g, halves, FF_CHUNKS[c][1])
                    if c:
                        turn_acts(c - 1)
                for c in range(2):
                    for g in range(3):
                        if (c, g) == (0, 2):
                            turn_acts(2)
                        if c == 0:
                            L.wait_emptied(pe, i, "aT", g)
                        group("down", c, actT_e, g, FF_GROUPS, 512)
                for c in range(2):
                    L.wait_emptied(pe, i, "down", c)
                    for t in range(NT):
                        b = L.begin(pe, i, "scatter", c, t)
                        for low in range(2):
                            ins = nc.tensor.matmul(b[:, :], ST[:, t, :], Y[low][:, 0, c * 512:(c + 1) * 512],
                                                   start=(low == 0), stop=(low == 1))
                        ins.then_inc(L.filled, 1)

            pe.wait_ge(s_first, 16)
            for l in range(DEPTH):
                norm(3 * l, (0,))
                for c, (c0, w) in enumerate(IN_CHUNKS):
                    if (l, c) == (0, 3):
                        pe.wait_ge(s_mem, 16)
                        for j in range(4):
                            b = begin("memT", j)
                            for k in range(2):
                                for t in range(2):
                                    ins = turn(b[:, k * 256 + t * P:k * 256 + (t + 1) * P],
                                               memtok[:, t, (2 * j + k) * P:(2 * j + k + 1) * P])
                            end(ins, "memT", j)
                    if c == 0:
                        first_chunk(("in", l), "w_in", w, 3 * l)
                        pe.wait_ge(s_cw, 32 * (l + 1))
                        b = begin("cw", l)
                        for k in range(2):
                            ins = turn(b[:, 32 * k:32 * k + 32], cwr[0:32, k * P:(k + 1) * P])
                        end(ins, "cw", l)
                        pe.wait_ge(s_cbuf, 16 * (l + 1))
                        b = begin("cbuf", l)
                        for k in range(2):
                            for g in range(2):
                                ins = turn(b[:, 240 * k + 120 * g:240 * k + 120 * g + 120],
                                           cbufr[0:120, g, k * P:(k + 1) * P])
                        end(ins, "cbuf", l)
                        continue
                    product(("in", l), "w_in", hT_at, halves, w, NT, c)
                    if c == 1:
                        pe.wait_ge(s_u, l + 1)
                        for k in range(2):
                            b = begin("uT", l, k)
                            for t in range(NT):
                                ins = turn(b[:, t * P:(t + 1) * P], proj[:, t, CA + k * P:CA + (k + 1) * P])
                            end(ins, "uT", l, k)
                def memory_values(c):
                    product(("mv", l), "wx_v", lambda k, t: memT[:, k, t * P:(t + 1) * P], halves, 512, 2, c)

                wait_emptied(pe, "memT", 3)
                for c in range(2):
                    product(("mk", l), "wx_k", lambda k, t: memT[:, k, t * P:(t + 1) * P], halves, 512, 2, c,)
                wait_emptied(pe, "mk", l, 1, 1)
                for j in range(4):
                    b = begin("mkT", l, j)
                    for k in range(2):
                        for t in range(2):
                            ins = turn(b[:, k * 256 + t * P:k * 256 + (t + 1) * P],
                                       mk[:, t, (2 * j + k) * P:(2 * j + k + 1) * P])
                    end(ins, "mkT", l, j)
                for t in range(NT):
                    b = begin("qkA", l, t)
                    for j in range(4):
                        ins = turn(b[:, j * P:(j + 1) * P], proj[:, t, j * P:(j + 1) * P])
                    end(ins, "qkA", l, t)
                for t in range(NT):
                    pe.wait_ge(s_rot, NT * l + t + 1)
                    b = begin("qkB", l, t)
                    for j in range(4):
                        ins = turn(b[:, j * P:(j + 1) * P], proj[:, t, QB + j * P:QB + (j + 1) * P])
                    end(ins, "qkB", l, t)
                wait_emptied(pe, "qkA", l, 2)
                for j in range(4):
                    b = begin("sA", l, j)
                    t, odd = divmod(j, 2)
                    w = (t + 1) * P
                    for i in range(2):
                        ins = nc.tensor.matmul(b[:, i * w:(i + 1) * w],
                                               qkA[64 * odd:64 * odd + 64, i, t * P:(t + 1) * P],
                                               qkA[64 * odd:64 * odd + 64, 2 + i, 0:w], start=True, stop=True)
                    end(ins, "sA", l, j)
                pe.wait_ge(s_blk, l + 1)
                past = None
                for n in range(NS):
                    if n % 4 == 0:
                        past = slab("cache_attn_k").rearrange("p (j d) -> p j d", j=8)
                    b = begin("ktA", l, n)
                    for k in range(2):
                        for t in range(2):
                            ins = turn(b[:, k * 256 + t * P:k * 256 + (t + 1) * P],
                                       past[:, 2 * (n % 4) + t, k * P:(k + 1) * P])
                    end(ins, "ktA", l, n)
                    if n % 2:
                        r = n // 2
                        wait_emptied(pe, "ktA", l, n)
                        b = begin("sS", l, r)
                        for n2 in range(2):
                            for k in range(2):
                                g = 32 * (2 * n2 + k)
                                s_ = 2 * r + n2
                                nc.tensor.matmul(b[g:g + 32, 0:256], qblk[:, k, s_, :], ktA[:, s_ % 4, k, :],
                                                 start=True, stop=True)
                                ins = nc.tensor.matmul(b[g:g + 32, 256:384], qblk[:, k, s_, :],
                                                       qkA[:, 2 + k, 256:384], start=True, stop=True)
                        end(ins, "sS", l, r)
                memory_values(0)
                for h in range(AH):
                    pe.wait_ge(s_p, 6 * l + 2)
                    b = begin("pTA", l, h)
                    turn(b[:, 0:P], lg0[:, h, :])
                    turn(b[:, P:2 * P], lg1[:, h, 0:P])
                    end(turn(b[:, 2 * P:3 * P], lg1[:, h, P:2 * P]), "pTA", l, h)
                wait_emptied(pe, "pTA", l, AH - 1)
                b = begin("oA", l)
                for h in range(AH):
                    lo = 64 * (h % 2)
                    col = 256 * (h // 2)
                    nc.tensor.matmul(b[lo:lo + 64, col:col + 256], proj[:, 0, VA + 64 * h:VA + 64 * h + 64],
                                     pTA[:, h, 0:256], start=True, stop=False)
                    ins = nc.tensor.matmul(b[lo:lo + 64, col + P:col + 256],
                                           proj[:, 1, VA + 64 * h:VA + 64 * h + 64],
                                           pTA[:, h, 256:384], start=False, stop=True)
                end(ins, "oA", l)
                for r in range(4):
                    pe.wait_ge(s_p, 6 * l + 3 + r)
                    b = begin("pTS", l, r)
                    for k in range(3):
                        ins = turn(b[:, k * P:(k + 1) * P], lgS[:, r, k * P:(k + 1) * P])
                    end(ins, "pTS", l, r)
                wait_emptied(pe, "pTS", l, 3)
                b = begin("oS", l)
                for n in range(NS):
                    if n % 4 == 0:
                        past = slab("cache_attn_v").rearrange("p (j d) -> p j d", j=8)
                    for k in range(2):
                        row = 64 * (n % 2) + 32 * k
                        out = b[row:row + 32, (n // 2) * P:(n // 2 + 1) * P]
                        for t in range(3):
                            right = (past[:, 2 * (n % 4) + t, k * P:(k + 1) * P] if t < 2
                                     else proj[:, 2, VA + k * P:VA + (k + 1) * P])
                            ins = nc.tensor.matmul(out, pTS[:, n // 2, t, row:row + 32], right,
                                                   start=(t == 0), stop=(t == 2))
                end(ins, "oS", l)
                wait_emptied(pe, "qkB", l, 2)
                for h in range(BH):
                    lo = 64 * (h % 2)
                    b = begin("aB", l, h)
                    nc.tensor.matmul(b[:, 0:256], qkB[lo:lo + 64, 2 + h // 2, 0:P], qkB[lo:lo + 64, h // 2, 0:256],
                                     start=True, stop=True)
                    end(nc.tensor.matmul(b[:, 256:384], qkB[lo:lo + 64, 2 + h // 2, P:2 * P],
                                         qkB[lo:lo + 64, h // 2, P:2 * P], start=True, stop=True), "aB", l, h)
                wait_emptied(pe, "oS", l)
                b = begin("oST", l)
                for r in range(4):
                    ins = turn(b[:, r * P:(r + 1) * P], svals[:, r * P:(r + 1) * P])
                end(ins, "oST", l)
                for odd in range(2):
                    b = begin("aS", l, odd)
                    for i in range(2):
                        ins = nc.tensor.matmul(b[:, i * P:(i + 1) * P], qkB[64 * odd:64 * odd + 64, 2 + i, 256:384],
                                               qkB[64 * odd:64 * odd + 64, i, 256:384], start=True, stop=True)
                    end(ins, "aS", l, odd)
                wait_emptied(pe, "aS", l, 1)
                pe.wait_ge(s_q0, BH * (l + 1))
                pe.wait_ge(s_s0, 128 * (l + 1))
                for t in range(NT):
                    b = begin("oB", l, t)
                    for h in range(BH):
                        out = b[:, h * P:(h + 1) * P]

                        def v(j):
                            return proj[:, j, VB + h * P:VB + (h + 1) * P]
                        if t == 0:
                            ins = nc.tensor.matmul(out, attT[:, h, 0:P], v(0), start=True, stop=True)
                        elif t == 1:
                            nc.tensor.matmul(out, attT[:, h, P:256], v(0), start=True, stop=False)
                            ins = nc.tensor.matmul(out, attT[:, h, 256:384], v(1), start=False, stop=True)
                        else:
                            nc.tensor.matmul(out, attS[:, h, :], v(2), start=True, stop=False)
                            for j in range(4):
                                ins = nc.tensor.matmul(out, q0[:, h, j * P:(j + 1) * P], s0[:, j, h, :],
                                                       start=False, stop=(j == 3))
                    end(ins, "oB", l, t)
                pe.wait_ge(s_kd, 2 * l + 1)
                b = begin("nsP", l)
                for h in range(BH):
                    for t in range(2):
                        ins = nc.tensor.matmul(b[0:64, h * P:(h + 1) * P], kd[:, t, h * 64:(h + 1) * 64],
                                               proj[:, t, VB + h * P:VB + (h + 1) * P], start=(t == 0), stop=(t == 1))
                end(ins, "nsP", l)
                pe.wait_ge(s_kd, 2 * l + 2)
                for h in range(BH):
                    b = begin("nsS", l, h)
                    for j in range(4):
                        ins = nc.tensor.matmul(b[:, j * P:(j + 1) * P], ks[:, h, 2 * j:2 * j + 2, :],
                                               proj[:, 2, VB + h * P:VB + (h + 1) * P], start=True, stop=True)
                    end(ins, "nsS", l, h)
                pe.wait_ge(s_conv, 2 * (l + 1))
                for t in range(NT):
                    b = begin("yc", l, t)
                    for k in range(2):
                        ins = turn(b[:, k * P:(k + 1) * P], conv[:, k, t * P:(t + 1) * P])
                    end(ins, "yc", l, t)
                memory_values(1)
                pe.wait_ge(s_ob, NT * (l + 1))
                for k in range(4):
                    b = begin("obT", l, k)
                    for t in range(NT):
                        ins = turn(b[:, t * P:(t + 1) * P], proj[:, t, GB + k * P:GB + (k + 1) * P])
                    end(ins, "obT", l, k)
                pe.wait_ge(s_oc, l + 1)
                for k in range(2):
                    b = begin("ocT", l, k)
                    for t in range(NT):
                        ins = turn(b[:, t * P:(t + 1) * P], proj[:, t, CA + k * P:CA + (k + 1) * P])
                    end(ins, "ocT", l, k)
                wait_emptied(pe, "ocT", l, 1)
                for c in range(2):
                    product(("out", l), "w_out", oT_at, halves, 512, NT, c)
                norm(3 * l + 1, (0,))
                wt = [w_parts(l, m) for m in range(2)]
                for t in range(NT):
                    wait_emptied(pe, "hT", 3 * l + 1, t, 1)
                    b = begin("q", l, 0, t)
                    for g in range(2):
                        if g and t < NT - 1:
                            norm(3 * l + 1, (t + 1,))
                        ins = split_tile(b, hT_parts, 4 * g, wt[g], t)
                    end(ins, "q", l, 0, t)
                split_product(("q", l), l, 2, hT_parts, 1)
                wait_emptied(pe, "q", l, 1, 2)
                for j in range(4):
                    b = begin("qTx", l, j)
                    for k in range(2):
                        for t in range(2):
                            ins = turn(b[:, k * 256 + t * P:k * 256 + (t + 1) * P],
                                       qx[:, t, (2 * j + k) * P:(2 * j + k + 1) * P])
                    end(ins, "qTx", l, j)
                for j in range(2):
                    b = begin("qTs", l, j)
                    for k in range(4):
                        ins = turn(b[:, k * P:(k + 1) * P], qx[:, 2, (4 * j + k) * P:(4 * j + k + 1) * P])
                    end(ins, "qTs", l, j)
                wait_emptied(pe, "qTs", l, 1)
                for j in range(4):
                    b = begin("xs", l, j)
                    for i in range(2):
                        h = 2 * (j % 2) + i
                        for k in range(2):
                            ins = nc.tensor.matmul(b[:, i * 256:(i + 1) * 256],
                                                   qxT[:, 2 * h + k, (j // 2) * P:(j // 2 + 1) * P],
                                                   mkT[:, 2 * h + k, :], start=(k == 0), stop=(k == 1))
                    end(ins, "xs", l, j)
                pe.wait_ge(s_xp, 6 * l + 2)
                for h in range(XH):
                    b = begin("xpT", l, h)
                    for mt in range(2):
                        for t in range(2):
                            ins = turn(b[:, mt * 256 + t * P:mt * 256 + (t + 1) * P],
                                       px[:, t, h, mt * P:(mt + 1) * P])
                    end(ins, "xpT", l, h)
                wait_emptied(pe, "xpT", l, XH - 1)
                for h in range(XH):
                    b = begin("xo", l, h)
                    for i in range(2):
                        for mt in range(2):
                            ins = nc.tensor.matmul(b[:, i * 256:(i + 1) * 256],
                                                   mv[:, mt, (2 * h + i) * P:(2 * h + i + 1) * P],
                                                   pxT[:, h, mt, :], start=(mt == 0), stop=(mt == 1))
                    end(ins, "xo", l, h)
                def turn_values(q):
                    wait_emptied(pe, "xv", l, q)
                    b = begin("xvT", l, q)
                    for k in range(4):
                        ins = turn(b[:, k * P:(k + 1) * P], xvals[:, k * P:(k + 1) * P])
                    end(ins, "xvT", l, q)

                for r in range(5):
                    if r < 4:
                        for n2 in range(2):
                            mem = slab("cache_mem_k").rearrange("p (m d) -> p m d", m=2)
                            for j in range(4):
                                b = begin("kTs", l, 2 * r + n2, j)
                                for k in range(2):
                                    for mt in range(2):
                                        ins = turn(b[:, k * 256 + mt * P:k * 256 + (mt + 1) * P],
                                                   mem[:, mt, (2 * j + k) * P:(2 * j + k + 1) * P])
                                end(ins, "kTs", l, 2 * r + n2, j)
                        wait_emptied(pe, "kTs", l, 2 * r + 1, 2)
                        wait_emptied(pe, "kTs", l, 2 * r + 1, 3)
                        b = begin("xss", l, r)
                        for n2 in range(2):
                            for hp in range(2):
                                g = 32 * (2 * n2 + hp)
                                for i in range(4):
                                    ins = nc.tensor.matmul(b[g:g + 32, 0:256], qxb[:, 4 * hp + i, 2 * r + n2, :],
                                                           kTs[:, n2, 4 * hp + i, :], start=(i == 0), stop=(i == 3))
                        end(ins, "xss", l, r)
                    if r >= 2:
                        turn_values(r - 2)
                    if r >= 1:
                        q = r - 1
                        pe.wait_ge(s_xp, 6 * l + 3 + q)
                        b = begin("xpTs", l, q)
                        for mt in range(2):
                            ins = turn(b[:, mt * P:(mt + 1) * P], pxs[:, q % 2, mt * P:(mt + 1) * P])
                        end(ins, "xpTs", l, q)
                        wait_emptied(pe, "xpTs", l, q)
                        b = begin("xv", l, q)
                        for n2 in range(2):
                            mem = slab("cache_mem_v").rearrange("p (m d) -> p m d", m=2)
                            for hp in range(2):
                                g = 32 * (2 * n2 + hp)
                                for mt in range(2):
                                    ins = nc.tensor.matmul(b[g:g + 32, :], pxsT[:, q % 2, mt, g:g + 32],
                                                           mem[:, mt, 512 * hp:512 * (hp + 1)],
                                                           start=(mt == 0), stop=(mt == 1))
                        end(ins, "xv", l, q)
                turn_values(3)
                wait_emptied(pe, "xvT", l, 3)
                for c in range(2):
                    split_product(("o", l), l, 4 + 2 * c, oT_parts, c)
                (routed if l % 2 else half_ffn).prime(turn(bank[7][:, 0:P], ident))
                norm(3 * l + 2)
                wait_emptied(pe, "hT", 3 * l + 2, NT - 1, 1)
                if l % 2:
                    pe.wait_ge(s_rw, 16)
                    b = begin("route", l)
                    for t in range(NT):
                        for k in range(KC):
                            ins = nc.tensor.matmul(b[:, t * NE:(t + 1) * NE], hT_at(k, t), rw[:, k, :],
                                                   start=(k == 0), stop=(k == KC - 1))
                    end(ins, "route", l)
                    pe.wait_ge(s_mask, 1)
                    b = begin("pos", l)
                    for t in range(NT):
                        for j in range(t + 1):
                            nc.tensor.matmul(b[:, t * NE:(t + 1) * NE], before if j == t else ones, mask[:, j, :],
                                             start=(j == 0), stop=(j == t))
                    for t in range(NT):
                        ins = nc.tensor.matmul(b[:, NT * NE:(NT + 1) * NE], ones, mask[:, t, :],
                                               start=(t == 0), stop=(t == NT - 1))
                    end(ins, "pos", l)
                    units(pe, routed_step)
                else:
                    dense_steps(half_ffn)
                    half_ffn.wait_emptied(pe, half_ffn.n - 1, "down", 1, NT - 1)
            assert at == [len(JOBS), len(SLABS)]

        @block.scalar
        def _(act):
            st = Steps(act, "a")
            A = nc.scalar.activation

            def copy(out, in_, *key):
                wait_filled(act, *key)
                st.emptied(A(out, in_, ACT.Copy), *key)

            def squares(n, tiles=range(NT)):
                for t in tiles:
                    ready_x(act, n, t)
                    st.did(A(htok[:, t, :], x[:, t, :], ACT.Square, accum_out=stat[:, t:t + 1]), s_sq)

            def h_high(n, tiles):
                for t in tiles:
                    for half in range(2):
                        wait_filled(act, "hT", n, t, half)
                        A(hT_parts[0][:, 4 * half:4 * half + 4, t * P:(t + 1) * P],
                          bank[BANK[("hT", n, t, half)][0]][:, :].rearrange("p (k n) -> p k n", k=4),
                          ACT.Copy).then_inc(s_hpart, 1)

            def dense_steps(L):
                with act.Fori(0, L.n) as i:
                    for key in L.events:
                        if key[0] == "split":
                            L.split_high(act, i, key[1])
                        elif key[0] == "gate":
                            _, c, t = key
                            w = FF_CHUNKS[c][1]
                            L.wait_filled(act, i, *key)
                            L.emptied_by(A(acts[:, NT * (c % 2) + t, 0:w], bank[t][:, 0:w], ACT.Silu), *key)
                        elif key[0] == "aT":
                            _, c, t = key
                            k0, nk = FF_GROUPS[c]
                            L.high_part(act, i, actT[0][:, k0:k0 + nk, t * P:(t + 1) * P],
                                        bank[L.bank[key][0]][:, 0:nk * P].rearrange("p (k n) -> p k n", k=nk), *key)

            def routed_step(i):
                L = routed
                for key in L.events:
                    if key[0] == "split":
                        L.split_high(act, i, key[1])
                        continue
                    b = bank[L.bank[key][0]]
                    if key[0] == "gather":
                        g = key[1]
                        L.high_part(act, i, hTe[0][:, 4 * g:4 * g + 4, :].rearrange("p k n -> p (k n)"), b[:, :], *key)
                    elif key[0] == "ST":
                        L.wait_filled(act, i, *key)
                        L.emptied_by(A(ST.rearrange("p t n -> p (t n)"), b[:, 0:NT * P], ACT.Copy), *key)
                    elif key[0] == "gate":
                        c = key[1]
                        w = FF_CHUNKS[c][1]
                        L.wait_filled(act, i, *key)
                        L.emptied_by(A(acts_e[:, c % 2, 0:w], b[:, 0:w], ACT.Silu), *key)
                    elif key[0] == "aT":
                        k0, nk = FF_GROUPS[key[1]]
                        L.wait_filled(act, i, *key)
                        L.emptied_by(A(actT_e[:, k0:k0 + nk, :].rearrange("p k n -> p (k n)"), b[:, 0:nk * P],
                                       ACT.Copy), *key)
                    elif key[0] == "down":
                        c = key[1]
                        L.high_part(act, i, Y[0][:, 0, c * 512:(c + 1) * 512], b[:, :], *key)

            squares(0)
            act.dma_start(memtok, a["mem_prompt"].rearrange("b (t p) d -> p (b t) d", p=P)).then_inc(s_mem, 16)
            for l in range(DEPTH):
                def in_chunk(c):
                    c0, w = IN_CHUNKS[c]
                    for t in range(NT):
                        copy(proj[:, t, c0:c0 + w], bank[BANK[("in", l, c, t)][0]][:, 0:w], "in", l, c, t)
                wait_filled(act, "hT", 3 * l, NT - 1, 1)
                in_chunk(0)
                st.settle()
                for t in range(NT):
                    st.did(A(sig[:, t, :], proj[:, t, CB:CB + CC], ACT.Sigmoid), s_sig)
                copy(cw, bank[BANK[("cw", l)][0]][:, 0:64].rearrange("p (k n) -> p k n", k=2), "cw", l)
                b = bank[BANK[("cbuf", l)][0]]
                wait_filled(act, "cbuf", l)
                for k in range(2):
                    ins = A(us[:, k, :, 0:30], b[:, 240 * k:240 * k + 240].rearrange("p (n w) -> p n w", n=NS), ACT.Copy)
                    if k:
                        st.emptied(ins, "cbuf", l)

                in_chunk(1)
                for k in range(2):
                    b = bank[BANK[("uT", l, k)][0]]
                    wait_filled(act, "uT", l, k)
                    A(up[:, k, 30:30 + SEQ], b[:, 0:SEQ], ACT.Copy)
                    st.emptied(A(us[:, k, :, 30:46], b[:, SEQ:TOK].rearrange("p (n w) -> p n w", n=NS), ACT.Copy),
                               "uT", l, k)
                for c in range(2, len(IN_CHUNKS)):
                    if (l, c) == (0, 3):
                        for j in range(4):
                            copy(memT[:, 2 * j:2 * j + 2, :],
                                 bank[BANK[("memT", j)][0]][:, :].rearrange("p (k n) -> p k n", k=2), "memT", j)
                    in_chunk(c)
                st.settle()
                pk = o["new_attn_k_prompt"][l, 0].rearrange("(t p) h d -> p t (h d)", p=P)
                pv = o["new_attn_v_prompt"][l, 0].rearrange("(t p) h d -> p t (h d)", p=P)
                act.dma_start(pk, proj[:, 0:2, KA:KA + 256]).then_inc(s_kvo, 16)
                act.dma_start(pv, proj[:, 0:2, VA:VA + 256]).then_inc(s_kvo, 16)
                act.dma_start(o["new_attn_k_sample"][l].rearrange("n t h d -> (n t) (h d)"),
                              proj[:, 2, KA:KA + 256]).then_inc(s_kvo, 16)
                act.dma_start(o["new_attn_v_sample"][l].rearrange("n t h d -> (n t) (h d)"),
                              proj[:, 2, VA:VA + 256]).then_inc(s_kvo, 16)
                for t in range(NT):
                    st.did(A(proj[:, t, GB:GB + 512], proj[:, t, GB:GB + 512], ACT.Silu), s_silu)
                def memory_rows(name, dst, c):
                    for t in range(2):
                        copy(dst[:, t, c * 512:(c + 1) * 512], bank[BANK[(name, l, c, t)][0]][:, :], name, l, c, t)

                for c in range(2):
                    memory_rows("mk", mk, c)
                for j in range(4):
                    copy(mkT[:, 2 * j:2 * j + 2, :],
                         bank[BANK[("mkT", l, j)][0]][:, :].rearrange("p (k n) -> p k n", k=2), "mkT", l, j)
                st.settle()
                act.dma_start(o["new_mem_k_prompt"][l, 0].rearrange("(t p) h d -> p t (h d)", p=P), mk).then_inc(s_mko, 16)
                for kind, dst in (("qkA", qkA), ("qkB", qkB)):
                    for t in range(NT):
                        copy(dst[:, :, t * P:(t + 1) * P],
                             bank[BANK[(kind, l, t)][0]][:, :].rearrange("p (k n) -> p k n", k=4), kind, l, t)

                def softmax_exp(dst, neg_max, sums, value, last):
                    ins = A(dst, dst, ACT.Exp, bias=neg_max, accum_out=sums)
                    st.did(ins, s_exp if last else None)

                def exp_prompt():
                    act.wait_ge(s_max, 6 * l + 2)
                    for h in range(AH):
                        softmax_exp(lg0[:, h, :], small[:, h:h + 1], small[:, 16 + h:17 + h], 0, False)
                    for h in range(AH):
                        softmax_exp(lg1[:, h, :], small[:, 4 + h:5 + h], small[:, 20 + h:21 + h], 0, h == AH - 1)

                def exp_sample(r):
                    act.wait_ge(s_max, 6 * l + 3 + r)
                    softmax_exp(lgS[:, r, :], small[:, 8 + r:9 + r], small[:, 24 + r:25 + r], 0, True)

                for n in range(NS):
                    copy(ktA[:, n % 4, :, :],
                         bank[BANK[("ktA", l, n)][0]][:, :].rearrange("p (k n) -> p k n", k=2), "ktA", l, n)
                    if n == 3:
                        exp_prompt()
                    if n % 2 and n >= 5:
                        exp_sample((n - 5) // 2)
                exp_sample(2)
                exp_sample(3)
                memory_rows("mv", mv, 0)
                for h in range(AH):
                    copy(pTA[:, h, :], bank[BANK[("pTA", l, h)][0]][:, 0:TOK], "pTA", l, h)
                copy(oT[:, 0:2, 0:SEQ], bank[BANK[("oA", l)][0]][:, :].rearrange("p (k n) -> p k n", k=2), "oA", l)
                for r in range(4):
                    copy(pTS[:, r, :, :], bank[BANK[("pTS", l, r)][0]][:, 0:TOK].rearrange("p (k n) -> p k n", k=3),
                         "pTS", l, r)
                copy(svals, bank[BANK[("oS", l)][0]][:, :], "oS", l)
                b = bank[BANK[("oST", l)][0]]
                wait_filled(act, "oST", l)
                for i in range(2):
                    for k in range(2):
                        src = b[64 * i:64 * i + 64, :].rearrange("p (n k c) -> p n k c", n=NS, k=2)[
                            :, :, k, TS * i:TS * i + TS]
                        dst = oT[64 * i:64 * i + 64, k, SEQ:TOK].rearrange("p (n w) -> p n w", n=NS)
                        ins = A(dst, src, ACT.Copy)
                st.emptied(ins, "oST", l)
                wait_filled(act, "nsP", l)
                st.emptied(A(spr[0:64, :], bank[BANK[("nsP", l)][0]][0:64, :], ACT.Copy), "nsP", l)
                st.settle()
                act.dma_start(o["new_ret_prompt"][l, 0].rearrange("h k v -> k h v"),
                              spr[0:64, :].rearrange("p (h v) -> p h v", h=BH)).then_inc(s_spo, 16)
                memory_rows("mv", mv, 1)
                st.settle()
                act.dma_start(o["new_mem_v_prompt"][l, 0].rearrange("(t p) h d -> p t (h d)", p=P), mv).then_inc(s_mvo, 16)
                act.wait_ge(s_lnr, 2 * l + 2)
                A(proj[:, :, CA:CA + CC], proj[:, :, CA:CA + CC], ACT.Silu).then_inc(s_oc, 1)
                for k in range(4):
                    copy(oT[:, 2 + k, :], bank[BANK[("obT", l, k)][0]][:, 0:TOK], "obT", l, k)
                for k in range(2):
                    copy(oT[:, 6 + k, :], bank[BANK[("ocT", l, k)][0]][:, 0:TOK], "ocT", l, k)
                wait_emptied(act, "nsS", l, BH - 1)
                for n2 in range(2):
                    dst = o["new_ret_sample"][l].rearrange("(j s) h k v -> s k j h v", s=2)[n2]
                    for j in range(4):
                        act.dma_start(dst[:, j], s0[64 * n2:64 * n2 + 64, j]).then_inc(s_st, 16)
                act.wait_ge(s_kvo, 64 * (l + 1))
                act.wait_ge(s_outp, 48 * (l + 1))
                act.wait_ge(s_spo, 16 * (l + 1))
                act.wait_ge(s_st, 16 * 8 * (l + 1))
                wait_emptied(act, "out", l, 0, NT - 1)
                w_high(act, l, 0)
                w_high(act, l, 1)
                squares(3 * l + 1, (0, 1))
                h_high(3 * l + 1, (0,))
                squares(3 * l + 1, (2,))
                h_high(3 * l + 1, (1,))
                w_high(act, l, 2)
                for c in range(2):
                    for t in range(NT):
                        if (c, t) == (0, 0):
                            act.wait_ge(s_h, NT * (3 * l + 2))
                        if (c, t) == (0, 1):
                            h_high(3 * l + 1, (2,))
                        if (c, t) == (1, 0):
                            w_high(act, l, 3)
                        copy(qx[:, t, c * 512:(c + 1) * 512], bank[BANK[("q", l, c, t)][0]][:, :], "q", l, c, t)
                for j in range(4):
                    copy(qxT[:, 2 * j:2 * j + 2, :],
                         bank[BANK[("qTx", l, j)][0]][:, :].rearrange("p (k n) -> p k n", k=2), "qTx", l, j)
                act.wait_ge(s_zero, l + 1)
                for j in range(2):
                    b = bank[BANK[("qTs", l, j)][0]]
                    wait_filled(act, "qTs", l, j)
                    for k in range(4):
                        c0 = TS * (k // 2)
                        ins = A(qxb[:, 4 * j + k, :, c0:c0 + TS],
                                b[:, k * P:(k + 1) * P].rearrange("p (n w) -> p n w", n=NS), ACT.Copy)
                    st.emptied(ins, "qTs", l, j)
                for j in range(4):
                    act.wait_ge(s_xmax, 8 * l + j + 1)
                    b = bank[BANK[("xs", l, j)][0]]
                    for i in range(2):
                        c = 2 * j + i
                        ins = A(px[:, j // 2, 2 * (j % 2) + i, :], b[:, i * 256:(i + 1) * 256], ACT.Exp,
                                bias=small[:, 32 + c:33 + c], scale=XD ** -0.5, accum_out=small[:, 40 + c:41 + c])
                        if i == 0:
                            st.did(ins)
                    st.emptied(ins, "xs", l, j)
                for h in range(XH):
                    copy(pxT[:, h, :, :], bank[BANK[("xpT", l, h)][0]][:, :].rearrange("p (k n) -> p k n", k=2),
                         "xpT", l, h)
                for h in range(XH):
                    wait_filled(act, "xo", l, h)
                    A(oT_parts[0][:, 2 * h:2 * h + 2, 0:SEQ],
                      bank[BANK[("xo", l, h)][0]][:, :].rearrange("p (k n) -> p k n", k=2), ACT.Copy).then_inc(s_opart, 1)

                def values_T(q):
                    wait_filled(act, "xvT", l, q)
                    for src, high, _ in stream_values(l, q):
                        ins = A(high, src, ACT.Copy)
                    ins.then_inc(s_opart, 1)

                for r in range(5):
                    if r < 4:
                        for n2 in range(2):
                            for j in (0, 2):
                                copy(kTs[:, n2, 2 * j:2 * j + 2, :],
                                     bank[BANK[("kTs", l, 2 * r + n2, j)][0]][:, :].rearrange("p (k n) -> p k n", k=2),
                                     "kTs", l, 2 * r + n2, j)
                        act.wait_ge(s_xmax, 8 * l + 5 + r)
                        if r >= 2:
                            wait_filled(act, "xpTs", l, r - 2)
                        st.emptied(A(pxs[:, r % 2, :], bank[BANK[("xss", l, r)][0]][:, 0:NMEM], ACT.Exp,
                                     bias=small[:, 48 + r:49 + r], scale=XD ** -0.5,
                                     accum_out=small[:, 52 + r:53 + r]), "xss", l, r)
                    if r >= 2:
                        values_T(r - 2)
                    if r >= 1:
                        copy(pxsT[:, (r - 1) % 2, :, :],
                             bank[BANK[("xpTs", l, r - 1)][0]][:, 0:2 * P].rearrange("p (k n) -> p k n", k=2),
                             "xpTs", l, r - 1)
                w_high(act, l, 4)
                values_T(3)
                w_high(act, l, 5)
                w_high(act, l, 6)
                w_high(act, l, 7)
                squares(3 * l + 2, (0, 1))
                if l % 2 == 0:
                    h_high(3 * l + 2, (0,))
                squares(3 * l + 2, (2,))
                act.wait_ge(s_st, 16 * 8 * (l + 1))
                if l % 2:
                    for t in range(NT):
                        act.wait_ge(s_h, NT * (3 * l + 2) + t + 1)
                        A(h_parts[0][:, t, :], htok[:, t, :], ACT.Copy).then_inc(s_gpart, 1)
                    act.wait_ge(s_rmax, 1)
                    for t in range(NT):
                        ins = A(rtv(1)[:, t, :], rtv(0)[:, t, :], ACT.Exp, bias=stat[:, 8 + t:9 + t],
                                accum_out=stat[:, 12 + t:13 + t])
                        st.did(ins, s_rexp)
                if l % 2:
                    routed.prime(A(full[:, 0:1], minus_half[:, 0:1], ACT.Copy), "a")
                    units(act, routed_step)
                else:
                    h_high(3 * l + 2, (1, 2))
                    act.wait_ge(s_mvo, 16 * (l + 1))
                    half_ffn.prime(A(full[:, 0:1], minus_half[:, 0:1], ACT.Copy), "a")
                    dense_steps(half_ffn)
                squares(3 * l + 3)
            for t in range(NT):
                act.wait_ge(s_h, NT * 3 * DEPTH + t + 1)
                if t < 2:
                    act.dma_start(o["y_prompt"][0, t * P:(t + 1) * P, :], htok[:, t, :]).then_inc(s_yo, 16)
                else:
                    act.dma_start(o["y_sample"].rearrange("n t d -> (n t) d"), htok[:, t, :]).then_inc(s_yo, 16)
            act.wait_ge(s_kvo, 64 * DEPTH)
            act.wait_ge(s_mko, 16 * DEPTH)
            act.wait_ge(s_mvo, 16 * DEPTH)
            act.wait_ge(s_spo, 16 * DEPTH)
            act.wait_ge(s_yo, 16 * NT)
            act.wait_ge(s_st, 16 * 8 * DEPTH)

        def route(dve, st):
            V = nc.vector

            def go(ins, signal=None):
                st.did(ins, signal)
                st.settle()
            lgts, e_, p_, w_, h1, h2, p2 = (rtv(i) for i in range(7))
            r3 = rt[:, 7 * NT * NE:7 * NT * NE + 24]
            m1, m2, mw, den = (r3[:, 3 * i:3 * i + 3] for i in range(4))
            wait_filled(dve, "route", 1)
            st.emptied(V.tensor_copy(lgts, bank[BANK[("route", 1)][0]][:, 0:NT * NE].rearrange(
                "p (t e) -> p t e", t=NT)), "route", 1)
            st.settle()
            go(V.tensor_reduce(stat[:, 8:11], lgts, AX.X, ALU.max, negate=True), s_rmax)
            dve.wait_ge(s_rexp, NT)
            go(V.reciprocal(stat[:, 12:15], stat[:, 12:15]))
            go(V.tensor_tensor(p_, e_, insert(stat[:, 12:15], 2, NE), ALU.mult))
            order = insert(eight, 1, NT)
            go(V.tensor_reduce(m1, p_, AX.X, ALU.max))
            go(V.tensor_tensor(w_, p_, insert(m1, 2, NE), ALU.is_equal))
            go(V.tensor_tensor(w_, w_, order, ALU.mult))
            go(V.tensor_reduce(mw, w_, AX.X, ALU.max))
            go(V.tensor_tensor(h1, w_, insert(mw, 2, NE), ALU.is_equal))
            go(V.scalar_tensor_tensor(p2, h1, -2.0, p_, ALU.mult, ALU.add))
            go(V.tensor_reduce(m2, p2, AX.X, ALU.max))
            go(V.tensor_tensor(w_, p2, insert(m2, 2, NE), ALU.is_equal))
            go(V.tensor_tensor(w_, w_, order, ALU.mult))
            go(V.tensor_reduce(mw, w_, AX.X, ALU.max))
            go(V.tensor_tensor(h2, w_, insert(mw, 2, NE), ALU.is_equal))
            go(V.tensor_tensor(mask, h1, h2, ALU.add), s_mask)
            go(V.tensor_tensor(den, m1, m2, ALU.add))
            go(V.reciprocal(den, den))
            go(V.tensor_tensor(m1, m1, den, ALU.mult))
            go(V.tensor_tensor(m2, m2, den, ALU.mult))
            go(V.tensor_tensor(h1, h1, insert(m1, 2, NE), ALU.mult))
            go(V.tensor_tensor(h2, h2, insert(m2, 2, NE), ALU.mult))
            go(V.tensor_tensor(comb, h1, h2, ALU.add), s_comb)
            wait_filled(dve, "pos", 1)
            b = bank[BANK[("pos", 1)][0]]
            st.did(V.tensor_copy(full[:, 4:4 + NE], b[:, NT * NE:(NT + 1) * NE]))
            st.emptied(V.scalar_tensor_tensor(posm, b[:, 0:NT * NE].rearrange("p (t e) -> p t e", t=NT), 1.0, mask,
                                              ALU.add, ALU.mult), "pos", 1)
            st.settle()
            go(V.tensor_scalar(posm, posm, 1.0, None, ALU.subtract))
            for t in range(NT):
                ins = V.tensor_scalar(S_r[:, t, :], slots, posm[:, t, 0:1], None, ALU.is_equal)
                st.did(ins, s_S if t == NT - 1 else None)
            K = 2 * NE
            here, sums, sums2 = (more[:, i * K:(i + 1) * K] for i in range(3))
            pick = cut(more[:, 3 * K:(3 + EXTRA) * K], u=EXTRA)
            src = cut(more[:, (3 + EXTRA) * K:(10 + EXTRA) * K], j=7)
            got = cut(more[:, (10 + EXTRA) * K:(10 + EXTRA) * K + EXTRA * 7], u=EXTRA)
            prod = prod_at.rearrange("p (u j c) -> p u j c", u=EXTRA, j=7)
            here_ = here.rearrange("p (e b) -> p e b", b=2)
            src_ = src.rearrange("p j (e b) -> p j e b", b=2)
            for i in range(2):
                st.did(V.tensor_scalar(here_[:, :, i], full[:, 4:4 + NE], P * (i + 1) + 0.5, None, ALU.is_ge))
                st.did(V.tensor_scalar(src_[:, NT:2 * NT, :, i], posm, float(P * (i + 1)), None, ALU.subtract))
                st.did(V.tensor_copy(src_[:, 0:NT, :, i], comb))
                st.did(V.tensor_scalar(src_[:, 6, :, i], eight, -1.0, float(NE), ALU.mult, ALU.add))
            st.settle()
            was, now = here, sums
            for d in (1, 2, 4, 8):
                st.did(V.tensor_copy(now[:, 0:d], was[:, 0:d]))
                go(V.tensor_tensor(now[:, d:K], was[:, d:K], was[:, 0:K - d], ALU.add))
                was, now = now, (sums2 if now is sums else sums)
            st.did(V.memset(expert[:, :], 0))
            st.did(V.tensor_scalar(full[:, 12:13], was[:, K - 1:K], float(NE), None, ALU.add))
            go(V.tensor_tensor(now, was, here, ALU.mult))
            for u in range(EXTRA):
                st.did(V.tensor_scalar(pick[:, u, :], now, float(u + 1), None, ALU.is_equal))
            st.settle()
            go(V.tensor_tensor(prod, insert(pick, 2, 7), insert(src, 1, EXTRA), ALU.mult))
            go(V.tensor_reduce(got, prod, AX.X, ALU.add))
            st.did(V.tensor_copy(expert[:, NE:UNITS], got[:, :, 6]))
            st.did(V.tensor_copy(expert[:, UNITS:UNITS + 1], full[:, 12:13]), s_units)
            go(V.memset(table[:, UNITS - 1, NT:2 * NT], -1.0))
            st.did(V.tensor_copy(table[:, 0:NE, 0:NT], comb.rearrange("p t e -> p e t")))
            st.did(V.tensor_copy(table[:, 0:NE - 1, NT:2 * NT], posm[:, :, 1:NE].rearrange("p t e -> p e t")))
            st.did(V.tensor_copy(table[:, NE:UNITS, 0:NT], got[:, :, 0:NT]))
            go(V.tensor_copy(table[:, NE - 1:UNITS - 1, NT:2 * NT], got[:, :, NT:2 * NT]))

        @block.vector
        def _(dve):
            st = Steps(dve, "v")
            V = nc.vector

            def norm_row(n, t):
                if t == 0:
                    dve.wait_ge(s_gain[n], 16)
                dve.wait_ge(s_rstd, NT * n + t + 1)
                st.did(V.scalar_tensor_tensor(htok[:, t, :], x[:, t, :], stat[:, 4 + t:5 + t], g_row[n],
                                              ALU.mult, ALU.mult), s_h)

            def norm_T(n, rows_left=NT):
                def take(t):
                    for half in range(2):
                        wait_filled(dve, "hT", n, t, half)
                        at_ = (slice(None), slice(4 * half, 4 * half + 4), slice(t * P, (t + 1) * P))
                        b = bank[BANK[("hT", n, t, half)][0]][:, :].rearrange("p (k n) -> p k n", k=4)
                        if n in (1, 2, 4):
                            dve.wait_ge(s_hpart, {1: 0, 2: 2 * NT, 4: 4 * NT}[n] + 2 * t + half + 1)
                            ins = V.tensor_tensor(hT_parts[1][at_], b, hT_parts[0][at_].bitcast(F32), ALU.subtract)
                        else:
                            ins = V.tensor_copy(hT[at_], b)
                        st.emptied(ins, "hT", n, t, half)

                if rows_left == NT:
                    norm_row(n, 0)
                take(0)
                norm_row(n, 1)
                norm_row(n, 2)
                take(1)
                if n in (1, 4):
                    w_low(dve, n // 3, 2)
                take(2)
                if n in (1, 4):
                    w_low(dve, n // 3, 3)

            def add_x(name, l, n):
                for c in range(2):
                    for t in range(NT):
                        key = (name, l, c, t)
                        wait_filled(dve, *key)
                        xs = x[:, t, c * 512:(c + 1) * 512]
                        st.emptied(V.tensor_tensor(xs, bank[BANK[key][0]][:, :], xs, ALU.add), *key)
                        if (c, t) == (1, 0):
                            norm_row(n, 0)
                        if name == "out" and (c, t) == (0, NT - 1):
                            w_low(dve, l, 0)
                            w_low(dve, l, 1)
                        if name == "o" and (c, t) in ((0, 0), (0, NT - 1)):
                            w_low(dve, l, 6 + (t > 0))

            def dense_steps(L):
                with dve.Fori(0, L.n) as i:
                    for key in L.events:
                        if key[0] == "split":
                            L.split_low(dve, i, key[1])
                        elif key[0] == "up":
                            _, c, t = key
                            at_ = acts[:, NT * (c % 2) + t, 0:FF_CHUNKS[c][1]]
                            L.wait_filled(dve, i, *key)
                            L.wait_emptied(dve, i, "gate", c, t)
                            L.emptied_by(V.tensor_tensor(at_, bank[3 + t][:, 0:FF_CHUNKS[c][1]], at_, ALU.mult), *key)
                        elif key[0] == "aT":
                            _, c, t = key
                            k0, nk = FF_GROUPS[c]
                            at_ = (slice(None), slice(k0, k0 + nk), slice(t * P, (t + 1) * P))
                            L.low_part(dve, i, actT[1][at_], bank[L.bank[key][0]][:, 0:nk * P].rearrange(
                                "p (k n) -> p k n", k=nk), actT[0][at_], *key)
                        elif key[0] == "down":
                            _, c, t = key
                            L.wait_filled(dve, i, *key)
                            xs = x[:, t, c * 512:(c + 1) * 512]
                            L.emptied_by(V.tensor_tensor(xs, bank[L.bank[key][0]][:, :], xs, ALU.add), *key)

            def routed_step(i):
                L = routed
                L.wait_emptied(dve, i, "scatter", 1, NT - 1, back=1)
                V.tensor_copy(cur, table[:, bass.ds(i, 1), :].rearrange("p e j -> p (e j)")).then_inc(s_cur, 1)
                for key in L.events:
                    if key[0] == "split":
                        L.split_low(dve, i, key[1])
                        continue
                    b = bank[L.bank[key][0]]
                    if key[0] == "gather":
                        g = key[1]
                        hi, lo = (q[:, 4 * g:4 * g + 4, :].rearrange("p k n -> p (k n)") for q in hTe)
                        L.low_part(dve, i, lo, b[:, :], hi, *key)
                    elif key[0] == "ST":
                        L.wait_filled(dve, i, *key)
                        dve.wait_ge(s_cur, i + 1)
                        for t in range(NT):
                            ins = V.tensor_scalar(S_r[:, t, :], slots, cur[:, NT + t:NT + t + 1], None, ALU.is_equal)
                        ins.then_inc(s_S, 1)
                    elif key[0] == "up":
                        c = key[1]
                        at_ = acts_e[:, c % 2, 0:FF_CHUNKS[c][1]]
                        L.wait_filled(dve, i, *key)
                        L.wait_emptied(dve, i, "gate", c)
                        L.emptied_by(V.tensor_tensor(at_, b[:, 0:FF_CHUNKS[c][1]], at_, ALU.mult), *key)
                    elif key[0] == "down":
                        hi, lo = (q[:, 0, key[1] * 512:(key[1] + 1) * 512] for q in Y)
                        L.low_part(dve, i, lo, b[:, :], hi, *key)
                    elif key[0] == "scatter":
                        _, c, t = key
                        L.wait_filled(dve, i, *key)
                        xs = x[:, t, c * 512:(c + 1) * 512]
                        L.emptied_by(V.scalar_tensor_tensor(xs, b[:, :], cur[:, t:t + 1], xs, ALU.mult, ALU.add), *key)

            for l in range(DEPTH):
                norm_T(3 * l)
                if l == 0:
                    dve.wait_ge(s_relr, 16)
                    st.did(V.tensor_copy(relx[0:8, 0:RPAD], relx[0:8, RPAD:RPAD + 1].to_broadcast([8, RPAD])), s_relx)
                    dve.wait_ge(s_const, 16)
                st.did(V.memset(up[:, :, 0:30], 0.0))
                dve.wait_ge(s_rel, 16 * 9 * (l + 1))
                st.did(V.tensor_tensor(rel_p[:, :, P:256], rel_p[:, :, P:256], insert(cmask, 1, AH), ALU.add))
                st.did(V.tensor_tensor(rel_n.rearrange("p r (n j) -> p (r n) j", j=TS),
                                       insert(rel_s[:, PAST:PAST + TS], 1, 32),
                                       smask.rearrange("p r (n j) -> p (r n) j", j=TS), ALU.add))
                dve.wait_ge(s_sig, NT * (l + 1))
                st.did(V.tensor_tensor(proj[:, :, CA:CA + CC], proj[:, :, CA:CA + CC], sig, ALU.mult), s_u)
                for k in range(2):
                    wait_emptied(dve, "uT", l, k)
                    outp = conv[:, k, 0:SEQ]
                    outs_ = conv[:, k, SEQ:TOK].rearrange("p (n w) -> p n w", n=NS)
                    for j in range(CW):
                        inp = up[:, k, j:j + SEQ]
                        ins_ = us[:, k, :, j:j + TS]
                        wj = cw[:, k, j:j + 1]
                        if j == 0:
                            st.did(V.tensor_scalar(outp, inp, wj, cw[:, k, 31:32], ALU.mult, ALU.add))
                            st.did(V.tensor_scalar(outs_, ins_, wj, cw[:, k, 31:32], ALU.mult, ALU.add))
                        else:
                            dve.wait_ge(st.own, st.count[id(st.own)] - 1)
                            st.did(V.scalar_tensor_tensor(outp, inp, wj, outp, ALU.mult, ALU.add))
                            dve.wait_ge(st.own, st.count[id(st.own)] - 1)
                            st.did(V.scalar_tensor_tensor(outs_, ins_, wj, outs_, ALU.mult, ALU.add),
                                   s_conv if j == CW - 1 else None)
                dve.wait_ge(s_mko, 16 * (l + 1))
                for j in range(4):
                    wait_filled(dve, "sA", l, j)
                    t, odd = divmod(j, 2)
                    w = (t + 1) * P
                    ins = V.scalar_tensor_tensor((lg0, lg1)[t][:, odd::2, :], bank[BANK[("sA", l, j)][0]][:, 0:2 * w].rearrange(
                        "p (h k) -> p h k", h=2), AD ** -0.5, rel_p[:, odd::2, 256 - w:256], ALU.mult, ALU.add)
                    st.emptied(ins, "sA", l, j)
                st.settle()
                st.did(V.tensor_reduce(small[:, 0:4], lg0, AX.X, ALU.max, negate=True), s_max)
                st.did(V.tensor_reduce(small[:, 4:8], lg1, AX.X, ALU.max, negate=True), s_max)
                for r in range(4):
                    wait_filled(dve, "sS", l, r)
                    b = bank[BANK[("sS", l, r)][0]]
                    st.did(V.scalar_tensor_tensor(lgS[:, r, 0:PAST], b[:, 0:PAST], AD ** -0.5, rel_s[:, 0:PAST],
                                                  ALU.mult, ALU.add))
                    st.emptied(V.scalar_tensor_tensor(lgS[:, r, PAST:TOK], b[:, PAST:TOK], AD ** -0.5, rel_n[:, r, :],
                                                      ALU.mult, ALU.add), "sS", l, r)
                    st.settle()
                    st.did(V.tensor_reduce(small[:, 8 + r:9 + r], lgS[:, r, :], AX.X, ALU.max, negate=True), s_max)
                dve.wait_ge(s_exp, 5 * l + 1)
                st.did(V.reciprocal(small[:, 16:24], small[:, 16:24]))
                st.settle()
                st.did(V.tensor_tensor(lg0, lg0, insert(small[:, 16:20], 2, P), ALU.mult), s_p)
                st.did(V.tensor_tensor(lg1, lg1, insert(small[:, 20:24], 2, 256), ALU.mult), s_p)
                for r in range(4):
                    dve.wait_ge(s_exp, 5 * l + 2 + r)
                    st.did(V.reciprocal(small[:, 24 + r:25 + r], small[:, 24 + r:25 + r]))
                    st.settle()
                    st.did(V.tensor_scalar(lgS[:, r, :], lgS[:, r, :], small[:, 24 + r:25 + r], None, ALU.mult), s_p)
                wait_emptied(dve, "qkB", l, 2)
                wait_emptied(dve, "oS", l)
                st.did(V.memset(q0, 0.0))
                st.settle()
                for h in range(BH):
                    lo = 64 * (h % 2)
                    for n2 in range(2):
                        src = steps(qkB[lo:lo + 64, h // 2, SEQ + TS * n2:SEQ + TS * n2 + 1], [[32, 4], [1, TS]])
                        dst = steps(q0[64 * n2:64 * n2 + 64, h, TS * n2:TS * n2 + 1], [[160, 4], [1, TS]])
                        ins = V.tensor_tensor(dst, src, insert(qdec[lo:lo + 64, h, :], 1, 4), ALU.mult)
                        if n2:
                            st.did(ins, s_q0)
                        else:
                            st.did(ins)
                for h in range(BH):
                    wait_filled(dve, "aB", l, h)
                    b = bank[BANK[("aB", l, h)][0]]
                    st.did(V.tensor_tensor(attT[:, h, 0:256], b[:, 0:256], decay[:, h, :], ALU.mult))
                    st.emptied(V.tensor_tensor(attT[:, h, 256:384], b[:, 256:384], decay[:, h, 0:P], ALU.mult),
                               "aB", l, h)
                for odd in range(2):
                    wait_filled(dve, "aS", l, odd)
                    st.emptied(V.tensor_tensor(attS[:, odd::2, :], bank[BANK[("aS", l, odd)][0]][:, 0:256].rearrange(
                        "p (h k) -> p h k", h=2), decay_s[:, odd::2, :], ALU.mult), "aS", l, odd)
                for t in range(NT):
                    wait_filled(dve, "oB", l, t)
                    b = bank[BANK[("oB", l, t)][0]]
                    for h in range(BH):
                        st.did(V.bn_stats(bnst[:, 6 * h:6 * h + 6], b[:, h * P:(h + 1) * P]))
                    st.settle()
                    for h in range(BH):
                        st.did(V.bn_aggr(bnag[:, t, 2 * h:2 * h + 2], bnst[:, 6 * h:6 * h + 6]),
                               s_gnv if h == 3 else None)
                    dve.wait_ge(s_gnr, NT * l + t + 1)
                    for h in range(BH):
                        st.did(V.tensor_scalar(gnt[:, h * P:(h + 1) * P], b[:, h * P:(h + 1) * P],
                                               bnag[:, t, 2 * h:2 * h + 1], rstd8[:, t, h:h + 1],
                                               ALU.subtract, ALU.mult), emptied["v"] if h == 3 else None)
                    assert st.last[1] == DRAIN[("oB", l, t)][1]
                    dve.wait_ge(s_gs, NT * l + t + 1)
                    st.settle()
                    st.did(V.tensor_tensor(proj[:, t, GB:GB + 512], gnt, proj[:, t, GB:GB + 512], ALU.mult), s_ob)
                for h in range(BH):
                    wait_filled(dve, "nsS", l, h)
                    st.emptied(V.scalar_tensor_tensor(
                        s0[:, :, h, :], s0[:, :, h, :], GAMMA[h] ** TS,
                        bank[BANK[("nsS", l, h)][0]][:, :].rearrange("p (j v) -> p j v", j=4),
                        ALU.mult, ALU.add), "nsS", l, h)
                dve.wait_ge(s_outp, 48 * (l + 1))
                for t in range(NT):
                    wait_filled(dve, "yc", l, t)
                    b = bank[BANK[("yc", l, t)][0]]
                    st.did(V.bn_stats(bnst[:, 0:6], b[:, 0:CC]))
                    st.settle()
                    st.did(V.bn_aggr(lnag[:, 2 * t:2 * t + 2], bnst[:, 0:6]), s_lnv)
                    dve.wait_ge(s_cln, NT * l + t + 1)
                    st.emptied(V.tensor_scalar(proj[:, t, CA:CA + CC], b[:, 0:CC], lnag[:, 2 * t:2 * t + 1],
                                               lnr[:, t:t + 1], ALU.subtract, ALU.mult), "yc", l, t)
                st.settle()
                dve.wait_ge(s_bc, 48 * (l + 1))
                st.did(V.tensor_tensor(proj[:, :, CA:CA + CC], proj[:, :, CA:CA + CC], insert(bc_cg[:, :], 1, NT),
                                       ALU.mult), s_lnr)
                st.settle()
                st.did(V.tensor_tensor(proj[:, :, CA:CA + CC], proj[:, :, CA:CA + CC], insert(bc_cb[:, :], 1, NT),
                                       ALU.add), s_lnr)
                add_x("out", l, 3 * l + 1)
                norm_T(3 * l + 1, NT - 1)
                wait_filled(dve, "q", l, 1, NT - 1)
                st.did(V.memset(qxb, 0.0), s_zero)
                for j in range(4):
                    wait_filled(dve, "xs", l, j)
                    b = bank[BANK[("xs", l, j)][0]]
                    cs = small[:, 32 + 2 * j:34 + 2 * j]
                    st.did(V.tensor_reduce(cs, b[:, :].rearrange("p (h k) -> p h k", h=2), AX.X, ALU.max, negate=True))
                    st.settle()
                    st.did(V.tensor_scalar(cs, cs, XD ** -0.5, None, ALU.mult), s_xmax)
                for t in range(2):
                    wait_emptied(dve, "xs", l, 2 * t + 1)
                    ss = small[:, 40 + 4 * t:44 + 4 * t]
                    st.did(V.reciprocal(ss, ss))
                    st.settle()
                    st.did(V.tensor_tensor(px[:, t, :, :], px[:, t, :, :], insert(ss, 2, NMEM), ALU.mult), s_xp)
                def values(q):
                    wait_filled(dve, "xv", l, q)
                    st.emptied(V.tensor_copy(xvals, bank[BANK[("xv", l, q)][0]][:, :]), "xv", l, q)

                def values_low(q):
                    dve.wait_ge(s_opart, 8 * l + 5 + q)
                    for src, high, low in stream_values(l, q):
                        ins = V.tensor_tensor(low, src, high.bitcast(F32), ALU.subtract)
                    st.emptied(ins, "xvT", l, q)

                for h in range(XH):
                    dve.wait_ge(s_opart, 8 * l + h + 1)
                    at_ = (slice(None), slice(2 * h, 2 * h + 2), slice(0, SEQ))
                    st.emptied(V.tensor_tensor(oT_parts[1][at_], bank[BANK[("xo", l, h)][0]][:, :].rearrange(
                        "p (k n) -> p k n", k=2), oT_parts[0][at_].bitcast(F32), ALU.subtract), "xo", l, h)

                for r in range(4):
                    for n2 in range(2):
                        for j in (1, 3):
                            wait_filled(dve, "kTs", l, 2 * r + n2, j)
                            st.emptied(V.tensor_copy(
                                kTs[:, n2, 2 * j:2 * j + 2, :],
                                bank[BANK[("kTs", l, 2 * r + n2, j)][0]][:, :].rearrange("p (k n) -> p k n", k=2)),
                                "kTs", l, 2 * r + n2, j)
                    wait_filled(dve, "xss", l, r)
                    b = bank[BANK[("xss", l, r)][0]]
                    cs = small[:, 48 + r:49 + r]
                    st.did(V.tensor_reduce(cs, b[:, 0:NMEM], AX.X, ALU.max, negate=True))
                    st.settle()
                    st.did(V.tensor_scalar(cs, cs, XD ** -0.5, None, ALU.mult), s_xmax)
                    wait_emptied(dve, "xss", l, r)
                    ss = small[:, 52 + r:53 + r]
                    st.did(V.reciprocal(ss, ss))
                    st.settle()
                    st.did(V.tensor_scalar(pxs[:, r % 2, :], pxs[:, r % 2, :], ss, None, ALU.mult), s_xp)
                    if r >= 2:
                        values_low(r - 2)
                    if r >= 1:
                        values(r - 1)
                values_low(2)
                values(3)
                w_low(dve, l, 4)
                values_low(3)
                w_low(dve, l, 5)
                add_x("o", l, 3 * l + 2)
                (routed if l % 2 else half_ffn).prime(V.memset(full[:, 2:3], 0.0), "split")
                norm_T(3 * l + 2, NT - 1)
                if l % 2:
                    for t in range(NT):
                        dve.wait_ge(s_gpart, t + 1)
                        st.did(V.tensor_tensor(h_parts[1][:, t, :], htok[:, t, :], h_parts[0][:, t, :].bitcast(F32),
                                               ALU.subtract))
                    route(dve, st)
                    routed.prime(V.memset(full[:, 13:14], 0.0), "v")
                    units(dve, routed_step)
                    V.memset(full[:, 3:4], 0.0).then_inc(s_xlast, 1)
                else:
                    half_ffn.prime(V.memset(full[:, 13:14], 0.0), "v")
                    dense_steps(half_ffn)
            for t in range(NT):
                norm_row(3 * DEPTH, t)

        @block.gpsimd
        def _(pool):
            st = Steps(pool, "g")
            G = nc.gpsimd

            def rstd(n):
                for t in range(NT):
                    pool.wait_ge(s_sq, NT * n + t + 1)
                    st.did(G.tensor_scalar(stat[:, t:t + 1], stat[:, t:t + 1], 1.0 / D, EPS, ALU.mult, ALU.add))
                    st.settle()
                    st.did(G.tensor_tensor(stat[:, 4 + t:5 + t], stat[:, t:t + 1], minus_half[:, 0:1], ALU.pow), s_rstd)

            def gain(n):
                src = (("norm_mix_g", "norm_mem_g", "norm_ffn_g")[n % 3], n // 3 * D) if n < 3 * DEPTH else ("final_norm_g", 0)
                pool.dma_start(g_row[n], rows(a[src[0]], src[1], [[0, P], [1, D]])).then_inc(s_gain[n], 16)

            pool.dma_start(cst[:, 0:NFIRST], a["constants"][:, 0:NFIRST]).then_inc(s_first, 16)
            gain(0)
            pool.wait_ge(s_first, 16)
            rstd(0)
            pool.dma_start(cst[:, NFIRST:NCONST], a["constants"][:, NFIRST:NCONST]).then_inc(s_const, 16)
            def load_conv(l):
                pool.dma_start(cwr[0:31, :], a["conv_w"][l]).then_inc(s_cw, 16)
                pool.dma_start(cwr[31:32, :], a["conv_b"][l:l + 1]).then_inc(s_cw, 16)
                pool.dma_start(cbufr[0:120, :, :],
                               a["state_conv"][l].rearrange("(g n) w c -> (n w) g c", g=2)).then_inc(s_cbuf, 16)

            load_conv(0)
            pool.dma_start(relx[0:8, RPAD:RLEN], a["rel_bias_reversed"].rearrange("l h r -> (l h) r")).then_inc(s_relr, 16)
            pool.dma_start(rw, a["router_w"][0].rearrange("(k p) e -> p k e", p=P)).then_inc(s_rw, 16)
            pool.wait_ge(s_relx, 1)
            pool.dma_start(scratch[0], relx[0:8, :]).then_inc(s_relv, 16)
            pool.wait_ge(s_relv, 16)
            pool.dma_start(scratch[1], rows(scratch[0], 0, [[0, P], [1, DEPTH * AH * RLEN]])).then_inc(s_relv, 16)
            for e in range(NE):
                ins = G.memset(eight[:, e:e + 1], float(NE - e))
            st.did(ins)

            def load(l):
                if l == 0:
                    pool.wait_ge(s_relv, 32)
                pool.dma_start(rel_p, rows(scratch[1], l * AH * RLEN + RPAD, [[DEPTH * AH * RLEN - 1, P], [RLEN, AH], [1, 256]])).then_inc(s_rel, 16)
                for n2 in range(2):
                    for h in range(AH):
                        r0 = 64 * n2 + TS * h
                        pool.dma_start(rel_s[r0:r0 + TS, :],
                                       rows(scratch[1], (l * AH + h) * RLEN + TS - 1,
                                            [[DEPTH * AH * RLEN - 1, TS], [1, PAST + TS]])).then_inc(s_rel, 16)
                for dst, name, w in ((bc_gn, "ret_gn_g", BH * BV), (bc_cg, "conv_ln_g", CC), (bc_cb, "conv_ln_b", CC)):
                    pool.dma_start(dst[:, :], rows(a[name], l * w, [[0, P], [1, w]])).then_inc(s_bc, 16)
                for n2 in range(2):
                    src = a["state_ret"][l].rearrange("(j s) h k v -> s k j h v", s=2)[n2]
                    for j in range(4):
                        pool.dma_start(s0[64 * n2:64 * n2 + 64, j], src[:, j]).then_inc(s_s0, 16)

            for l in range(DEPTH):
                if l:
                    load_conv(l)
                load(l)
                pool.wait_ge(s_const, 16)
                pool.wait_ge(s_u, l + 1)
                pool.dma_start(o["new_conv_prompt"][l, 0], proj[98:128, 1, CA:CA + CC]).then_inc(s_outp, 16)
                pool.dma_start(o["new_conv_sample"][l, :, 0:14, :], a["state_conv"][l, :, 16:30, :]).then_inc(s_outp, 16)
                pool.dma_start(o["new_conv_sample"][l, :, 14:30, :], proj[:, 2, CA:CA + CC]).then_inc(s_outp, 16)
                for c in range(2, 4):
                    wait_emptied(pool, "in", l, c, 2)
                for t in range(NT):
                    def part(i):
                        return proj[:, t, QB:QB + 512].rearrange("p (b h s w) -> p b h s w", b=2, h=4, s=2)[:, :, :, i, :]

                    def to(i):
                        return part(i)
                    for b_ in range(2):
                        co, si = insert(cos_t[:, t, b_, :], 1, 4), insert(sin_t[:, t, b_, :], 1, 4)
                        tm = [rtmp[:, 128 * i:128 * i + 128].rearrange("p (h w) -> p h w", h=4) for i in range(4)]
                        x1, x2 = part(0)[:, b_], part(1)[:, b_]
                        st.did(G.tensor_tensor(tm[0], x1, co, ALU.mult))
                        st.did(G.tensor_tensor(tm[1], x2, si, ALU.mult))
                        st.did(G.tensor_tensor(tm[2], x2, co, ALU.mult))
                        st.did(G.tensor_tensor(tm[3], x1, si, ALU.mult))
                        st.settle()
                        st.did(G.tensor_tensor(to(0)[:, b_], tm[0], tm[1], ALU.subtract))
                        st.did(G.tensor_tensor(to(1)[:, b_], tm[2], tm[3], ALU.add), s_rot if b_ else None)
                        st.settle()
                for t in range(2):
                    ins = G.tensor_tensor(kd[:, t, :].rearrange("p (h d) -> p h d", h=BH),
                                          proj[:, t, KB:KB + 256].rearrange("p (h d) -> p h d", h=BH),
                                          insert(kdec[:, t, :], 2, BK), ALU.mult)
                    st.did(ins, s_kd if t else None)
                st.did(G.memset(qblk, 0.0))
                wait_emptied(pool, "qkA", l, 2)
                st.settle()
                for i in range(2):
                    for k in range(2):
                        ins = G.tensor_copy(qblk[64 * i:64 * i + 64, k, :, TS * i:TS * i + TS],
                                            qkA[64 * i:64 * i + 64, k, SEQ:TOK].rearrange("p (n w) -> p n w", n=NS))
                        st.did(ins, s_blk if (i, k) == (1, 1) else None)
                wait_emptied(pool, "oS", l)
                for h in range(BH):
                    ins = G.tensor_tensor(ks[:, h, :, :], insert(proj[:, 2, KB + 64 * h:KB + 64 * h + 64], 1, NS),
                                          insert(kmask[:, h, :], 2, BK), ALU.mult)
                    st.did(ins, s_kd if h == 3 else None)
                pool.wait_ge(s_bc, 48 * (l + 1))
                for t in range(NT):
                    pool.wait_ge(s_silu, NT * l + t + 1)
                    st.did(G.tensor_tensor(proj[:, t, GB:GB + 512], proj[:, t, GB:GB + 512], bc_gn[:, :], ALU.mult), s_gs)
                for t in range(NT):
                    pool.wait_ge(s_gnv, NT * l + t + 1)
                    var = bnag[:, t, :].rearrange("p (h s) -> p h s", s=2)[:, :, 1]
                    st.did(G.tensor_scalar(rstd8[:, t, :], var, EPS, None, ALU.add))
                    st.settle()
                    st.did(G.tensor_tensor(rstd8[:, t, :], rstd8[:, t, :], minus_half, ALU.pow), s_gnr)
                for t in range(NT):
                    pool.wait_ge(s_lnv, NT * l + t + 1)
                    st.did(G.tensor_scalar(lnr[:, t:t + 1], lnag[:, 2 * t + 1:2 * t + 2], EPS, None, ALU.add))
                    st.settle()
                    st.did(G.tensor_tensor(lnr[:, t:t + 1], lnr[:, t:t + 1], minus_half[:, 0:1], ALU.pow), s_cln)
                if l == 0:
                    wait_filled(pool, "ocT", l, 1)
                    pool.wait_ge(s_kvo, 64 * (l + 1))
                    gain(1)
                else:
                    wait_filled(pool, "mv", l, 1, 1)
                    gain(4)
                    gain(5)
                rstd(3 * l + 1)
                if l == 0:
                    wait_filled(pool, "xs", l, 3)
                    gain(2)
                rstd(3 * l + 2)
                if l == 0:
                    pool.wait_ge(s_h, 3 * NT)
                    gain(3)
                else:
                    gain(6)
                rstd(3 * l + 3)
                if l == 0:
                    pool.wait_ge(s_st, 16 * 8)
            pool.wait_ge(s_outp, 16 * 3 * DEPTH)


_INS = ["x_prompt", "x_sample", "cache_attn_k", "cache_attn_v", "state_ret", "state_conv", "cache_mem_k",
        "cache_mem_v", "mem_prompt", "norm_mix_g", "w_in", "ret_gn_g", "conv_w", "conv_b", "conv_ln_g",
        "conv_ln_b", "w_out", "norm_mem_g", "wx_q", "wx_k", "wx_v", "wx_o", "norm_ffn_g", "ffn_w_gate",
        "ffn_w_up", "ffn_w_down", "router_w", "moe_w_gate", "moe_w_up", "moe_w_down", "final_norm_g"]
_OUTS = [("y_prompt", (1, SEQ, D)), ("y_sample", (NS, TS, D)),
         ("new_attn_k_prompt", (DEPTH, 1, SEQ, AH, AD)), ("new_attn_v_prompt", (DEPTH, 1, SEQ, AH, AD)),
         ("new_ret_prompt", (DEPTH, 1, BH, BK, BV)), ("new_conv_prompt", (DEPTH, 1, CW - 1, CC)),
         ("new_mem_k_prompt", (DEPTH, 1, NMEM, XH, XD)), ("new_mem_v_prompt", (DEPTH, 1, NMEM, XH, XD)),
         ("new_attn_k_sample", (DEPTH, NS, TS, AH, AD)), ("new_attn_v_sample", (DEPTH, NS, TS, AH, AD)),
         ("new_ret_sample", (DEPTH, NS, BH, BK, BV)), ("new_conv_sample", (DEPTH, NS, CW - 1, CC))]


def kernel(**inputs):
    import concourse.bacc as _bacc
    from concourse.bass_utils import run_bass_kernel_spmd as _run

    nc = _bacc.Bacc("TRN2", target_bir_lowering=False, num_devices=1)
    arrays, a = {}, {}

    def give(name, array):
        array = np.ascontiguousarray(array)
        arrays[f"in_{name}"] = array
        a[name] = nc.dram_tensor(f"in_{name}", array.shape, mybir.dt.from_np(array.dtype), kind="ExternalInput").ap()

    for name in _INS:
        give(name, np.asarray(inputs[name]))
    give("rel_bias_reversed", np.asarray(inputs["rel_bias"])[:, :, ::-1])
    give("constants", constants())
    o = {name: nc.dram_tensor(f"out_{name}", shape, F32, kind="ExternalOutput").ap() for name, shape in _OUTS}
    scratch = (nc.dram_tensor("bias_vectors", (DEPTH * AH, RLEN), F32, kind="Internal").ap(),
               nc.dram_tensor("bias_vectors_by_row", (P, DEPTH * AH * RLEN), F32, kind="Internal").ap())
    hybrid_encoder(nc, a, o, scratch)
    r = _run(nc, [arrays], core_ids=[0])
    return tuple(r.results[0][f"out_{name}"] for name, _ in _OUTS)
```
